# Optimizing a Trainium2 kernel written in Bass

```python
import math
import jax, jax.numpy as jnp
from jax import lax
import numpy as np

D_MODEL = 1024
BATCH = 1
SEQ = 256
DEPTH = 2

HEAD_DIM = 64
MIX_WIDTH = D_MODEL
SSM_WIDTH = 3 * D_MODEL // 8
SSM_GROUP_CH = 16
SSM_GROUPS = SSM_WIDTH // SSM_GROUP_CH
SSM_STATE = 64
DIL_WIDTH = 3 * D_MODEL // 8
DIL_HEADS = DIL_WIDTH // HEAD_DIM
DIL_PATTERNS = ((128, 1), (512, 4), (2048, 16))
DIFF_WIDTH = MIX_WIDTH - SSM_WIDTH - DIL_WIDTH
DIFF_HEADS = DIFF_WIDTH // HEAD_DIM
DIFF_QK_DIM = HEAD_DIM // 2
IN_WIDTH = SSM_WIDTH + 3 * DIL_WIDTH + 3 * DIFF_WIDTH
Q_BLOCK = 128
PEER_HEADS = 8
PEER_KEYS = 128
PEER_EXPERTS = PEER_KEYS * PEER_KEYS
PEER_TOPK = 16
PEER_QUERY_DIM = 256
PEER_HALF = PEER_QUERY_DIM // 2
PEER_TOKEN_BLOCK = 128
NORM_EPS = 1e-6

kernel_name = "hybrid_s5_dilated_diffattn_peer"

def rms_norm(x, gain):
    xf = x.astype(jnp.float32)
    y = xf * lax.rsqrt(jnp.mean(xf * xf, axis=-1, keepdims=True) + NORM_EPS)
    return (y * gain.astype(jnp.float32)).astype(x.dtype)

def _linear_recurrence_combine(left, right):
    a_l, b_l = left
    a_r, b_r = right
    return a_r * a_l, a_r * b_l + b_r

def s5_mixer(u, lam_re, lam_im, log_step, b_re, b_im, c_re, c_im, d_skip):
    f32 = jnp.float32
    bsz, seq, _ = u.shape
    uf = u.astype(f32).reshape(bsz, seq, SSM_GROUPS, SSM_GROUP_CH)
    lam = lax.complex(lam_re.astype(f32), lam_im.astype(f32))
    step = jnp.exp(log_step.astype(f32))[:, None]
    lam_bar = jnp.exp(lam * step)
    b_mat = lax.complex(b_re.astype(f32), b_im.astype(f32))
    b_bar = ((lam_bar - 1.0) / lam)[:, :, None] * b_mat
    bu = jnp.einsum("gpc,blgc->blgp", b_bar, uf.astype(jnp.complex64))
    decay = jnp.broadcast_to(lam_bar, bu.shape)
    _, states = lax.associative_scan(_linear_recurrence_combine, (decay, bu), axis=1)
    c_mat = lax.complex(c_re.astype(f32), c_im.astype(f32))
    y = jnp.real(jnp.einsum("gcp,blgp->blgc", c_mat, states))
    y = y + d_skip.astype(f32).reshape(SSM_GROUPS, SSM_GROUP_CH) * uf
    return y.reshape(bsz, seq, SSM_WIDTH)

def dilated_attention(q, k, v):
    f32 = jnp.float32
    bsz, seq, _ = q.shape
    q = q.reshape(bsz, seq, DIL_HEADS, HEAD_DIM).transpose(0, 2, 1, 3)
    k = k.reshape(bsz, seq, DIL_HEADS, HEAD_DIM).transpose(0, 2, 1, 3)
    v = v.reshape(bsz, seq, DIL_HEADS, HEAD_DIM).transpose(0, 2, 1, 3)
    n_blk = seq // Q_BLOCK
    q_blocks = q.reshape(bsz, DIL_HEADS, n_blk, Q_BLOCK, HEAD_DIM).transpose(2, 0, 1, 3, 4)
    scale = HEAD_DIM ** -0.5

    def one_block(args):
        qb, blk = args
        pos = blk * Q_BLOCK + jnp.arange(Q_BLOCK)
        outs, lses = [], []
        for window, dil in DIL_PATTERNS:
            offs = dil * jnp.arange(window // dil + 1)
            idx = pos[:, None] - offs[None, :]
            valid = idx >= 0
            idx = jnp.maximum(idx, 0)
            kg = k[:, :, idx]
            vg = v[:, :, idx]
            s = jnp.einsum("bhqd,bhqjd->bhqj", qb, kg).astype(f32) * scale
            s = jnp.where(valid, s, -jnp.inf)
            m = jnp.max(s, axis=-1, keepdims=True)
            p = jnp.exp(s - m)
            den = jnp.sum(p, axis=-1, keepdims=True)
            outs.append(jnp.einsum("bhqj,bhqjd->bhqd", p / den, vg.astype(f32)))
            lses.append(m[..., 0] + jnp.log(den[..., 0]))
        weights = jax.nn.softmax(jnp.stack(lses), axis=0)
        return jnp.sum(weights[..., None] * jnp.stack(outs), axis=0)

    out = lax.map(one_block, (q_blocks, jnp.arange(n_blk)))
    return out.transpose(1, 0, 3, 2, 4).reshape(bsz, seq, DIL_WIDTH)

def diff_attention(q, k, v, lam_q1, lam_k1, lam_q2, lam_k2, subln_g, lambda_init):
    f32 = jnp.float32
    bsz, seq, _ = q.shape
    q = q.reshape(bsz, seq, DIFF_HEADS, 2, DIFF_QK_DIM).transpose(0, 2, 3, 1, 4)
    k = k.reshape(bsz, seq, DIFF_HEADS, 2, DIFF_QK_DIM).transpose(0, 2, 3, 1, 4)
    v = v.reshape(bsz, seq, DIFF_HEADS, HEAD_DIM).transpose(0, 2, 1, 3).astype(f32)
    lam = (jnp.exp(jnp.sum(lam_q1.astype(f32) * lam_k1.astype(f32)))
           - jnp.exp(jnp.sum(lam_q2.astype(f32) * lam_k2.astype(f32))) + lambda_init)
    n_blk = seq // Q_BLOCK
    q_blocks = q.reshape(bsz, DIFF_HEADS, 2, n_blk, Q_BLOCK, DIFF_QK_DIM).transpose(3, 0, 1, 2, 4, 5)
    key_pos = jnp.arange(seq)
    scale = DIFF_QK_DIM ** -0.5

    def one_block(args):
        qb, blk = args
        pos = blk * Q_BLOCK + jnp.arange(Q_BLOCK)
        s = jnp.einsum("bhmqd,bhmkd->bhmqk", qb, k).astype(f32) * scale
        s = jnp.where(key_pos[None, :] <= pos[:, None], s, -jnp.inf)
        p = jax.nn.softmax(s, axis=-1)
        attn = p[:, :, 0] - lam * p[:, :, 1]
        return jnp.einsum("bhqk,bhkd->bhqd", attn, v)

    out = lax.map(one_block, (q_blocks, jnp.arange(n_blk)))
    out = out.transpose(1, 0, 3, 2, 4)
    out = rms_norm(out, subln_g) * (1.0 - lambda_init)
    return out.reshape(bsz, seq, DIFF_WIDTH)

def hybrid_mixer(h, w_in, lam_re, lam_im, log_step, b_re, b_im, c_re, c_im, d_skip,
                 w_glu, ssm_norm_g, dil_norm_g, lam_q1, lam_k1, lam_q2, lam_k2, subln_g,
                 w_out, lambda_init):
    proj = h @ w_in
    cuts = [SSM_WIDTH,
            SSM_WIDTH + DIL_WIDTH,
            SSM_WIDTH + 2 * DIL_WIDTH,
            SSM_WIDTH + 3 * DIL_WIDTH,
            SSM_WIDTH + 3 * DIL_WIDTH + DIFF_WIDTH,
            SSM_WIDTH + 3 * DIL_WIDTH + 2 * DIFF_WIDTH]
    u_ssm, dq, dk, dv, fq, fk, fv = jnp.split(proj, cuts, axis=-1)
    y = s5_mixer(u_ssm, lam_re, lam_im, log_step, b_re, b_im, c_re, c_im, d_skip)
    g = jax.nn.gelu(y)
    y = g * jax.nn.sigmoid(g @ w_glu.astype(jnp.float32))
    y_ssm = rms_norm(y, ssm_norm_g).astype(h.dtype)
    y_dil = rms_norm(dilated_attention(dq, dk, dv), dil_norm_g).astype(h.dtype)
    y_diff = diff_attention(fq, fk, fv, lam_q1, lam_k1, lam_q2, lam_k2, subln_g,
                            lambda_init).astype(h.dtype)
    return jnp.concatenate([y_ssm, y_dil, y_diff], axis=-1) @ w_out

def peer_ffn(h, w_query, sub_keys, u_exp, v_exp):
    f32 = jnp.float32
    bsz, seq, dm = h.shape
    flat = h.reshape(-1, dm)
    n_chunks = flat.shape[0] // PEER_TOKEN_BLOCK
    chunks = flat.reshape(n_chunks, PEER_TOKEN_BLOCK, dm)

    def one_chunk(xc):
        q = (xc @ w_query).reshape(PEER_TOKEN_BLOCK, PEER_HEADS, 2, PEER_HALF)
        s = jnp.einsum("thcd,hcnd->thcn", q, sub_keys).astype(f32)
        top_s, top_i = lax.top_k(s, PEER_TOPK)
        cand_s = top_s[:, :, 0, :, None] + top_s[:, :, 1, None, :]
        cand_i = top_i[:, :, 0, :, None] * PEER_KEYS + top_i[:, :, 1, None, :]
        cand_s = cand_s.reshape(PEER_TOKEN_BLOCK, PEER_HEADS, PEER_TOPK * PEER_TOPK)
        cand_i = cand_i.reshape(PEER_TOKEN_BLOCK, PEER_HEADS, PEER_TOPK * PEER_TOPK)
        best_s, best_j = lax.top_k(cand_s, PEER_TOPK)
        expert = jnp.take_along_axis(cand_i, best_j, axis=-1)
        gate = jax.nn.softmax(best_s, axis=-1)
        u = u_exp[expert]
        act = jax.nn.gelu(jnp.einsum("thkd,td->thk", u, xc).astype(f32))
        vv = v_exp[expert]
        return jnp.einsum("thk,thkd->td", (gate * act).astype(vv.dtype), vv).astype(xc.dtype)

    out = lax.map(one_chunk, chunks)
    return out.reshape(bsz, seq, dm)

def setup_inputs(seed: int = 0) -> dict:
    key = jax.random.key(seed)
    ks = jax.random.split(key, 26)
    f32 = jnp.float32

    def nrm(k, shape, scale):
        return scale * jax.random.normal(k, shape, f32)

    def gain(k, shape):
        return 1.0 + 0.02 * jax.random.normal(k, shape, f32)

    L = DEPTH
    x = jax.random.normal(ks[0], (BATCH, SEQ, D_MODEL), f32)
    norm1_g = gain(ks[1], (L, D_MODEL))
    w_in = nrm(ks[2], (L, D_MODEL, IN_WIDTH), D_MODEL ** -0.5)
    ssm_lam_re = -0.5 + nrm(ks[3], (L, SSM_GROUPS, SSM_STATE), 0.01)
    ssm_lam_im = jnp.pi * jnp.arange(SSM_STATE, dtype=f32) + nrm(ks[4], (L, SSM_GROUPS, SSM_STATE), 0.01)
    ssm_log_step = jax.random.uniform(ks[5], (L, SSM_GROUPS), f32,
                                      minval=math.log(1e-3), maxval=math.log(1e-1))
    ssm_b_re = nrm(ks[6], (L, SSM_GROUPS, SSM_STATE, SSM_GROUP_CH), (2 * SSM_GROUP_CH) ** -0.5)
    ssm_b_im = nrm(ks[7], (L, SSM_GROUPS, SSM_STATE, SSM_GROUP_CH), (2 * SSM_GROUP_CH) ** -0.5)
    ssm_c_re = nrm(ks[8], (L, SSM_GROUPS, SSM_GROUP_CH, SSM_STATE), SSM_STATE ** -0.5)
    ssm_c_im = nrm(ks[9], (L, SSM_GROUPS, SSM_GROUP_CH, SSM_STATE), SSM_STATE ** -0.5)
    ssm_d = nrm(ks[10], (L, SSM_WIDTH), 1.0)
    ssm_w_glu = nrm(ks[11], (L, SSM_WIDTH, SSM_WIDTH), SSM_WIDTH ** -0.5)
    ssm_norm_g = gain(ks[12], (L, SSM_WIDTH))
    dil_norm_g = gain(ks[13], (L, DIL_WIDTH))
    diff_lam_q1 = nrm(ks[14], (L, DIFF_QK_DIM), 0.1)
    diff_lam_k1 = nrm(ks[15], (L, DIFF_QK_DIM), 0.1)
    diff_lam_q2 = nrm(ks[16], (L, DIFF_QK_DIM), 0.1)
    diff_lam_k2 = nrm(ks[17], (L, DIFF_QK_DIM), 0.1)
    diff_subln_g = gain(ks[18], (L, HEAD_DIM))
    w_out = nrm(ks[19], (L, MIX_WIDTH, D_MODEL), MIX_WIDTH ** -0.5)
    norm2_g = gain(ks[20], (L, D_MODEL))
    peer_w_query = nrm(ks[21], (L, D_MODEL, PEER_HEADS * PEER_QUERY_DIM), D_MODEL ** -0.5)
    peer_sub_keys = nrm(ks[22], (L, PEER_HEADS, 2, PEER_KEYS, PEER_HALF), PEER_HALF ** -0.5)
    peer_u = nrm(ks[23], (L, PEER_EXPERTS, D_MODEL), D_MODEL ** -0.5)
    peer_v = nrm(ks[24], (L, PEER_EXPERTS, D_MODEL), PEER_HEADS ** -0.5)
    final_norm_g = gain(ks[25], (D_MODEL,))
    return {"x": x, "norm1_g": norm1_g, "w_in": w_in,
            "ssm_lam_re": ssm_lam_re, "ssm_lam_im": ssm_lam_im, "ssm_log_step": ssm_log_step,
            "ssm_b_re": ssm_b_re, "ssm_b_im": ssm_b_im, "ssm_c_re": ssm_c_re, "ssm_c_im": ssm_c_im,
            "ssm_d": ssm_d, "ssm_w_glu": ssm_w_glu, "ssm_norm_g": ssm_norm_g, "dil_norm_g": dil_norm_g,
            "diff_lam_q1": diff_lam_q1, "diff_lam_k1": diff_lam_k1, "diff_lam_q2": diff_lam_q2,
            "diff_lam_k2": diff_lam_k2, "diff_subln_g": diff_subln_g, "w_out": w_out,
            "norm2_g": norm2_g, "peer_w_query": peer_w_query, "peer_sub_keys": peer_sub_keys,
            "peer_u": peer_u, "peer_v": peer_v, "final_norm_g": final_norm_g}

def reference(x, norm1_g, w_in, ssm_lam_re, ssm_lam_im, ssm_log_step, ssm_b_re, ssm_b_im,
              ssm_c_re, ssm_c_im, ssm_d, ssm_w_glu, ssm_norm_g, dil_norm_g, diff_lam_q1,
              diff_lam_k1, diff_lam_q2, diff_lam_k2, diff_subln_g, w_out, norm2_g,
              peer_w_query, peer_sub_keys, peer_u, peer_v, final_norm_g):
    for layer in range(DEPTH):
        lambda_init = 0.8 - 0.6 * math.exp(-0.3 * layer)
        h = rms_norm(x, norm1_g[layer])
        x = x + hybrid_mixer(h, w_in[layer], ssm_lam_re[layer], ssm_lam_im[layer],
                             ssm_log_step[layer], ssm_b_re[layer], ssm_b_im[layer],
                             ssm_c_re[layer], ssm_c_im[layer], ssm_d[layer], ssm_w_glu[layer],
                             ssm_norm_g[layer], dil_norm_g[layer], diff_lam_q1[layer],
                             diff_lam_k1[layer], diff_lam_q2[layer], diff_lam_k2[layer],
                             diff_subln_g[layer], w_out[layer], lambda_init)
        h = rms_norm(x, norm2_g[layer])
        x = x + peer_ffn(h, peer_w_query[layer], peer_sub_keys[layer], peer_u[layer], peer_v[layer])
    return rms_norm(x, final_norm_g)


_drawn_inputs = setup_inputs


def setup_inputs(seed=0):
    import zlib

    import numpy as np

    out = dict(_drawn_inputs(seed))
    spreads = {}
    factors = {}
    for name, (base, spread) in spreads.items():
        noise = np.random.default_rng([zlib.crc32(name.encode()), seed]).standard_normal(out[name].shape)
        drawn = base * np.exp(spread * noise) if base else spread * noise
        out[name] = __import__('jax').numpy.asarray(drawn.astype(out[name].dtype))
    for name, factor in factors.items():
        out[name] = (out[name] * factor).astype(out[name].dtype)
    return out
```

```python
from contextlib import ExitStack

import concourse.bass as bass
from concourse import mybir

ALU = mybir.AluOpType
ACT = mybir.ActivationFunctionType
AX_X = mybir.AxisListType.X
F32 = mybir.dt.float32
I32 = mybir.dt.int32
U32 = mybir.dt.uint32

P = 128
D = 1024
KT = D // P
L = 2
CHUNKS = 2
STAGES = L * CHUNKS
EPS = 1e-6
PI = 3.14159265358979

SSM_W, DIL_W, DIFF_W = 384, 384, 256
SSM_T = SSM_W // P
GROUPS, GROUP_CH, STATE = 24, 16, 64
ST = GROUPS * STATE // P
SQ = 4
DIL_HEADS, DIFF_HEADS, HD, DQK = 6, 4, 64, 32
HEADS, TOPK, KEYS = 8, 16, 128
HC = 2 * HEADS
SLOTS = HEADS * TOPK
EXPERTS = KEYS * KEYS

RING = 8
HALF = RING // 2
ITERS = SLOTS // RING

WB = 2048
W_SLOTS = 4
B_IN, B_SSM, B_OUT, B_QUERY, B_KEYS = 0, 9, 10, 14, 22
BLOCKS = 23
W_PER_SLOT = [len(range(j, BLOCKS, W_SLOTS)) for j in range(W_SLOTS)]

ROW_FIELDS = [("g2", D), ("mask_dil", 2 * P), ("mask_diff", 2 * P), ("c_re", ST * 32), ("c_im", ST * 32),
              ("d_skip", SSM_T), ("quarter", SQ), ("g1", KT), ("gy", KT), ("lam_re", ST), ("lam_im", ST), ("log_step", ST),
              ("lam_q1", DQK), ("lam_k1", DQK), ("lam_q2", DQK), ("lam_k2", DQK),
              ("lambda_init", 1), ("one_less_init", 1), ("first_expert", 1)]
ROW_AT, _at = {}, 0
for _name, _n in ROW_FIELDS:
    ROW_AT[_name] = (_at, _n)
    _at += _n
ROWS_W = _at

GELU_A = 0.7978845608028654
GELU_B = GELU_A * 0.044715
DIL_SCALE = HD ** -0.5
DIFF_SCALE = DQK ** -0.5
ROUND = 1.5 * 2.0 ** 23
RSQRT_SEED = float(0x5F3759DF)

VEC_STEPS = 375

AFTER_PART = [1, 0, 1, 0, 0, 1, 1, 1, 1, 1, 0, 1, 0, 1, 1, 0, 1, 0, 1, 0, 1, 1, 2]


def trunk(nc, x_in, wts, rows_in_dram, uv, ident_in, final_g, out):
    with ExitStack() as ctx:
        def sb(name, width, dt=F32):
            return ctx.enter_context(nc.sbuf_tensor(name, [P, width], dt))

        def sem(name):
            return ctx.enter_context(nc.semaphore(name))

        ring = sb("ring", RING * 2 * D)
        wring = sb("wring", W_SLOTS * WB)
        x = sb("x", CHUNKS * D)
        hy = sb("hy", D)
        h2 = sb("h2", D)
        h2_cur = sb("h2_cur", D)
        hT = sb("hT", KT * P)
        uqT = sb("uqT", 6 * P)
        fqT = sb("fqT", 2 * P)
        kT = sb("kT", 3 * 2 * P)
        fkT = sb("fkT", 2 * 2 * P)
        dv = sb("dv", 2 * DIL_W)
        fv = sb("fv", 2 * DIFF_W)
        rows = sb("rows", ROWS_W)
        cos = sb("cos", ST * P)
        sin = sb("sin", ST * P)
        crot = sb("crot", 3 * ST * 32)
        ddiag = sb("ddiag", SSM_W)
        work = sb("work", 7680)
        ident = sb("ident", P)
        diag = sb("diag", RING * P)
        carry = sb("carry", (STAGES + 1) * 2 * ST)
        small = sb("small", 640)
        gate = sb("gate", 2 * SLOTS)
        idx = sb("idx", 2 * SLOTS, I32)
        idx_stage = sb("idx_stage", RING, I32)
        peer = sb("peer", 4 * RING)

        def row(name):
            a, n = ROW_AT[name]
            return rows[:, a:a + n]

        taken = [0]

        def tiny(n, dt=F32):
            a = small[:, taken[0]:taken[0] + n]
            taken[0] += n
            assert taken[0] <= 640
            return a

        v_re, v_im, z_re, z_im = (work[:, 512 * i:512 * i + 512] for i in range(4))
        p_cr, p_si, p_sr, p_ci = (work[:, 2048 + 512 * i:2560 + 512 * i] for i in range(4))
        dbl = [work[:, 2048 + 768 * i:2048 + 768 * i + 768] for i in range(2)]
        y_sq, y_in, y_th, g_x2, g_T, glu_th, y_glu = (work[:, 384 * i:384 * i + 384] for i in range(7))
        u_spread = work[:, 4096:5632]
        probs = work[:, 4096:6144]
        pT = work[:, 6144:7680]
        wide_a, wide_b, wide_c = (work[:, 2048 * i:2048 * i + 2048] for i in range(3))
        p2 = work[:, 0:256]
        o_sq = work[:, 256:512]

        wslot = [wring[:, WB * j:WB * (j + 1)] for j in range(W_SLOTS)]
        u_of = [ring[:, 2 * D * r:2 * D * r + D] for r in range(RING)]
        v_of = [ring[:, 2 * D * r + D:2 * D * (r + 1)] for r in range(RING)]
        w_as = lambda b, k, n: wslot[b % W_SLOTS].rearrange("p (k n) -> p k n", k=k)[:, :, 0:n]
        ssm_w = wslot[B_SSM % W_SLOTS]
        w_glu = ssm_w[:, 0:SSM_T * SSM_W].rearrange("p (k n) -> p k n", k=SSM_T)
        b_re = ssm_w[:, 1152:1536].rearrange("p (k n) -> p k n", k=3)
        b_im = ssm_w[:, 1536:1920].rearrange("p (k n) -> p k n", k=3)

        ssq, ms, rstd, nt = tiny(1), tiny(4), tiny(4), tiny(4)
        ti_a = tiny(4)
        step_t, theta, rad, turn_n = (tiny(ST) for _ in range(4))
        cos1, sin1, f_re, f_im, ta, tb = (tiny(ST) for _ in range(6))
        lam = tiny(1)
        lsum = tiny(2)
        lexp = tiny(2)
        nmax = tiny(14)
        den = tiny(14)
        rden = tiny(14)
        ssq4 = tiny(4)
        lprod = tiny(DQK)
        gsum, grec = tiny(HEADS), tiny(HEADS)
        iota16 = tiny(TOPK)

        top_s = sb("top_s", HC * TOPK)
        top_i = sb("top_i", HC * TOPK, U32)
        top_f = sb("top_f", HC * TOPK)
        best_s = sb("best_s", SLOTS)
        best_j = sb("best_j", SLOTS, U32)
        jpart = sb("jpart", SLOTS, U32)
        jf = sb("jf", SLOTS)
        e_row = sb("e_row", SLOTS)
        e_col = sb("e_col", SLOTS)

        acc = ctx.enter_context(nc.psum_tensor("acc", [P, 2, 512], F32))
        bank = [ctx.enter_context(nc.psum_tensor(f"bank{i}", [P, 512], F32)) for i in range(6)]

        class Signal:

            def __init__(self, name, per_stage=1, before=0):
                self.sem, self.n, self.before = sem(name), per_stage, before

            def at(self, s, k=1):
                return s * self.n + (self.before + k)

        consts_in = sem("consts_in")
        rows_in = sem("rows_in")
        w_in = [sem(f"w_in{j}") for j in range(W_SLOTS)]
        w_free = Signal("w_free", BLOCKS, W_SLOTS)
        x_ready = Signal("x_ready", 1, 2)
        mixer_done = Signal("mixer_done")
        mem_ready = sem("mem_ready")
        iota_ready = sem("iota_ready")
        sep = sem("sep")

        ssq_done = Signal("ssq_done", 4)
        rstd_ready = Signal("rstd_ready")
        hn_ready = Signal("hn_ready")
        hn_turned = Signal("hn_turned", 2)
        hT_ready = Signal("hT_ready", 2)
        proj_done = Signal("proj_done", 5)
        proj_kept = Signal("proj_kept", 8)
        par_exp = Signal("par_exp", 3)
        par_vec = Signal("par_vec", 4)
        spread_ready = Signal("spread_ready", 3)
        tables_ready = Signal("tables_ready")
        bu_done = Signal("bu_done", 3)
        bu_free = Signal("bu_free", 3)
        prod_ready = Signal("prod_ready", 3)
        y_part = Signal("y_part", 3)
        y_sq_ready = Signal("y_sq_ready")
        y_in_ready = Signal("y_in_ready")
        y_th_ready = Signal("y_th_ready")
        g_ready = Signal("g_ready")
        g_turned = Signal("g_turned")
        gT_ready = Signal("gT_ready")
        glu_done = Signal("glu_done")
        glu_th_ready = Signal("glu_th_ready")
        ysum_ready = Signal("ysum_ready", 2)
        scores_done = Signal("scores_done", 7)
        masked_ready = Signal("masked_ready", 14)
        exp_ready = Signal("exp_ready", 14)
        attn_ready = Signal("attn_ready", 4)
        p_turned = Signal("p_turned", 5)
        pT_ready = Signal("pT_ready", 5)
        o_done = Signal("o_done", 2)
        y_ready = Signal("y_ready")
        y_turned = Signal("y_turned", 2)
        yT_ready = Signal("yT_ready", 2)
        mixed_done = Signal("mixed_done", 2)
        x_mid = Signal("x_mid")
        h2_ready = Signal("h2_ready")
        h2_turned = Signal("h2_turned", 2)
        h2T_ready = Signal("h2T_ready", 2)
        q_done = Signal("q_done", 4)
        q_kept = Signal("q_kept", 4)
        key_scores_done = Signal("key_scores_done", 4)
        key_scores_kept = Signal("key_scores_kept", 4)
        gate_in = Signal("gate_in")
        gate_exp = Signal("gate_exp")
        vec = Signal("vec_step", VEC_STEPS)

        handed = Signal("handed")
        staged = Signal("staged", 2 * ITERS)
        gathered = [Signal(f"gathered{r}", ITERS) for r in range(RING)]
        dots_done = Signal("dots_done", SLOTS)
        gelu_step = Signal("gelu_step", 3 * 2 * ITERS)
        inner_ready = Signal("inner_ready", 2 * ITERS)
        tanh_ready = Signal("tanh_ready", 2 * ITERS)
        weight_ready = Signal("weight_ready", 2 * ITERS)
        diag_ready = Signal("diag_ready", SLOTS)
        slot_free = Signal("slot_free", SLOTS, RING)
        copied = Signal("copied", 1)
        fin_ssq, fin_vec, fin_rows = sem("fin_ssq"), sem("fin_vec"), sem("fin_rows")
        stored = sem("stored")

        def chunk_cols(s, width):
            return bass.ds((s & 1) * width, width)

        def slot_cols(p, i, q):
            return bass.ds((p & 1) * SLOTS + i * RING + HALF * q, HALF)

        def apart(eng, sem_, value):
            eng.wait_ge(sem_, value)
            eng.sem_inc(sep, 1)

        block = ctx.enter_context(nc.Block())

        def load_stage(sp, s):
            if not (type(s) is int and s == 0):
                sp.wait_ge(mixer_done.sem, mixer_done.at(s, 0))
            sp.dma_start(rows[:, :], rows_in_dram[bass.ds(s, 1)].rearrange("a p n -> (a p) n")).then_inc(rows_in, 16)
            for b in range(BLOCKS):
                j = b % W_SLOTS
                sp.wait_ge(w_free.sem, s * BLOCKS + b + (2 if b < BLOCKS % W_SLOTS else 1))
                src = wts[bass.ds((s // 2) * BLOCKS + b, 1)].rearrange("a p n -> (a p) n")
                sp.dma_start(wslot[j], src).then_inc(w_in[j], 16)

        @block.sync
        def _(sp):
            sp.dma_start(x[:, :].rearrange("p (c d) -> p c d", c=CHUNKS),
                         x_in.rearrange("a (c p) d -> p (a c) d", p=P)).then_inc(consts_in, 16)
            sp.dma_start(ident[:, :], ident_in).then_inc(consts_in, 16)
            load_stage(sp, 0)
            with sp.Fori(1, STAGES) as s:
                load_stage(sp, s)
            sp.wait_ge(mixer_done.sem, STAGES)
            sp.dma_start(rows[:, 0:D], final_g).then_inc(fin_rows, 16)
            for c in range(CHUNKS):
                sp.wait_ge(fin_vec, c + 1)
                sp.dma_start(out[0, P * c:P * (c + 1), :], work[:, D * c:D * (c + 1)]).then_inc(stored, 16)
            sp.wait_ge(stored, 16 * CHUNKS)

        def block_here(eng, s, b):
            j = b % W_SLOTS
            eng.wait_ge(w_in[j], s * (16 * W_PER_SLOT[j]) + 16 * (b // W_SLOTS + 1))

        def dil_scores(h):
            return (bank[3], bank[4], bank[3], bank[4], bank[5], bank[1])[h], 256 * (h in (2, 3))

        def diff_scores(h, m):
            return (bank[4], bank[5], bank[1], bank[2])[2 * (h % 2) + m], 256 * (h // 2)

        dil_turn = (bank[2], bank[3], bank[1])
        diff_turn = (bank[3], bank[4])

        def mixer_pe(pe, s):
            mm = nc.tensor.matmul

            def turn(src, ready, banks, done):
                for j in range(2):
                    for k in range(4):
                        t = 4 * j + k
                        last = nc.tensor.transpose(banks[j][:, P * k:P * (k + 1)], src[:, P * t:P * (t + 1)], ident[:, :])
                    last.then_inc(done.sem, 1)

            pe.wait_ge(hn_ready.sem, hn_ready.at(s))
            turn(hy, None, bank[0:2], hn_turned)
            yield

            pe.wait_ge(hT_ready.sem, hT_ready.at(s, 2))
            for i in range(18):
                b = B_IN + i // 2
                if i % 2 == 0:
                    block_here(pe, s, b)
                w = w_as(b, KT, 256)[:, :, P * (i % 2):P * (i % 2 + 1)]
                o = bank[i // 4][:, P * (i % 4):P * (i % 4 + 1)]
                for k in range(KT):
                    h = hT[:, P * k:P * (k + 1)]
                    lhsT, rhs = (h, w[:, k, :]) if i in (9, 10, 11, 16, 17) else (w[:, k, :], h)
                    last = mm(o, lhsT, rhs, start=(k == 0), stop=(k == KT - 1))
                    if k == KT - 1 and i % 2:
                        last.then_inc(w_free.sem, 1)
                if i % 4 == 3 or i == 17:


                    pe.wait_ge(w_free.sem, w_free.at(s, b + 1))
                    pe.sem_inc(proj_done.sem, 1)
                    yield

            block_here(pe, s, B_SSM)
            for g in range(3):
                pe.wait_ge(proj_kept.sem, proj_kept.at(s, (3, 7, 8)[g]))
                pe.wait_ge(spread_ready.sem, spread_ready.at(s, g + 1))
                for b_w, o in ((b_re, bank[2 * g]), (b_im, bank[2 * g + 1])):
                    last = mm(o[:, :], b_w[:, g, :], u_spread[:, 512 * g:512 * (g + 1)], start=True, stop=True)
                last.then_inc(bu_done.sem, 1)
            y_ps = bank[0]
            pe.wait_ge(tables_ready.sem, tables_ready.at(s))
            pe.wait_ge(bu_free.sem, bu_free.at(s, 1))
            for i in range(SSM_T):
                mm(y_ps[:, P * i:P * (i + 1)], uqT[:, P * i:P * (i + 1)], ddiag[:, P * i:P * (i + 1)],
                   start=(i == 0), stop=False, skip_group_check=True)
            cr = crot[:, :].rearrange("p (c j n) -> p c j n", c=3, j=ST)
            for g in range(3):
                pe.wait_ge(prod_ready.sem, prod_ready.at(s, g + 1))
                for j in range(SQ):
                    t = SQ * g + j
                    for prod, which in ((p_cr, 0), (p_si, 1), (p_sr, 2), (p_ci, 2)):
                        last = mm(y_ps[:, 32 * t:32 * t + 32], prod[:, P * j:P * (j + 1)], cr[:, which, t, :],
                                  start=False, stop=False, skip_group_check=True)
                last.then_inc(y_part.sem, 1)
                yield

            pe.wait_ge(g_ready.sem, g_ready.at(s))
            for i in range(SSM_T):
                last = nc.tensor.transpose(bank[1][:, P * i:P * (i + 1)], g_x2[:, P * i:P * (i + 1)], ident[:, :])
            last.then_inc(g_turned.sem, 1)
            pe.wait_ge(gT_ready.sem, gT_ready.at(s))
            pe.wait_ge(bu_free.sem, bu_free.at(s, 3))
            for i in range(SSM_T):
                last = mm(bank[2][:, 0:SSM_W], g_T[:, P * i:P * (i + 1)], w_glu[:, i, :],
                          start=(i == 0), stop=(i == SSM_T - 1))
            last.then_inc(glu_done.sem, 1)
            pe.wait_ge(glu_done.sem, glu_done.at(s))
            pe.sem_inc(w_free.sem, 1)
            yield

            for h in range(DIL_HEADS):
                a, i = HD * (h % 2), h // 2
                o, half = dil_scores(h)
                last = mm(o[:, half:half + 256], uqT[a:a + HD, P * (3 + i):P * (4 + i)],
                          kT[a:a + HD, 256 * i:256 * (i + 1)], start=True, stop=True)
                if h % 2:
                    last.then_inc(scores_done.sem, 1)
            yield
            for i, o in enumerate(dil_turn):
                pe.wait_ge(exp_ready.sem, exp_ready.at(s, (4, 4, 6)[i]))
                if i == 0:
                    pe.wait_ge(glu_th_ready.sem, glu_th_ready.at(s))
                for b in range(4):
                    last = nc.tensor.transpose(o[:, P * b:P * (b + 1)], probs[:, 512 * i + P * b:512 * i + P * (b + 1)],
                                               ident[:, :])
                last.then_inc(p_turned.sem, 1)
            for i in range(3):
                pe.wait_ge(pT_ready.sem, pT_ready.at(s, i + 1))
                for b in range(2):
                    h = 2 * i + b
                    for kc in range(2):
                        last = mm(bank[0][:, HD * h:HD * (h + 1)], pT[:, 512 * i + P * (2 * b + kc):512 * i + P * (2 * b + kc + 1)],
                                  dv[:, DIL_W * kc + HD * h:DIL_W * kc + HD * (h + 1)],
                                  start=(h == 0 and kc == 0), stop=False, skip_group_check=True)
            last.then_inc(o_done.sem, 1)
            yield

            for h in range(DIFF_HEADS):
                for m in range(2):
                    a = HD * (h % 2) + DQK * m
                    o, half = diff_scores(h, m)
                    last = mm(o[:, half:half + 256], fqT[a:a + DQK, P * (h // 2):P * (h // 2 + 1)],
                              fkT[a:a + DQK, 256 * (h // 2):256 * (h // 2 + 1)], start=True, stop=True)
                last.then_inc(scores_done.sem, 1)
            yield
            for i, o in enumerate(diff_turn):
                pe.wait_ge(attn_ready.sem, attn_ready.at(s, 2 * i + 2))
                for b in range(2):
                    for kc in range(2):
                        a = 512 * (2 * i + b) + P * kc
                        last = nc.tensor.transpose(o[:, P * (2 * b + kc):P * (2 * b + kc + 1)], probs[:, a:a + P], ident[:, :])
                last.then_inc(p_turned.sem, 1)
            for i in range(2):
                pe.wait_ge(pT_ready.sem, pT_ready.at(s, 4 + i))
                for b in range(2):
                    h = 2 * i + b
                    for kc in range(2):
                        a = 512 * i + P * (2 * b + kc)
                        last = mm(bank[5][:, HD * h:HD * (h + 1)], pT[:, a:a + P],
                                  fv[:, DIFF_W * kc + HD * h:DIFF_W * kc + HD * (h + 1)],
                                  start=(h == 0 and kc == 0), stop=False, skip_group_check=True)
            last.then_inc(o_done.sem, 1)
            yield

            pe.wait_ge(y_ready.sem, y_ready.at(s))
            turn(hy, None, bank[0:2], y_turned)
            pe.wait_ge(yT_ready.sem, yT_ready.at(s, 2))
            for n in range(4):
                b = B_OUT + n
                block_here(pe, s, b)
                w = w_as(b, KT, 256)
                for k in range(KT):
                    last = mm(bank[2 + n // 2][:, 256 * (n % 2):256 * (n % 2) + 256], hT[:, P * k:P * (k + 1)], w[:, k, :],
                              start=(k == 0), stop=(k == KT - 1))
                last.then_inc(w_free.sem, 1)
                if n % 2:
                    pe.wait_ge(w_free.sem, w_free.at(s, b + 1))
                    pe.sem_inc(mixed_done.sem, 1)
            yield

            pe.wait_ge(h2_ready.sem, h2_ready.at(s))
            turn(h2, None, bank[4:6], h2_turned)
            yield
            pe.wait_ge(h2T_ready.sem, h2T_ready.at(s, 2))
            for i in range(HC):
                b = B_QUERY + i // 2
                if i % 2 == 0:
                    block_here(pe, s, b)
                w = w_as(b, KT, 256)[:, :, P * (i % 2):P * (i % 2 + 1)]
                for k in range(KT):
                    last = mm(bank[i // 4][:, P * (i % 4):P * (i % 4 + 1)], w[:, k, :], hT[:, P * k:P * (k + 1)],
                              start=(k == 0), stop=(k == KT - 1))
                if i % 2:
                    last.then_inc(w_free.sem, 1)
                if i % 4 == 3:
                    pe.wait_ge(w_free.sem, w_free.at(s, b + 1))
                    pe.sem_inc(q_done.sem, 1)
                    yield
            block_here(pe, s, B_KEYS)
            keys = w_as(B_KEYS, HC, P)
            for n, o in enumerate((bank[4], bank[5], bank[0], bank[1])):
                pe.wait_ge(q_kept.sem, q_kept.at(s, n + 1))
                for i in range(4 * n, 4 * n + 4):
                    last = mm(o[:, P * (i % 4):P * (i % 4 + 1)], wide_c[:, P * i:P * (i + 1)], keys[:, i, :],
                              start=True, stop=True)
                last.then_inc(key_scores_done.sem, 1)
            pe.wait_ge(key_scores_done.sem, key_scores_done.at(s, 4))
            pe.sem_inc(w_free.sem, 1)
            yield
            yield
            yield

        def experts_pe_start(pe, p):
            pe.wait_ge(handed.sem, handed.at(p))
            apart(pe, x_ready.sem, x_ready.at(p, 0))
            xs = x[:, chunk_cols(p, D)]
            for n in range(2):
                nc.tensor.matmul(acc[:, n, :], ident[:, :], xs[:, 512 * n:512 * (n + 1)],
                                 start=True, stop=False, skip_group_check=True)

        def experts_pe(pe, p, i):
            for r in range(RING):
                pe.wait_ge(diag_ready.sem, diag_ready.at(p, i * RING + (r + 1)))
                for n in range(2):
                    last = nc.tensor.matmul(acc[:, n, :], diag[:, P * r:P * (r + 1)], v_of[r][:, 512 * n:512 * (n + 1)],
                                            start=False, stop=False, skip_group_check=True)
                last.then_inc(slot_free.sem, 1)

        def mixer_act(act, s):
            A = nc.scalar.activation
            xs = x[:, chunk_cols(s, D)]

            def keep(out_ap, in_ap, sig):
                A(out_ap, in_ap, ACT.Copy).then_inc(sig.sem, 1)

            apart(act, x_ready.sem, x_ready.at(s, -1))
            A(hy[:, :], xs, ACT.Square, accum_out=ssq).then_inc(ssq_done.sem, 1)
            apart(act, rstd_ready.sem, rstd_ready.at(s))
            A(hy[:, :], xs, ACT.Copy, scale=rstd[:, 0:1]).then_inc(hn_ready.sem, 1)
            yield

            kT3 = kT[:, :].rearrange("p (t c n) -> p t c n", t=3, c=2)
            fkT3 = fkT[:, :].rearrange("p (t c n) -> p t c n", t=2, c=2)
            one = bass.ds(s & 1, 1)

            def bk(i, a, b):
                return bank[i][:, P * a:P * b]

            act.wait_ge(par_vec.sem, par_vec.at(s, 1))
            A(step_t, row("log_step"), ACT.Exp).then_inc(par_exp.sem, 1)
            act.wait_ge(proj_done.sem, proj_done.at(s, 1))
            keep(uqT[:, 0:4 * P], bk(0, 0, 4), proj_kept)
            yield
            act.wait_ge(par_vec.sem, par_vec.at(s, 2))
            A(rad, ta, ACT.Exp).then_inc(par_exp.sem, 1)
            act.wait_ge(proj_done.sem, proj_done.at(s, 2))
            keep(uqT[:, 4 * P:6 * P], bk(1, 0, 2), proj_kept)
            keep(kT3[:, 0:2, one, :], bk(1, 2, 4).rearrange("p (t c n) -> p t c n", t=2, c=1), proj_kept)
            act.wait_ge(par_vec.sem, par_vec.at(s, 3))
            A(sin1, theta, ACT.Sin)
            A(cos1, tb, ACT.Sin).then_inc(par_exp.sem, 1)
            yield
            apart(act, proj_done.sem, proj_done.at(s, 3))
            keep(kT3[:, 2:3, one, :], bk(2, 0, 1).rearrange("p (t c n) -> p t c n", t=1, c=1), proj_kept)
            keep(dv[:, chunk_cols(s, DIL_W)], bk(2, 1, 4), proj_kept)
            yield
            act.wait_ge(par_vec.sem, par_vec.at(s, 4))
            A(lexp, lsum, ACT.Exp)
            act.wait_ge(proj_done.sem, proj_done.at(s, 4))
            keep(fqT[:, :], bk(3, 0, 2), proj_kept)
            keep(fkT3[:, :, one, :], bk(3, 2, 4).rearrange("p (t c n) -> p t c n", t=2, c=1), proj_kept)
            yield
            apart(act, proj_done.sem, proj_done.at(s, 5))
            keep(fv[:, chunk_cols(s, DIFF_W)], bk(4, 0, 2), proj_kept)
            yield
            yield
            yield
            yield

            act.wait_ge(y_part.sem, y_part.at(s, 3))
            A(y_sq, bank[0][:, 0:SSM_W], ACT.Square).then_inc(y_sq_ready.sem, 1)
            act.wait_ge(y_in_ready.sem, y_in_ready.at(s))
            A(y_th, y_in, ACT.Tanh).then_inc(y_th_ready.sem, 1)
            act.wait_ge(g_turned.sem, g_turned.at(s))
            A(g_T, bank[1][:, 0:SSM_W], ACT.Copy).then_inc(gT_ready.sem, 1)
            act.wait_ge(glu_done.sem, glu_done.at(s))
            A(glu_th, bank[2][:, 0:SSM_W], ACT.Tanh, scale=0.25).then_inc(glu_th_ready.sem, 1)
            act.wait_ge(ysum_ready.sem, ysum_ready.at(s, 1))
            A(y_sq, y_glu, ACT.Square, accum_out=ssq).then_inc(ssq_done.sem, 1)
            yield

            def soften(m):
                act.wait_ge(masked_ready.sem, masked_ready.at(s, m + 1))
                pm = probs[:, 256 * (m % 6 if m < 6 else m - 6):][:, 0:256]
                A(pm, pm, ACT.Exp, scale=-1.0, bias=nmax[:, m:m + 1], accum_out=den[:, m:m + 1]).then_inc(exp_ready.sem, 1)

            for m in range(6):
                soften(m)
            yield
            for i in range(3):
                act.wait_ge(p_turned.sem, p_turned.at(s, i + 1))
                A(pT[:, 512 * i:512 * (i + 1)], dil_turn[i][:, :], ACT.Copy).then_inc(pT_ready.sem, 1)
            act.wait_ge(ysum_ready.sem, ysum_ready.at(s, 2))
            A(y_sq, hy[:, SSM_W:SSM_W + DIL_W], ACT.Square, accum_out=ssq).then_inc(ssq_done.sem, 1)
            yield
            for m in range(6, 14):
                soften(m)
            yield
            for i in range(2):
                act.wait_ge(p_turned.sem, p_turned.at(s, 4 + i))
                A(pT[:, 512 * i:512 * (i + 1)], diff_turn[i][:, :], ACT.Copy).then_inc(pT_ready.sem, 1)
            yield
            yield
            apart(act, x_mid.sem, x_mid.at(s))
            A(hy[:, :], xs, ACT.Square, accum_out=ssq).then_inc(ssq_done.sem, 1)
            for j in range(2):
                act.wait_ge(h2_turned.sem, h2_turned.at(s, j + 1))
                A(hT[:, 512 * j:512 * (j + 1)], bank[4 + j][:, :], ACT.Copy).then_inc(h2T_ready.sem, 1)
            yield
            for n in range(4):
                act.wait_ge(q_done.sem, q_done.at(s, n + 1))
                A(wide_c[:, 512 * n:512 * (n + 1)], bank[n][:, :], ACT.Copy).then_inc(q_kept.sem, 1)
                yield
            for n, o in enumerate((bank[4], bank[5], bank[0], bank[1])):
                act.wait_ge(key_scores_done.sem, key_scores_done.at(s, n + 1))
                A(wide_a[:, 512 * n:512 * (n + 1)], o[:, :], ACT.Copy).then_inc(key_scores_kept.sem, 1)
            yield
            yield
            apart(act, gate_in.sem, gate_in.at(s))
            own_gate = gate[:, chunk_cols(s, SLOTS)]
            A(own_gate, own_gate, ACT.Exp).then_inc(gate_exp.sem, 1)
            yield

        def experts_act(act, p, i):
            for q in range(2):
                m = i * 2 + (q + 1)
                act.wait_ge(inner_ready.sem, inner_ready.at(p, 0) + m)
                inner = peer[:, RING:RING + HALF]
                nc.scalar.activation(peer[:, RING + HALF:2 * RING], inner, ACT.Tanh).then_inc(tanh_ready.sem, 1)
                act.wait_ge(weight_ready.sem, weight_ready.at(p, 0) + m)
                for r in range(HALF * q, HALF * (q + 1)):
                    nc.scalar.activation(diag[:, P * r:P * (r + 1)], ident[:, :], ACT.Copy,
                                         scale=peer[:, 2 * RING + r:2 * RING + r + 1]).then_inc(diag_ready.sem, 1)

        steps = [0]

        def mixer_dve(dve, s):
            V = nc.vector
            steps[0] = 0

            def step(ins):
                steps[0] += 1
                ins.then_inc(vec.sem, 1)

            def settle():
                dve.wait_ge(vec.sem, vec.at(s, steps[0]))

            def link(ins):
                step(ins)
                settle()

            def rsqrt(y, m, n):
                y, m, t = y[:, 0:n], m[:, 0:n], nt[:, 0:n]
                ti = ti_a[:, 0:n].bitcast(I32)
                link(V.tensor_scalar(ti, m.bitcast(I32), 1, None, ALU.logical_shift_right))
                link(V.tensor_scalar(y.bitcast(I32), ti, -1.0, RSQRT_SEED, ALU.mult, ALU.add))
                for _ in range(3):
                    link(V.tensor_tensor(t, y, y, ALU.mult))
                    link(V.tensor_tensor(t, t, m, ALU.mult))
                    link(V.tensor_scalar(t, t, -0.5, 1.5, ALU.mult, ALU.add))
                    link(V.tensor_tensor(y, y, t, ALU.mult))

            dve.wait_ge(ssq_done.sem, ssq_done.at(s, 1))
            link(V.tensor_scalar(ms[:, 0:1], ssq, 1.0 / D, EPS, ALU.mult, ALU.add))
            rsqrt(rstd, ms, 1)
            V.tensor_copy(rstd[:, 1:2], rstd[:, 0:1]).then_inc(rstd_ready.sem, 1)
            dve.wait_ge(rows_in, 16 * s + 16)
            hT3 = hT[:, :].rearrange("p (k n) -> p k n", k=KT)

            def turned_gain(banks, done, gain, ready):
                for j in range(2):
                    dve.wait_ge(done.sem, done.at(s, j + 1))
                    V.tensor_tensor(hT3[:, 4 * j:4 * j + 4, :], banks[j][:, :].rearrange("p (k n) -> p k n", k=4),
                                    gain[:, 4 * j:4 * j + 4].unsqueeze(2).broadcast_to([P, 4, P]),
                                    ALU.mult).then_inc(ready.sem, 1)

            turned_gain(bank[0:2], hn_turned, row("g1"), hT_ready)
            yield

            V.tensor_tensor(lprod, row("lam_q1"), row("lam_k1"), ALU.mult).then_inc(par_vec.sem, 1)
            dve.wait_ge(par_vec.sem, par_vec.at(s, 1))
            link(V.tensor_reduce(lsum[:, 0:1], lprod, AX_X, ALU.add))
            link(V.tensor_tensor(lprod, row("lam_q2"), row("lam_k2"), ALU.mult))
            link(V.tensor_reduce(lsum[:, 1:2], lprod, AX_X, ALU.add))
            dve.wait_ge(par_exp.sem, par_exp.at(s, 1))
            step(V.tensor_tensor(theta, row("lam_im"), step_t, ALU.mult))
            V.tensor_tensor(ta, row("lam_re"), step_t, ALU.mult).then_inc(par_vec.sem, 1)
            yield
            settle()
            link(V.tensor_scalar(turn_n, theta, 1.0 / (2 * PI), ROUND, ALU.mult, ALU.add))
            link(V.tensor_scalar(turn_n, turn_n, ROUND, None, ALU.subtract))
            for part in (6.28125, 0.001934051513671875, 1.2556659146e-06):
                link(V.scalar_tensor_tensor(theta, turn_n, -part, theta, ALU.mult, ALU.add))
            link(V.tensor_scalar(theta, theta, 3.1415925, -3.1415925, ALU.min, ALU.max))
            link(V.scalar_tensor_tensor(tb, theta, -1.0, theta, ALU.mult, ALU.max))
            V.tensor_scalar(tb, tb, -1.0, PI / 2, ALU.mult, ALU.add).then_inc(par_vec.sem, 1)
            dve.wait_ge(par_exp.sem, par_exp.at(s, 3))
            step(V.tensor_tensor(f_re, cos1, cos1, ALU.mult))
            link(V.tensor_tensor(f_im, sin1, sin1, ALU.mult))
            link(V.tensor_tensor(f_re, f_re, f_im, ALU.add))
            link(V.tensor_scalar(f_re, f_re, -0.5, 1.5, ALU.mult, ALU.add))
            step(V.tensor_tensor(cos1, cos1, f_re, ALU.mult))
            link(V.tensor_tensor(sin1, sin1, f_re, ALU.mult))
            step(V.tensor_tensor(f_re, rad, cos1, ALU.mult))
            link(V.tensor_tensor(f_im, rad, sin1, ALU.mult))
            link(V.tensor_scalar(f_re, f_re, 1.0, None, ALU.subtract))
            step(V.tensor_tensor(ta, row("lam_re"), row("lam_re"), ALU.mult))
            link(V.tensor_tensor(tb, row("lam_im"), row("lam_im"), ALU.mult))
            link(V.tensor_tensor(ta, ta, tb, ALU.add))
            link(V.reciprocal(turn_n, ta))
            step(V.tensor_tensor(ta, f_re, row("lam_re"), ALU.mult))
            step(V.tensor_tensor(tb, f_im, row("lam_im"), ALU.mult))
            step(V.tensor_tensor(theta, f_im, row("lam_re"), ALU.mult))
            link(V.tensor_tensor(step_t, f_re, row("lam_im"), ALU.mult))
            step(V.tensor_tensor(ta, ta, tb, ALU.add))
            link(V.tensor_tensor(theta, theta, step_t, ALU.subtract))
            step(V.tensor_tensor(f_re, ta, turn_n, ALU.mult))
            link(V.tensor_tensor(f_im, theta, turn_n, ALU.mult))
            V.tensor_copy(nt[:, 0:1], rstd[:, 0:1]).then_inc(par_vec.sem, 1)
            yield

            cos3 = cos[:, :].rearrange("p (j t) -> p j t", j=ST)
            sin3 = sin[:, :].rearrange("p (j t) -> p j t", j=ST)
            step(V.tensor_copy(cos3[:, :, 0:1], cos1.unsqueeze(2)))
            link(V.tensor_copy(sin3[:, :, 0:1], sin1.unsqueeze(2)))
            n = 1
            while n < P:
                t1, t2 = (d[:, 0:ST * n].rearrange("p (j t) -> p j t", j=ST) for d in dbl)
                cn = cos3[:, :, n - 1:n].broadcast_to([P, ST, n])
                sn = sin3[:, :, n - 1:n].broadcast_to([P, ST, n])
                step(V.tensor_tensor(t1, cos3[:, :, 0:n], cn, ALU.mult))
                link(V.tensor_tensor(t2, sin3[:, :, 0:n], sn, ALU.mult))
                link(V.tensor_tensor(cos3[:, :, n:2 * n], t1, t2, ALU.subtract))
                step(V.tensor_tensor(t1, cos3[:, :, 0:n], sn, ALU.mult))
                link(V.tensor_tensor(t2, sin3[:, :, 0:n], cn, ALU.mult))
                link(V.tensor_tensor(sin3[:, :, n:2 * n], t1, t2, ALU.add))
                n *= 2
            yield
            cr = crot[:, :].rearrange("p (c j n) -> p c j n", c=3, j=ST)
            c_re = row("c_re").rearrange("p (j n) -> p j n", j=ST)
            c_im = row("c_im").rearrange("p (j n) -> p j n", j=ST)
            fr = f_re.unsqueeze(2).broadcast_to([P, ST, 32])
            fi = f_im.unsqueeze(2).broadcast_to([P, ST, 32])
            t1, t2 = (d[:, 0:ST * 32].rearrange("p (j t) -> p j t", j=ST) for d in dbl)
            step(V.tensor_tensor(t1, c_re, fr, ALU.mult))
            link(V.tensor_tensor(t2, c_im, fi, ALU.mult))
            step(V.tensor_tensor(cr[:, 0], t1, t2, ALU.subtract))
            link(V.tensor_tensor(cr[:, 1], t2, t1, ALU.subtract))
            step(V.tensor_tensor(t1, c_re, fi, ALU.mult))
            link(V.tensor_tensor(t2, c_im, fr, ALU.mult))
            link(V.tensor_tensor(t1, t1, t2, ALU.add))
            step(V.tensor_scalar(cr[:, 2], t1, -1.0, None, ALU.mult))
            for i in range(SSM_T):
                ins = V.tensor_scalar(ddiag[:, P * i:P * (i + 1)], ident[:, :], row("d_skip")[:, i:i + 1], None, ALU.mult)
                if i < SSM_T - 1:
                    step(ins)
            ins.then_inc(tables_ready.sem, 1)
            yield
            dve.wait_ge(proj_kept.sem, proj_kept.at(s, 1))
            for g in range(3):
                V.tensor_tensor(u_spread[:, 512 * g:512 * (g + 1)].rearrange("p (j t) -> p j t", j=SQ),
                                uqT[:, P * g:P * (g + 1)].unsqueeze(1).broadcast_to([P, SQ, P]),
                                row("quarter").unsqueeze(2).broadcast_to([P, SQ, P]), ALU.mult).then_inc(spread_ready.sem, 1)
            yield

            w5 = 512
            start = carry[:, bass.ds(s * (2 * ST), 2 * ST)]
            keep_at = carry[:, bass.ds((s // 2) * (4 * ST) + 2 * ST, 2 * ST)]
            for g in range(3):
                dve.wait_ge(bu_done.sem, bu_done.at(s, g + 1))
                cg, sg = cos[:, w5 * g:w5 * (g + 1)], sin[:, w5 * g:w5 * (g + 1)]
                br, bi = bank[2 * g][:, :], bank[2 * g + 1][:, :]
                if g:
                    dve.wait_ge(y_part.sem, y_part.at(s, g))
                step(V.tensor_tensor(p_cr, br, cg, ALU.mult))
                step(V.tensor_tensor(p_si, bi, sg, ALU.mult))
                step(V.tensor_tensor(p_ci, bi, cg, ALU.mult))
                V.tensor_tensor(p_sr, br, sg, ALU.mult).then_inc(bu_free.sem, 1)
                dve.wait_ge(bu_free.sem, bu_free.at(s, g + 1))
                step(V.tensor_tensor(v_re, p_cr, p_si, ALU.add))
                link(V.tensor_tensor(v_im, p_ci, p_sr, ALU.subtract))
                for j in range(SQ):
                    t = SQ * g + j
                    decay = rad[:, t:t + 1].broadcast_to([P, P])
                    for part, (v, z) in enumerate(((v_re, z_re), (v_im, z_im))):
                        step(V.tensor_tensor_scan(z[:, P * j:P * (j + 1)], decay, v[:, P * j:P * (j + 1)],
                                                  start[:, ST * part + t:ST * part + t + 1], ALU.mult, ALU.add))
                settle()
                step(V.tensor_tensor(p_cr, cg, z_re, ALU.mult))
                step(V.tensor_tensor(p_si, sg, z_im, ALU.mult))
                step(V.tensor_tensor(p_sr, sg, z_re, ALU.mult))
                V.tensor_tensor(p_ci, cg, z_im, ALU.mult).then_inc(prod_ready.sem, 1)
                dve.wait_ge(prod_ready.sem, prod_ready.at(s, g + 1))
                last = lambda a: a.rearrange("p (j t) -> p j t", j=SQ)[:, :, P - 1]
                step(V.tensor_tensor(keep_at[:, SQ * g:SQ * (g + 1)], last(p_cr), last(p_si), ALU.subtract))
                step(V.tensor_tensor(keep_at[:, ST + SQ * g:ST + SQ * (g + 1)], last(p_sr), last(p_ci), ALU.add))
                settle()
                yield

            y_ps = bank[0][:, 0:SSM_W]
            dve.wait_ge(y_sq_ready.sem, y_sq_ready.at(s))
            link(V.tensor_scalar(y_in, y_sq, GELU_B, GELU_A, ALU.mult, ALU.add))
            V.tensor_tensor(y_in, y_in, y_ps, ALU.mult).then_inc(y_in_ready.sem, 1)
            dve.wait_ge(y_th_ready.sem, y_th_ready.at(s))
            V.scalar_tensor_tensor(g_x2, y_th, 1.0, y_ps, ALU.add, ALU.mult).then_inc(g_ready.sem, 1)
            dve.wait_ge(glu_th_ready.sem, glu_th_ready.at(s))
            V.scalar_tensor_tensor(y_glu, glu_th, 1.0, g_x2, ALU.add, ALU.mult).then_inc(ysum_ready.sem, 1)
            dve.wait_ge(ssq_done.sem, ssq_done.at(s, 2))
            link(V.tensor_scalar(ms[:, 0:1], ssq, 1.0 / (16 * SSM_W), EPS, ALU.mult, ALU.add))
            rsqrt(rstd, ms, 1)
            link(V.tensor_scalar(hy[:, 0:SSM_W], y_glu, rstd[:, 0:1], 0.25, ALU.mult, ALU.mult))
            yield

            def masked(m, ps, mask, scale):
                V.tensor_tensor_reduce(out=probs[:, 256 * (m if m < 6 else m - 6):][:, 0:256], in0=ps, in1=mask, scale=-scale,
                                       scalar=3.0e38, op0=ALU.add, op1=ALU.min,
                                       accum_out=nmax[:, m:m + 1]).then_inc(masked_ready.sem, 1)

            for m in range(6):
                if m in (0, 4):
                    apart(dve, scores_done.sem, scores_done.at(s, 2 if m == 0 else 3))
                o, half = dil_scores(m)
                masked(m, o[:, half:half + 256], row("mask_dil"), DIL_SCALE)
            yield
            dve.wait_ge(exp_ready.sem, exp_ready.at(s, 6))
            link(V.reciprocal(rden[:, 0:6], den[:, 0:6]))
            dve.wait_ge(o_done.sem, o_done.at(s, 1))
            y_dil = hy[:, SSM_W:SSM_W + DIL_W]
            V.tensor_tensor(y_dil.rearrange("p (h d) -> p h d", h=DIL_HEADS),
                            bank[0][:, 0:DIL_W].rearrange("p (h d) -> p h d", h=DIL_HEADS),
                            rden[:, 0:6].unsqueeze(2).broadcast_to([P, DIL_HEADS, HD]), ALU.mult).then_inc(ysum_ready.sem, 1)
            dve.wait_ge(ssq_done.sem, ssq_done.at(s, 3))
            link(V.tensor_scalar(ms[:, 0:1], ssq, 1.0 / DIL_W, EPS, ALU.mult, ALU.add))
            rsqrt(rstd, ms, 1)
            link(V.tensor_scalar(y_dil, y_dil, rstd[:, 0:1], None, ALU.mult))
            yield
            apart(dve, scores_done.sem, scores_done.at(s, 7))
            for h in range(DIFF_HEADS):
                for m in range(2):
                    o, half = diff_scores(h, m)
                    masked(6 + 2 * h + m, o[:, half:half + 256], row("mask_diff"), DIFF_SCALE)
            dve.wait_ge(exp_ready.sem, exp_ready.at(s, 7))
            link(V.tensor_tensor(lam, lexp[:, 0:1], lexp[:, 1:2], ALU.subtract))
            link(V.tensor_tensor(lam, lam, row("lambda_init"), ALU.add))
            yield
            for h in range(DIFF_HEADS):
                a = 6 + 2 * h
                dve.wait_ge(exp_ready.sem, exp_ready.at(s, a + 2))
                link(V.reciprocal(rden[:, a:a + 2], den[:, a:a + 2]))
                link(V.tensor_tensor(rden[:, a + 1:a + 2], rden[:, a + 1:a + 2], lam, ALU.mult))
                m1, m2 = probs[:, 512 * h:512 * h + 256], probs[:, 512 * h + 256:512 * (h + 1)]
                link(V.tensor_scalar(m2, m2, rden[:, a + 1:a + 2], None, ALU.mult))
                V.scalar_tensor_tensor(m1, m1, rden[:, a:a + 1], m2, ALU.mult, ALU.subtract).then_inc(attn_ready.sem, 1)
            dve.wait_ge(o_done.sem, o_done.at(s, 2))
            y_diff = hy[:, SSM_W + DIL_W:D]
            yd3 = y_diff.rearrange("p (h d) -> p h d", h=DIFF_HEADS)
            link(V.tensor_copy(y_diff, bank[5][:, 0:DIFF_W]))
            link(V.tensor_tensor(o_sq, y_diff, y_diff, ALU.mult))
            link(V.tensor_reduce(ssq4, o_sq.rearrange("p (h d) -> p h d", h=DIFF_HEADS), AX_X, ALU.add))
            link(V.tensor_scalar(ms, ssq4, 1.0 / HD, EPS, ALU.mult, ALU.add))
            rsqrt(rstd, ms, 4)
            link(V.tensor_scalar(rstd, rstd, row("one_less_init"), None, ALU.mult))
            V.tensor_tensor(yd3, yd3, rstd.unsqueeze(2).broadcast_to([P, DIFF_HEADS, HD]), ALU.mult).then_inc(y_ready.sem, 1)
            yield

            turned_gain(bank[0:2], y_turned, row("gy"), yT_ready)
            xs = x[:, chunk_cols(s, D)]
            for n in range(2):
                dve.wait_ge(mixed_done.sem, mixed_done.at(s, n + 1))
                ins = V.tensor_tensor(xs[:, 512 * n:512 * (n + 1)], xs[:, 512 * n:512 * (n + 1)], bank[2 + n][:, :], ALU.add)
                if n == 0:
                    step(ins)
            ins.then_inc(x_mid.sem, 1)
            yield

            dve.wait_ge(ssq_done.sem, ssq_done.at(s, 4))
            link(V.tensor_scalar(ms[:, 0:1], ssq, 1.0 / D, EPS, ALU.mult, ALU.add))
            rsqrt(rstd, ms, 1)
            V.scalar_tensor_tensor(h2[:, :], xs, rstd[:, 0:1], row("g2"), ALU.mult, ALU.mult).then_inc(h2_ready.sem, 1)
            yield
            yield
            yield
            yield
            yield

            def top16(count, width, src, rest, vals, where):
                def part(a, i, w=width):
                    return a[:, w * i:w * (i + 1)]

                for i in range(count):
                    step(V.max(vals[:, TOPK * i:TOPK * i + 8], part(src, i)))
                apart(dve, vec.sem, vec.at(s, steps[0]))
                for i in range(count):
                    step(V.match_replace(part(rest, i), vals[:, TOPK * i:TOPK * i + 8], part(src, i), -3.0e38))
                    step(V.max_index(where[:, TOPK * i:TOPK * i + 8], vals[:, TOPK * i:TOPK * i + 8], part(src, i)))
                apart(dve, vec.sem, vec.at(s, steps[0]))
                for i in range(count):
                    step(V.max(vals[:, TOPK * i + 8:TOPK * i + 16], part(rest, i)))
                apart(dve, vec.sem, vec.at(s, steps[0]))
                for i in range(count):
                    step(V.max_index(where[:, TOPK * i + 8:TOPK * i + 16], vals[:, TOPK * i + 8:TOPK * i + 16], part(rest, i)))

            apart(dve, key_scores_kept.sem, key_scores_kept.at(s, 4))
            top16(HC, KEYS, wide_a, wide_b, top_s, top_i)
            settle()
            yield
            ts4 = top_s[:, :].rearrange("p (h c k) -> p h c k", h=HEADS, c=2)
            link(V.tensor_tensor(wide_a.rearrange("p (h i j) -> p h i j", h=HEADS, i=TOPK),
                                 ts4[:, :, 0, :].unsqueeze(3).broadcast_to([P, HEADS, TOPK, TOPK]),
                                 ts4[:, :, 1, :].unsqueeze(2).broadcast_to([P, HEADS, TOPK, TOPK]), ALU.add))
            step(V.tensor_copy(top_f[:, :], top_i[:, :]))
            apart(dve, vec.sem, vec.at(s, steps[0]))
            top16(HEADS, TOPK * TOPK, wide_a, wide_b, best_s, best_j)
            settle()
            yield
            b3 = best_s[:, :].rearrange("p (h k) -> p h k", h=HEADS)
            g3 = gate[:, chunk_cols(s, SLOTS)].rearrange("p (h k) -> p h k", h=HEADS)
            V.tensor_tensor(g3, b3, b3[:, :, 0:1].broadcast_to([P, HEADS, TOPK]), ALU.subtract).then_inc(gate_in.sem, 1)
            tf4 = top_f[:, :].rearrange("p (h c k) -> p h c k", h=HEADS, c=2)
            jf3 = jf[:, :].rearrange("p (h k) -> p h k", h=HEADS)
            for c, e in ((0, e_row), (1, e_col)):
                if c == 0:
                    link(V.tensor_scalar(jpart[:, :], best_j[:, :], 4, None, ALU.logical_shift_right))
                else:
                    link(V.tensor_scalar(jpart[:, :], best_j[:, :], TOPK - 1, None, ALU.bitwise_and))
                link(V.tensor_copy(jf[:, :], jpart[:, :]))
                hit = wide_b.rearrange("p (n i) -> p n i", i=TOPK)
                link(V.tensor_tensor(hit, iota16.unsqueeze(1).broadcast_to([P, SLOTS, TOPK]),
                                     jf[:, :].unsqueeze(2).broadcast_to([P, SLOTS, TOPK]), ALU.is_equal))
                hit4 = wide_b.rearrange("p (h k i) -> p h k i", h=HEADS, k=TOPK)
                link(V.tensor_tensor(hit4, hit4, tf4[:, :, c, :].unsqueeze(2).broadcast_to([P, HEADS, TOPK, TOPK]), ALU.mult))
                link(V.tensor_reduce(e[:, :], hit, AX_X, ALU.add))
            link(V.scalar_tensor_tensor(e_row[:, :], e_row[:, :], float(KEYS), e_col[:, :], ALU.mult, ALU.add))
            link(V.tensor_scalar(idx[:, chunk_cols(s, SLOTS)], e_row[:, :], row("first_expert"), None, ALU.add))
            apart(dve, gate_exp.sem, gate_exp.at(s))
            link(V.tensor_reduce(gsum, g3, AX_X, ALU.add))
            link(V.reciprocal(grec, gsum))
            link(V.tensor_scalar(grec, grec, 0.5, None, ALU.mult))
            V.tensor_tensor(g3, g3, grec.unsqueeze(2).broadcast_to([P, HEADS, TOPK]), ALU.mult).then_inc(mixer_done.sem, 1)
            assert steps[0] == VEC_STEPS, steps[0]
            yield

        def experts_dve_start(dve, p):
            dve.wait_ge(mixer_done.sem, mixer_done.at(p))
            nc.vector.tensor_copy(h2_cur[:, :], h2[:, :]).then_inc(handed.sem, 1)
            apart(dve, handed.sem, handed.at(p))

        def experts_dve(dve, p, i):
            V = nc.vector
            dots, inner, th = peer[:, 0:RING], peer[:, RING:RING + HALF], peer[:, RING + HALF:2 * RING]
            weight = peer[:, 2 * RING:3 * RING]
            act_x = peer[:, 3 * RING:3 * RING + HALF]
            for q in range(2):
                for r in range(HALF * q, HALF * (q + 1)):
                    g = gathered[r]
                    dve.wait_ge(g.sem, (p * ITERS + i + 1) * 16)
                    V.tensor_tensor_reduce(out=u_of[r], in0=u_of[r], in1=h2_cur[:, :], scale=1.0, scalar=0.0,
                                           op0=ALU.mult, op1=ALU.add, accum_out=dots[:, r:r + 1]).then_inc(dots_done.sem, 1)
                d = dots[:, HALF * q:HALF * (q + 1)]
                m = i * 6 + 3 * q
                dve.wait_ge(dots_done.sem, dots_done.at(p, 0) + (i * RING + HALF * (q + 1)))
                V.tensor_tensor(inner, d, d, ALU.mult).then_inc(gelu_step.sem, 1)
                dve.wait_ge(gelu_step.sem, gelu_step.at(p, 0) + (m + 1))
                V.tensor_scalar(inner, inner, GELU_B, GELU_A, ALU.mult, ALU.add).then_inc(gelu_step.sem, 1)
                dve.wait_ge(gelu_step.sem, gelu_step.at(p, 0) + (m + 2))
                V.tensor_tensor(inner, inner, d, ALU.mult).then_inc(inner_ready.sem, 1)
                dve.wait_ge(tanh_ready.sem, tanh_ready.at(p, 0) + (i * 2 + (q + 1)))
                V.scalar_tensor_tensor(act_x, th, 1.0, d, ALU.add, ALU.mult).then_inc(gelu_step.sem, 1)
                dve.wait_ge(gelu_step.sem, gelu_step.at(p, 0) + (m + 3))
                V.tensor_tensor(weight[:, HALF * q:HALF * (q + 1)], act_x, gate[:, slot_cols(p, i, q)],
                                ALU.mult).then_inc(weight_ready.sem, 1)

        def experts_dve_end(dve, p):
            dve.wait_ge(slot_free.sem, slot_free.at(p, SLOTS))
            xs = x[:, chunk_cols(p, D)]
            nc.vector.tensor_copy(xs[:, 0:512], acc[:, 0, :]).then_inc(copied.sem, 1)
            nc.vector.tensor_copy(xs[:, 512:D], acc[:, 1, :]).then_inc(x_ready.sem, 1)

        def experts_pool_start(pool, p):
            apart(pool, mixer_done.sem, mixer_done.at(p))

        def experts_pool(pool, p, i):
            for q in range(2):
                apart(pool, slot_free.sem, p * SLOTS + i * RING + HALF * (q + 1))
                nc.gpsimd.tensor_copy(idx_stage[:, HALF * q:HALF * (q + 1)],
                                      idx[:, slot_cols(p, i, q)]).then_inc(staged.sem, 1)
                apart(pool, staged.sem, staged.at(p, 0) + (i * 2 + (q + 1)))
                for r in range(HALF * q, HALF * (q + 1)):
                    nc.gpsimd.indirect_dma_start(ring[:, 2 * D * r:2 * D * (r + 1)], None, uv,
                                                 bass.IndirectOffsetOnAxis(idx_stage[:, r:r + 1], 0)).then_inc(gathered[r].sem, 16)

        def run(mixer):
            for _ in mixer:
                pass

        def run_over_experts(mixer, experts, eng, s):
            i = 0
            for part, _ in enumerate(mixer):
                for _ in range(AFTER_PART[part]):
                    experts(eng, s - 1, i)
                    i += 1
            assert i == ITERS and part == len(AFTER_PART) - 1

        @block.gpsimd
        def _(pool):
            nc.gpsimd.iota(iota16.bitcast(I32), pattern=[[1, TOPK]], base=0, channel_multiplier=0).then_inc(iota_ready, 1)
            with pool.Fori(0, STAGES) as p:
                experts_pool_start(pool, p)
                with pool.Fori(0, ITERS) as i:
                    experts_pool(pool, p, i)

        @block.scalar
        def _(act):
            act.wait_ge(consts_in, 32)
            run(mixer_act(act, 0))
            with act.Fori(1, STAGES) as s:
                run_over_experts(mixer_act(act, s), experts_act, act, s)
            with act.Fori(0, ITERS) as i:
                experts_act(act, STAGES - 1, i)
            for c in range(CHUNKS):
                act.wait_ge(x_ready.sem, x_ready.at(STAGES - 2 + c, 1))
                if c:
                    act.wait_ge(fin_vec, 1)
                nc.scalar.activation(hy[:, :], x[:, D * c:D * (c + 1)], ACT.Square, accum_out=ssq).then_inc(fin_ssq, 1)

        @block.tensor
        def _(pe):
            pe.sem_inc(w_free.sem, W_SLOTS)
            pe.sem_inc(slot_free.sem, RING)
            pe.wait_ge(mem_ready, 2)
            run(mixer_pe(pe, 0))
            with pe.Fori(1, STAGES) as s:
                experts_pe_start(pe, s - 1)
                run_over_experts(mixer_pe(pe, s), experts_pe, pe, s)
            experts_pe_start(pe, STAGES - 1)
            with pe.Fori(0, ITERS) as i:
                experts_pe(pe, STAGES - 1, i)

        @block.vector
        def _(dve):
            V = nc.vector
            dve.sem_inc(x_ready.sem, 2)
            for k, t in enumerate((kT, fkT, dv, fv, carry)):
                V.memset(t[:, :], 0.0).then_inc(copied.sem, 1)
            dve.wait_ge(copied.sem, 5)
            dve.sem_inc(mem_ready, 1)
            dve.wait_ge(consts_in, 32)
            dve.wait_ge(iota_ready, 1)
            V.tensor_copy(iota16, iota16.bitcast(I32)).then_inc(mem_ready, 1)
            run(mixer_dve(dve, 0))
            with dve.Fori(1, STAGES) as s:
                experts_dve_start(dve, s - 1)
                run_over_experts(mixer_dve(dve, s), experts_dve, dve, s)
                experts_dve_end(dve, s - 1)
            experts_dve_start(dve, STAGES - 1)
            with dve.Fori(0, ITERS) as i:
                experts_dve(dve, STAGES - 1, i)
            experts_dve_end(dve, STAGES - 1)

            n_own = [0]

            def own(ins):
                n_own[0] += 1
                ins.then_inc(mem_ready, 1)
                dve.wait_ge(mem_ready, 2 + n_own[0])

            dve.wait_ge(fin_rows, 16)
            for c in range(CHUNKS):
                dve.wait_ge(fin_ssq, c + 1)
                y, m, t = rstd[:, 0:1], ms[:, 0:1], nt[:, 0:1]
                ti = ti_a[:, 0:1].bitcast(I32)
                own(V.tensor_scalar(m, ssq, 1.0 / D, EPS, ALU.mult, ALU.add))
                own(V.tensor_scalar(ti, m.bitcast(I32), 1, None, ALU.logical_shift_right))
                own(V.tensor_scalar(y.bitcast(I32), ti, -1.0, RSQRT_SEED, ALU.mult, ALU.add))
                for _ in range(3):
                    own(V.tensor_tensor(t, y, y, ALU.mult))
                    own(V.tensor_tensor(t, t, m, ALU.mult))
                    own(V.tensor_scalar(t, t, -0.5, 1.5, ALU.mult, ALU.add))
                    own(V.tensor_tensor(y, y, t, ALU.mult))
                V.scalar_tensor_tensor(work[:, D * c:D * (c + 1)], x[:, D * c:D * (c + 1)], y, rows[:, 0:D],
                                       ALU.mult, ALU.mult).then_inc(fin_vec, 1)


def kernel(**inputs):
    import numpy as np
    import concourse.bacc as bacc
    from concourse import mybir as _mybir
    from concourse.bass_utils import run_bass_kernel_spmd

    a = {k: np.asarray(v) for k, v in inputs.items()}
    f32 = np.float32

    def cols(w, width):
        n = w.shape[1] // width
        return w.reshape(KT, P, n, width).transpose(2, 1, 0, 3).reshape(n, P, KT * width)

    wts = np.zeros((L, BLOCKS, P, WB), f32)
    rows = np.zeros((STAGES, P, ROWS_W), f32)
    for l in range(L):
        wts[l, B_IN:B_IN + 9] = cols(a["w_in"][l], 256)
        glu = a["ssm_w_glu"][l].reshape(SSM_T, P, SSM_W).transpose(1, 0, 2).reshape(P, -1)
        wts[l, B_SSM, :, 0:1152] = glu
        for n, name in ((1152, "ssm_b_re"), (1536, "ssm_b_im")):
            b = a[name][l]
            for g in range(GROUPS):
                t, ch = g // 2, (g % 8) * GROUP_CH
                at = n + P * (g // 8) + STATE * (g % 2)
                wts[l, B_SSM, ch:ch + GROUP_CH, at:at + STATE] = b[g].T
        wts[l, B_OUT:B_OUT + 4] = cols(a["w_out"][l], 256)
        wts[l, B_QUERY:B_QUERY + 8] = cols(a["peer_w_query"][l], 256)
        wts[l, B_KEYS] = a["peer_sub_keys"][l].reshape(HC, KEYS, P).transpose(2, 0, 1).reshape(P, -1)

    q = np.arange(P)[:, None]
    k = np.arange(2 * P)[None, :]
    for s in range(STAGES):
        l, c = s // 2, s % 2
        r = rows[s]

        def put(name, value):
            at, n = ROW_AT[name]
            r[:, at:at + n] = value

        put("g2", a["norm2_g"][l])
        back = P * c + q - k
        held = sum(((back >= 0) & (back <= w) & (back % d == 0)).astype(f32) for w, d in ((128, 1), (512, 4), (2048, 16)))
        put("mask_dil", np.where(held > 0, np.log(np.maximum(held, 1)) / DIL_SCALE, -1e30))
        put("mask_diff", np.where(back >= 0, 0.0, -1e30))
        for name, field in (("ssm_c_re", "c_re"), ("ssm_c_im", "c_im")):
            at, _ = ROW_AT[field]
            cm = a[name][l]
            for g in range(GROUPS):
                p0, o = STATE * (g % 2), at + 32 * (g // 2) + GROUP_CH * (g % 2)
                r[p0:p0 + STATE, o:o + GROUP_CH] = cm[g].T
        put("quarter", (np.arange(P)[:, None] // 32 == np.arange(SQ)[None, :]).astype(f32))
        put("d_skip", a["ssm_d"][l].reshape(SSM_T, P).T)
        put("g1", a["norm1_g"][l].reshape(KT, P).T)
        gy = np.concatenate([a["ssm_norm_g"][l], a["dil_norm_g"][l]] + [a["diff_subln_g"][l]] * DIFF_HEADS)
        put("gy", gy.reshape(KT, P).T)
        put("lam_re", a["ssm_lam_re"][l].reshape(ST, P).T)
        put("lam_im", a["ssm_lam_im"][l].reshape(ST, P).T)
        put("log_step", np.repeat(a["ssm_log_step"][l], STATE).reshape(ST, P).T)
        for name in ("lam_q1", "lam_k1", "lam_q2", "lam_k2"):
            put(name, a[f"diff_{name}"][l])
        init = 0.8 - 0.6 * np.exp(-0.3 * l)
        put("lambda_init", init)
        put("one_less_init", 1.0 - init)
        put("first_expert", float(EXPERTS * l))
    uv = np.concatenate([a["peer_u"], a["peer_v"]], axis=2).reshape(L * EXPERTS, 2 * D)
    arrays = {
        "x_dram": np.ascontiguousarray(a["x"]), "wts_dram": wts.reshape(L * BLOCKS, P, WB), "rows_dram": rows,
        "uv_dram": uv, "ident_dram": np.eye(P, dtype=f32),
        "final_g_dram": np.ascontiguousarray(np.broadcast_to(a["final_norm_g"], (P, D))),
    }
    nc = bacc.Bacc("TRN2", target_bir_lowering=False, num_devices=1)
    args = [nc.dram_tensor(n, t.shape, _mybir.dt.float32, kind="ExternalInput").ap() for n, t in arrays.items()]
    out = nc.dram_tensor("out_dram", a["x"].shape, _mybir.dt.float32, kind="ExternalOutput").ap()
    trunk(nc, *args, out)
    r = run_bass_kernel_spmd(nc, [arrays], core_ids=[0])
    return r.results[0]["out_dram"]
```

```python
from contextlib import ExitStack

import concourse.bass as bass
from concourse import mybir

ALU = mybir.AluOpType
ACT = mybir.ActivationFunctionType
AX_X = mybir.AxisListType.X
F32 = mybir.dt.float32
I32 = mybir.dt.int32
U32 = mybir.dt.uint32

P = 128
D = 1024
KT = D // P
L = 2
CHUNKS = 2
STAGES = L * CHUNKS
EPS = 1e-6
PI = 3.14159265358979

SSM_W, DIL_W, DIFF_W = 384, 384, 256
SSM_T = SSM_W // P
GROUPS, GROUP_CH, STATE = 24, 16, 64
ST = GROUPS * STATE // P
SQ = 4
DIL_HEADS, DIFF_HEADS, HD, DQK = 6, 4, 64, 32
HEADS, TOPK, KEYS = 8, 16, 128
HC = 2 * HEADS
SLOTS = HEADS * TOPK
EXPERTS = KEYS * KEYS

RING = 8
HALF = RING // 2
ITERS = SLOTS // RING

WB = 2048
W_SLOTS = 4
B_IN, B_SSM, B_OUT, B_QUERY, B_KEYS = 0, 9, 10, 14, 22
BLOCKS = 23
W_PER_SLOT = [len(range(j, BLOCKS, W_SLOTS)) for j in range(W_SLOTS)]

ROW_FIELDS = [("g2", D), ("mask_dil", 2 * P), ("mask_diff", 2 * P), ("c_re", ST * 32), ("c_im", ST * 32),
              ("d_skip", SSM_T), ("quarter", SQ), ("g1", KT), ("gy", KT), ("lam_re", ST), ("lam_im", ST), ("log_step", ST),
              ("lam_q1", DQK), ("lam_k1", DQK), ("lam_q2", DQK), ("lam_k2", DQK),
              ("lambda_init", 1), ("one_less_init", 1), ("first_expert", 1)]
ROW_AT, _at = {}, 0
for _name, _n in ROW_FIELDS:
    ROW_AT[_name] = (_at, _n)
    _at += _n
ROWS_W = _at

GELU_A = 0.7978845608028654
GELU_B = GELU_A * 0.044715
DIL_SCALE = HD ** -0.5
DIFF_SCALE = DQK ** -0.5
ROUND = 1.5 * 2.0 ** 23
RSQRT_SEED = float(0x5F3759DF)

VEC_STEPS = 392

def trunk(nc, x_in, wts, rows_in_dram, uv, ident_in, final_g, out):
    with ExitStack() as ctx:
        def sb(name, width, dt=F32):
            return ctx.enter_context(nc.sbuf_tensor(name, [P, width], dt))

        def sem(name):
            return ctx.enter_context(nc.semaphore(name))

        ring = sb("ring", RING * 2 * D)
        wring = sb("wring", W_SLOTS * WB)
        x = sb("x", CHUNKS * D)
        hy = sb("hy", D)
        h2 = sb("h2", D)
        h2_cur = sb("h2_cur", D)
        hT = sb("hT", KT * P)
        uqT = sb("uqT", 6 * P)
        fqT = sb("fqT", 2 * P)
        kT = sb("kT", 3 * 2 * P)
        fkT = sb("fkT", 2 * 2 * P)
        dv = sb("dv", 2 * DIL_W)
        fv = sb("fv", 2 * DIFF_W)
        rows = sb("rows", ROWS_W)
        cos = sb("cos", ST * P)
        sin = sb("sin", ST * P)
        crot = sb("crot", 3 * ST * 32)
        ddiag = sb("ddiag", SSM_W)
        work = sb("work", 7680)
        ident = sb("ident", P)
        diag = sb("diag", RING * P)
        carry = sb("carry", (STAGES + 1) * 2 * ST)
        small = sb("small", 640)
        gate = sb("gate", 2 * SLOTS)
        idx = sb("idx", 2 * SLOTS, I32)
        idx_stage = sb("idx_stage", RING, I32)
        peer = sb("peer", 4 * RING)

        def row(name):
            a, n = ROW_AT[name]
            return rows[:, a:a + n]

        taken = [0]

        def tiny(n, dt=F32):
            a = small[:, taken[0]:taken[0] + n]
            taken[0] += n
            assert taken[0] <= 640
            return a

        v_re, v_im, z_re, z_im = (work[:, 512 * i:512 * i + 512] for i in range(4))
        p_cr, p_si, p_sr, p_ci = (work[:, 2048 + 512 * i:2560 + 512 * i] for i in range(4))
        dbl = [work[:, 2048 + 768 * i:2048 + 768 * i + 768] for i in range(2)]
        y_sq, y_in, y_th, g_x2, g_T, glu_th, y_glu = (work[:, 384 * i:384 * i + 384] for i in range(7))
        u_spread = work[:, 4096:5632]
        probs = work[:, 4096:6144]
        pT = work[:, 6144:7680]
        wide_a, wide_b, wide_c = (work[:, 2048 * i:2048 * i + 2048] for i in range(3))
        squares = work[:, 2688:3072]
        o_sq = work[:, 7424:7680]

        wslot = [wring[:, WB * j:WB * (j + 1)] for j in range(W_SLOTS)]
        u_of = [ring[:, 2 * D * r:2 * D * r + D] for r in range(RING)]
        v_of = [ring[:, 2 * D * r + D:2 * D * (r + 1)] for r in range(RING)]
        w_as = lambda b, k, n: wslot[b % W_SLOTS].rearrange("p (k n) -> p k n", k=k)[:, :, 0:n]
        ssm_w = wslot[B_SSM % W_SLOTS]
        w_glu = ssm_w[:, 0:SSM_T * SSM_W].rearrange("p (k n) -> p k n", k=SSM_T)
        b_re = ssm_w[:, 1152:1536].rearrange("p (k n) -> p k n", k=3)
        b_im = ssm_w[:, 1536:1920].rearrange("p (k n) -> p k n", k=3)

        ssq, ms, rstd, nt = tiny(1), tiny(4), tiny(4), tiny(4)
        ti_a = tiny(4)
        step_t, theta, rad, turn_n = (tiny(ST) for _ in range(4))
        cos1, sin1, f_re, f_im, ta, tb = (tiny(ST) for _ in range(6))
        lam = tiny(1)
        lsum = tiny(2)
        lexp = tiny(2)
        nmax = tiny(14)
        den = tiny(14)
        rden = tiny(14)
        ssq4 = tiny(4)
        lprod = tiny(DQK)
        gsum, grec = tiny(HEADS), tiny(HEADS)
        iota16 = tiny(TOPK)

        top_s = sb("top_s", HC * TOPK)
        top_i = sb("top_i", HC * TOPK, U32)
        top_f = sb("top_f", HC * TOPK)
        best_s = sb("best_s", SLOTS)
        best_j = sb("best_j", SLOTS, U32)
        jpart = sb("jpart", SLOTS, U32)
        jf = sb("jf", SLOTS)
        e_row = sb("e_row", SLOTS)
        e_col = sb("e_col", SLOTS)

        acc = ctx.enter_context(nc.psum_tensor("acc", [P, 2, 512], F32))
        bank = [ctx.enter_context(nc.psum_tensor(f"bank{i}", [P, 512], F32)) for i in range(6)]

        class Signal:

            def __init__(self, name, per_stage=1, before=0):
                self.sem, self.n, self.before = sem(name), per_stage, before

            def at(self, s, k=1):
                return s * self.n + (self.before + k)

        consts_in = sem("consts_in")
        rows_in = sem("rows_in")
        w_in = [sem(f"w_in{j}") for j in range(W_SLOTS)]
        w_free = Signal("w_free", BLOCKS, W_SLOTS)
        x_ready = Signal("x_ready", 1, 2)
        mixer_done = Signal("mixer_done")
        picked = Signal("picked", 2)
        mem_ready = sem("mem_ready")
        iota_ready = sem("iota_ready")
        sep = sem("sep")

        ssq_done = Signal("ssq_done", 4)
        rstd_ready = Signal("rstd_ready")
        hn_ready = Signal("hn_ready")
        hn_turned = Signal("hn_turned", 2)
        hT_ready = Signal("hT_ready", 2)
        proj_done = Signal("proj_done", 5)
        proj_kept = Signal("proj_kept", 8)
        par_exp = Signal("par_exp", 3)
        par_vec = Signal("par_vec", 2)
        spread_ready = Signal("spread_ready", 3)
        tables_ready = Signal("tables_ready")
        bu_done = Signal("bu_done", 3)
        bu_free = Signal("bu_free", 3)
        prod_ready = Signal("prod_ready", 3)
        y_part = Signal("y_part", 3)
        y_sq_ready = Signal("y_sq_ready")
        y_in_ready = Signal("y_in_ready")
        y_th_ready = Signal("y_th_ready")
        g_ready = Signal("g_ready")
        g_turned = Signal("g_turned")
        gT_ready = Signal("gT_ready")
        glu_done = Signal("glu_done")
        glu_th_ready = Signal("glu_th_ready")
        gated_ready = Signal("gated_ready")
        dil_out = Signal("dil_out")
        scores_done = Signal("scores_done", 8)
        masked_ready = Signal("masked_ready", 14)
        exp_ready = Signal("exp_ready", 14)
        attn_ready = Signal("attn_ready", 4)
        p_turned = Signal("p_turned", 5)
        pT_ready = Signal("pT_ready", 5)
        o_done = Signal("o_done", 2)
        y_ready = Signal("y_ready")
        y_turned = Signal("y_turned", 2)
        yT_ready = Signal("yT_ready", 2)
        mixed_done = Signal("mixed_done", 2)
        x_mid = Signal("x_mid")
        h2_ready = Signal("h2_ready")
        h2_turned = Signal("h2_turned", 2)
        h2T_ready = Signal("h2T_ready", 2)
        q_done = Signal("q_done", 4)
        q_kept = Signal("q_kept", 4)
        key_scores_done = Signal("key_scores_done", 4)
        key_scores_kept = Signal("key_scores_kept", 4)
        gate_in = Signal("gate_in")
        gate_exp = Signal("gate_exp")
        vec = Signal("vec_step", VEC_STEPS)

        handed = Signal("handed")
        staged = Signal("staged", 2 * ITERS)
        gathered = [Signal(f"gathered{r}", ITERS) for r in range(RING)]
        dots_done = Signal("dots_done", SLOTS)
        gelu_step = Signal("gelu_step", 3 * 2 * ITERS)
        inner_ready = Signal("inner_ready", 2 * ITERS)
        tanh_ready = Signal("tanh_ready", 2 * ITERS)
        weight_ready = Signal("weight_ready", 2 * ITERS)
        diag_ready = Signal("diag_ready", SLOTS)
        slot_free = Signal("slot_free", SLOTS, RING)
        copied = Signal("copied", 1)
        fin_ssq, fin_vec, fin_rows = sem("fin_ssq"), sem("fin_vec"), sem("fin_rows")
        stored = sem("stored")

        def chunk_cols(s, width):
            return bass.ds((s & 1) * width, width)

        def slot_cols(p, i, q):
            return bass.ds((p & 1) * SLOTS + i * RING + HALF * q, HALF)

        def apart(eng, sem_, value):
            eng.wait_ge(sem_, value)
            eng.sem_inc(sep, 1)

        block = ctx.enter_context(nc.Block())

        def load_stage(sp, s):
            if not (type(s) is int and s == 0):
                sp.wait_ge(mixer_done.sem, mixer_done.at(s, 0))
            sp.dma_start(rows[:, :], rows_in_dram[bass.ds(s, 1)].rearrange("a p n -> (a p) n")).then_inc(rows_in, 16)
            for b in range(BLOCKS):
                j = b % W_SLOTS
                sp.wait_ge(w_free.sem, s * BLOCKS + b + (2 if b < BLOCKS % W_SLOTS else 1))
                src = wts[bass.ds((s // 2) * BLOCKS + b, 1)].rearrange("a p n -> (a p) n")
                sp.dma_start(wslot[j], src).then_inc(w_in[j], 16)

        @block.sync
        def _(sp):
            sp.dma_start(x[:, :].rearrange("p (c d) -> p c d", c=CHUNKS),
                         x_in.rearrange("a (c p) d -> p (a c) d", p=P)).then_inc(consts_in, 16)
            sp.dma_start(ident[:, :], ident_in).then_inc(consts_in, 16)
            load_stage(sp, 0)
            with sp.Fori(1, STAGES) as s:
                load_stage(sp, s)
            sp.wait_ge(mixer_done.sem, STAGES)
            sp.dma_start(rows[:, 0:D], final_g).then_inc(fin_rows, 16)
            for c in range(CHUNKS):
                sp.wait_ge(fin_vec, c + 1)
                sp.dma_start(out[0, P * c:P * (c + 1), :], work[:, D * c:D * (c + 1)]).then_inc(stored, 16)
            sp.wait_ge(stored, 16 * CHUNKS)

        def block_here(eng, s, b):
            j = b % W_SLOTS
            eng.wait_ge(w_in[j], s * (16 * W_PER_SLOT[j]) + 16 * (b // W_SLOTS + 1))

        def dil_scores(h):
            return (bank[3], bank[4], bank[3], bank[4], bank[5], bank[4])[h], 256 * (h in (2, 3))

        def diff_scores(h, m):
            return (bank[1], bank[2], bank[4], bank[5])[2 * (h % 2) + m], 256 * (h // 2)

        def scored(m):
            if m < 4:
                return h2[:, 256 * m:256 * (m + 1)]
            if m < 6:
                return work[:, 5632 + 256 * (m - 4):5888 + 256 * (m - 4)]
            return probs[:, 256 * (m - 6):256 * (m - 5)]

        def dil_probs(h, kc):
            return scored(h)[:, P * kc:P * (kc + 1)]

        dil_turn = (bank[3], bank[5], bank[4])
        diff_turn = (bank[1], bank[2])
        key_bank = (bank[4], bank[5], bank[0], bank[1])

        def mixer_pe(pe, s):
            mm = nc.tensor.matmul

            def turn(src, banks, done):
                for j in range(2):
                    for k in range(4):
                        t = 4 * j + k
                        last = nc.tensor.transpose(banks[j][:, P * k:P * (k + 1)], src[:, P * t:P * (t + 1)], ident[:, :])
                    last.then_inc(done.sem, 1)

            def project(n, tiles):
                for i in tiles:
                    b = B_IN + i // 2
                    if i % 2 == 0:
                        block_here(pe, s, b)
                    w = w_as(b, KT, 256)[:, :, P * (i % 2):P * (i % 2 + 1)]
                    for k in range(KT):
                        h = hT[:, P * k:P * (k + 1)]
                        lhsT, rhs = (h, w[:, k, :]) if i in (9, 10, 11, 16, 17) else (w[:, k, :], h)
                        last = mm(bank[n][:, P * (i % 4):P * (i % 4 + 1)], lhsT, rhs, start=(k == 0), stop=(k == KT - 1))
                    if i % 2:
                        last.then_inc(w_free.sem, 1)
                pe.wait_ge(w_free.sem, w_free.at(s, b + 1))
                pe.sem_inc(proj_done.sem, 1)

            def state_inputs(g):
                pe.wait_ge(spread_ready.sem, spread_ready.at(s, g + 1))
                for b_w, o in ((b_re, bank[1]), (b_im, bank[2])):
                    last = mm(o[:, :], b_w[:, g, :], u_spread[:, 512 * g:512 * (g + 1)], start=True, stop=True)
                last.then_inc(bu_done.sem, 1)

            y_ps = bank[0]
            cr = crot[:, :].rearrange("p (c j n) -> p c j n", c=3, j=ST)

            def state_outputs(g):
                pe.wait_ge(prod_ready.sem, prod_ready.at(s, g + 1))
                for j in range(SQ):
                    t = SQ * g + j
                    for prod, which in ((p_cr, 0), (p_si, 1), (p_sr, 2), (p_ci, 2)):
                        last = mm(y_ps[:, 32 * t:32 * t + 32], prod[:, P * j:P * (j + 1)], cr[:, which, t, :],
                                  start=False, stop=False, skip_group_check=True)
                last.then_inc(y_part.sem, 1)

            def dil_score(h):
                a, i = HD * (h % 2), h // 2
                o, half = dil_scores(h)
                return mm(o[:, half:half + 256], uqT[a:a + HD, P * (3 + i):P * (4 + i)],
                          kT[a:a + HD, 256 * i:256 * (i + 1)], start=True, stop=True)

            def dil_turned(i):
                for b in range(4):
                    last = nc.tensor.transpose(dil_turn[i][:, P * b:P * (b + 1)], dil_probs(2 * i + b // 2, b % 2),
                                               ident[:, :])
                last.then_inc(p_turned.sem, 1)

            def dil_values(i):
                pe.wait_ge(pT_ready.sem, pT_ready.at(s, i + 1))
                for b in range(2):
                    h = 2 * i + b
                    for kc in range(2):
                        last = mm(bank[3][:, HD * h:HD * (h + 1)], pT[:, 512 * i + P * (2 * b + kc):512 * i + P * (2 * b + kc + 1)],
                                  dv[:, DIL_W * kc + HD * h:DIL_W * kc + HD * (h + 1)],
                                  start=(h == 0 and kc == 0), stop=False, skip_group_check=True)
                return last

            pe.wait_ge(hn_ready.sem, hn_ready.at(s))
            turn(hy, bank[0:2], hn_turned)
            yield 1
            pe.wait_ge(hT_ready.sem, hT_ready.at(s, 2))
            project(0, range(0, 4))
            yield 2
            project(1, range(4, 8))
            yield 3
            project(2, range(8, 12))
            yield 4
            project(3, range(12, 16))
            yield 5
            project(4, range(16, 18))
            block_here(pe, s, B_SSM)
            pe.wait_ge(proj_kept.sem, proj_kept.at(s, 5))
            state_inputs(0)
            yield 6
            pe.wait_ge(proj_kept.sem, proj_kept.at(s, 8))
            for h in range(5):
                last = dil_score(h)
                if h in (1, 3, 4):
                    last.then_inc(scores_done.sem, 1)
            yield 7
            pe.wait_ge(bu_free.sem, bu_free.at(s, 1))
            state_inputs(1)
            pe.wait_ge(tables_ready.sem, tables_ready.at(s))
            for i in range(SSM_T):
                mm(y_ps[:, P * i:P * (i + 1)], uqT[:, P * i:P * (i + 1)], ddiag[:, P * i:P * (i + 1)],
                   start=(i == 0), stop=False, skip_group_check=True)
            state_outputs(0)
            yield 8
            pe.wait_ge(exp_ready.sem, exp_ready.at(s, 5))
            dil_score(5).then_inc(scores_done.sem, 1)
            dil_turned(0)
            dil_turned(1)
            yield 9
            pe.wait_ge(bu_free.sem, bu_free.at(s, 2))
            state_inputs(2)
            state_outputs(1)
            dil_values(0)
            dil_values(1)
            yield 10
            pe.wait_ge(exp_ready.sem, exp_ready.at(s, 6))
            dil_turned(2)
            yield 11
            state_outputs(2)
            dil_values(2).then_inc(o_done.sem, 1)
            yield 12
            pe.wait_ge(bu_free.sem, bu_free.at(s, 3))
            for h in range(DIFF_HEADS):
                for m in range(2):
                    a = HD * (h % 2) + DQK * m
                    o, half = diff_scores(h, m)
                    last = mm(o[:, half:half + 256], fqT[a:a + DQK, P * (h // 2):P * (h // 2 + 1)],
                              fkT[a:a + DQK, 256 * (h // 2):256 * (h // 2 + 1)], start=True, stop=True)
                last.then_inc(scores_done.sem, 1)
            yield 13
            pe.wait_ge(g_ready.sem, g_ready.at(s))
            for i in range(SSM_T):
                last = nc.tensor.transpose(bank[0][:, P * i:P * (i + 1)], g_x2[:, P * i:P * (i + 1)], ident[:, :])
            last.then_inc(g_turned.sem, 1)
            yield 14
            pe.wait_ge(gT_ready.sem, gT_ready.at(s))
            pe.wait_ge(dil_out.sem, dil_out.at(s))
            for i in range(SSM_T):
                last = mm(bank[3][:, 0:SSM_W], g_T[:, P * i:P * (i + 1)], w_glu[:, i, :],
                          start=(i == 0), stop=(i == SSM_T - 1))
            last.then_inc(glu_done.sem, 1)
            pe.wait_ge(glu_done.sem, glu_done.at(s))
            pe.sem_inc(w_free.sem, 1)
            for i, o in enumerate(diff_turn):
                pe.wait_ge(attn_ready.sem, attn_ready.at(s, 2 * i + 2))
                for b in range(2):
                    for kc in range(2):
                        a = 512 * (2 * i + b) + P * kc
                        last = nc.tensor.transpose(o[:, P * (2 * b + kc):P * (2 * b + kc + 1)], probs[:, a:a + P], ident[:, :])
                last.then_inc(p_turned.sem, 1)
            yield 15
            for i in range(2):
                pe.wait_ge(pT_ready.sem, pT_ready.at(s, 4 + i))
                for b in range(2):
                    h = 2 * i + b
                    for kc in range(2):
                        a = 512 * i + P * (2 * b + kc)
                        last = mm(bank[4][:, HD * h:HD * (h + 1)], pT[:, a:a + P],
                                  fv[:, DIFF_W * kc + HD * h:DIFF_W * kc + HD * (h + 1)],
                                  start=(h == 0 and kc == 0), stop=False, skip_group_check=True)
            last.then_inc(o_done.sem, 1)
            yield 16
            pe.wait_ge(y_ready.sem, y_ready.at(s))
            turn(hy, (bank[0], bank[5]), y_turned)
            for half in range(2):
                yield 17 + half
                if half == 0:
                    pe.wait_ge(yT_ready.sem, yT_ready.at(s, 2))
                for n in (2 * half, 2 * half + 1):
                    b = B_OUT + n
                    block_here(pe, s, b)
                    w = w_as(b, KT, 256)
                    for k in range(KT):
                        last = mm(bank[1 + half][:, 256 * (n % 2):256 * (n % 2) + 256], hT[:, P * k:P * (k + 1)], w[:, k, :],
                                  start=(k == 0), stop=(k == KT - 1))
                    last.then_inc(w_free.sem, 1)
                pe.wait_ge(w_free.sem, w_free.at(s, b + 1))
                pe.sem_inc(mixed_done.sem, 1)
            yield 19
            pe.wait_ge(h2_ready.sem, h2_ready.at(s))
            turn(h2, bank[4:6], h2_turned)
            keys = w_as(B_KEYS, HC, P)
            for n in range(7):
                yield 20 + n
                if n == 0:
                    pe.wait_ge(h2T_ready.sem, h2T_ready.at(s, 2))
                if n < 4:
                    for i in range(4 * n, 4 * n + 4):
                        b = B_QUERY + i // 2
                        if i % 2 == 0:
                            block_here(pe, s, b)
                        w = w_as(b, KT, 256)[:, :, P * (i % 2):P * (i % 2 + 1)]
                        for k in range(KT):
                            last = mm(bank[n][:, P * (i % 4):P * (i % 4 + 1)], w[:, k, :], hT[:, P * k:P * (k + 1)],
                                      start=(k == 0), stop=(k == KT - 1))
                        if i % 2:
                            last.then_inc(w_free.sem, 1)
                    pe.wait_ge(w_free.sem, w_free.at(s, b + 1))
                    pe.sem_inc(q_done.sem, 1)
                if n >= 3:
                    g = n - 3
                    if g == 0:
                        block_here(pe, s, B_KEYS)
                    pe.wait_ge(q_kept.sem, q_kept.at(s, g + 1))
                    for i in range(4 * g, 4 * g + 4):
                        last = mm(key_bank[g][:, P * (i % 4):P * (i % 4 + 1)], wide_c[:, P * i:P * (i + 1)], keys[:, i, :],
                                  start=True, stop=True)
                    last.then_inc(key_scores_done.sem, 1)
            pe.wait_ge(key_scores_done.sem, key_scores_done.at(s, 4))
            pe.sem_inc(w_free.sem, 1)

        def experts_pe_start(pe, p):
            pe.wait_ge(handed.sem, handed.at(p))
            apart(pe, x_ready.sem, x_ready.at(p, 0))
            xs = x[:, chunk_cols(p, D)]
            for n in range(2):
                nc.tensor.matmul(acc[:, n, :], ident[:, :], xs[:, 512 * n:512 * (n + 1)],
                                 start=True, stop=False, skip_group_check=True)

        def experts_pe(pe, p, i, q):
            for r in range(HALF * q, HALF * (q + 1)):
                pe.wait_ge(diag_ready.sem, diag_ready.at(p, i * RING + (r + 1)))
                for n in range(2):
                    last = nc.tensor.matmul(acc[:, n, :], diag[:, P * r:P * (r + 1)], v_of[r][:, 512 * n:512 * (n + 1)],
                                            start=False, stop=False, skip_group_check=True)
                last.then_inc(slot_free.sem, 1)

        def mixer_act(act, s):
            A = nc.scalar.activation
            xs = x[:, chunk_cols(s, D)]

            def keep(out_ap, in_ap, sig):
                A(out_ap, in_ap, ACT.Copy).then_inc(sig.sem, 1)

            kT3 = kT[:, :].rearrange("p (t c n) -> p t c n", t=3, c=2)
            fkT3 = fkT[:, :].rearrange("p (t c n) -> p t c n", t=2, c=2)
            one = bass.ds(s & 1, 1)

            def bk(i, a, b):
                return bank[i][:, P * a:P * b]

            def soften(m):
                act.wait_ge(masked_ready.sem, masked_ready.at(s, m + 1))
                pm = scored(m)
                A(pm, pm, ACT.Exp, scale=-1.0, bias=nmax[:, m:m + 1], accum_out=den[:, m:m + 1]).then_inc(exp_ready.sem, 1)

            apart(act, x_ready.sem, x_ready.at(s, -1))
            A(hy[:, :], xs, ACT.Square, accum_out=ssq).then_inc(ssq_done.sem, 1)
            act.wait_ge(rows_in, 16 * s + 16)
            A(step_t, row("log_step"), ACT.Exp).then_inc(par_exp.sem, 1)
            apart(act, rstd_ready.sem, rstd_ready.at(s))
            A(hy[:, :], xs, ACT.Copy, scale=rstd[:, 0:1]).then_inc(hn_ready.sem, 1)
            yield 2
            act.wait_ge(par_vec.sem, par_vec.at(s, 1))
            A(rad, ta, ACT.Exp).then_inc(par_exp.sem, 1)
            A(lexp, lsum, ACT.Exp)
            act.wait_ge(proj_done.sem, proj_done.at(s, 1))
            keep(uqT[:, 0:4 * P], bk(0, 0, 4), proj_kept)
            yield 3
            act.wait_ge(proj_done.sem, proj_done.at(s, 2))
            keep(uqT[:, 4 * P:6 * P], bk(1, 0, 2), proj_kept)
            keep(kT3[:, 0:2, one, :], bk(1, 2, 4).rearrange("p (t c n) -> p t c n", t=2, c=1), proj_kept)
            act.wait_ge(par_vec.sem, par_vec.at(s, 2))
            A(sin1, theta, ACT.Sin)
            A(cos1, tb, ACT.Sin).then_inc(par_exp.sem, 1)
            yield 4
            apart(act, proj_done.sem, proj_done.at(s, 3))
            keep(kT3[:, 2:3, one, :], bk(2, 0, 1).rearrange("p (t c n) -> p t c n", t=1, c=1), proj_kept)
            keep(dv[:, chunk_cols(s, DIL_W)], bk(2, 1, 4), proj_kept)
            yield 5
            act.wait_ge(proj_done.sem, proj_done.at(s, 4))
            keep(fqT[:, :], bk(3, 0, 2), proj_kept)
            keep(fkT3[:, :, one, :], bk(3, 2, 4).rearrange("p (t c n) -> p t c n", t=2, c=1), proj_kept)
            yield 6
            apart(act, proj_done.sem, proj_done.at(s, 5))
            keep(fv[:, chunk_cols(s, DIFF_W)], bk(4, 0, 2), proj_kept)
            yield 7
            for m in range(5):
                soften(m)
            yield 9
            soften(5)
            for i in range(2):
                act.wait_ge(p_turned.sem, p_turned.at(s, i + 1))
                A(pT[:, 512 * i:512 * (i + 1)], dil_turn[i][:, :], ACT.Copy).then_inc(pT_ready.sem, 1)
            yield 11
            act.wait_ge(p_turned.sem, p_turned.at(s, 3))
            A(pT[:, 1024:1536], dil_turn[2][:, :], ACT.Copy).then_inc(pT_ready.sem, 1)
            yield 12
            act.wait_ge(y_part.sem, y_part.at(s, 3))
            A(y_sq, bank[0][:, 0:SSM_W], ACT.Square).then_inc(y_sq_ready.sem, 1)
            act.wait_ge(y_in_ready.sem, y_in_ready.at(s))
            A(y_th, y_in, ACT.Tanh).then_inc(y_th_ready.sem, 1)
            act.wait_ge(dil_out.sem, dil_out.at(s))
            A(squares, hy[:, SSM_W:SSM_W + DIL_W], ACT.Square, accum_out=ssq).then_inc(ssq_done.sem, 1)
            yield 13
            for m in range(6, 14):
                soften(m)
            yield 14
            act.wait_ge(g_turned.sem, g_turned.at(s))
            A(g_T, bank[0][:, 0:SSM_W], ACT.Copy).then_inc(gT_ready.sem, 1)
            yield 15
            act.wait_ge(glu_done.sem, glu_done.at(s))
            A(glu_th, bank[3][:, 0:SSM_W], ACT.Tanh, scale=0.25).then_inc(glu_th_ready.sem, 1)
            for i in range(2):
                act.wait_ge(p_turned.sem, p_turned.at(s, 4 + i))
                A(pT[:, 512 * i:512 * (i + 1)], diff_turn[i][:, :], ACT.Copy).then_inc(pT_ready.sem, 1)
            act.wait_ge(gated_ready.sem, gated_ready.at(s))
            A(y_sq, y_glu, ACT.Square, accum_out=ssq).then_inc(ssq_done.sem, 1)
            yield 19
            apart(act, x_mid.sem, x_mid.at(s))
            A(hy[:, :], xs, ACT.Square, accum_out=ssq).then_inc(ssq_done.sem, 1)
            yield 20
            for j in range(2):
                act.wait_ge(h2_turned.sem, h2_turned.at(s, j + 1))
                A(hT[:, 512 * j:512 * (j + 1)], bank[4 + j][:, :], ACT.Copy).then_inc(h2T_ready.sem, 1)
            for n in range(7):
                yield 21 + n
                if n < 4:
                    act.wait_ge(q_done.sem, q_done.at(s, n + 1))
                    A(wide_c[:, 512 * n:512 * (n + 1)], bank[n][:, :], ACT.Copy).then_inc(q_kept.sem, 1)
                if n >= 3:
                    g = n - 3
                    act.wait_ge(key_scores_done.sem, key_scores_done.at(s, g + 1))
                    A(wide_a[:, 512 * g:512 * (g + 1)], key_bank[g][:, :], ACT.Copy).then_inc(key_scores_kept.sem, 1)
            yield 29
            apart(act, gate_in.sem, gate_in.at(s))
            own_gate = gate[:, chunk_cols(s, SLOTS)]
            A(own_gate, own_gate, ACT.Exp).then_inc(gate_exp.sem, 1)

        def experts_act(act, p, i, q):
            m = i * 2 + (q + 1)
            act.wait_ge(inner_ready.sem, inner_ready.at(p, 0) + m)
            inner = peer[:, RING:RING + HALF]
            nc.scalar.activation(peer[:, RING + HALF:2 * RING], inner, ACT.Tanh).then_inc(tanh_ready.sem, 1)
            act.wait_ge(weight_ready.sem, weight_ready.at(p, 0) + m)
            for r in range(HALF * q, HALF * (q + 1)):
                nc.scalar.activation(diag[:, P * r:P * (r + 1)], ident[:, :], ACT.Copy,
                                     scale=peer[:, 2 * RING + r:2 * RING + r + 1]).then_inc(diag_ready.sem, 1)

        steps = [0]

        def mixer_dve(dve, s):
            V = nc.vector
            steps[0] = 0

            def step(ins):
                steps[0] += 1
                ins.then_inc(vec.sem, 1)

            def settle():
                dve.wait_ge(vec.sem, vec.at(s, steps[0]))

            def link(ins):
                step(ins)
                settle()

            def rsqrt(y, m, n):
                y, m, t = y[:, 0:n], m[:, 0:n], nt[:, 0:n]
                ti = ti_a[:, 0:n].bitcast(I32)
                link(V.tensor_scalar(ti, m.bitcast(I32), 1, None, ALU.logical_shift_right))
                link(V.tensor_scalar(y.bitcast(I32), ti, -1.0, RSQRT_SEED, ALU.mult, ALU.add))
                for _ in range(3):
                    link(V.tensor_tensor(t, y, y, ALU.mult))
                    link(V.tensor_tensor(t, t, m, ALU.mult))
                    link(V.tensor_scalar(t, t, -0.5, 1.5, ALU.mult, ALU.add))
                    link(V.tensor_tensor(y, y, t, ALU.mult))

            def norm_scale(n, src, scale):
                link(V.tensor_scalar(ms[:, 0:n], src, scale, EPS, ALU.mult, ALU.add))
                rsqrt(rstd, ms, n)

            def turned_gain(banks, done, gain, ready):
                for j in range(2):
                    dve.wait_ge(done.sem, done.at(s, j + 1))
                    V.tensor_tensor(hT3[:, 4 * j:4 * j + 4, :], banks[j][:, :].rearrange("p (k n) -> p k n", k=4),
                                    gain[:, 4 * j:4 * j + 4].unsqueeze(2).broadcast_to([P, 4, P]),
                                    ALU.mult).then_inc(ready.sem, 1)

            hT3 = hT[:, :].rearrange("p (k n) -> p k n", k=KT)
            xs = x[:, chunk_cols(s, D)]
            cos3 = cos[:, :].rearrange("p (j t) -> p j t", j=ST)
            sin3 = sin[:, :].rearrange("p (j t) -> p j t", j=ST)
            start = carry[:, bass.ds(s * (2 * ST), 2 * ST)]
            keep_at = carry[:, bass.ds((s // 2) * (4 * ST) + 2 * ST, 2 * ST)]

            def double(n, top):
                while n < top:
                    t1, t2 = (d[:, 0:ST * n].rearrange("p (j t) -> p j t", j=ST) for d in dbl)
                    cn = cos3[:, :, n - 1:n].broadcast_to([P, ST, n])
                    sn = sin3[:, :, n - 1:n].broadcast_to([P, ST, n])
                    step(V.tensor_tensor(t1, cos3[:, :, 0:n], cn, ALU.mult))
                    link(V.tensor_tensor(t2, sin3[:, :, 0:n], sn, ALU.mult))
                    link(V.tensor_tensor(cos3[:, :, n:2 * n], t1, t2, ALU.subtract))
                    step(V.tensor_tensor(t1, cos3[:, :, 0:n], sn, ALU.mult))
                    link(V.tensor_tensor(t2, sin3[:, :, 0:n], cn, ALU.mult))
                    link(V.tensor_tensor(sin3[:, :, n:2 * n], t1, t2, ALU.add))
                    n *= 2

            def spread(g):
                V.tensor_tensor(u_spread[:, 512 * g:512 * (g + 1)].rearrange("p (j t) -> p j t", j=SQ),
                                uqT[:, P * g:P * (g + 1)].unsqueeze(1).broadcast_to([P, SQ, P]),
                                row("quarter").unsqueeze(2).broadcast_to([P, SQ, P]), ALU.mult).then_inc(spread_ready.sem, 1)

            def scan(g):
                dve.wait_ge(bu_done.sem, bu_done.at(s, g + 1))
                cg, sg = cos[:, 512 * g:512 * (g + 1)], sin[:, 512 * g:512 * (g + 1)]
                br, bi = bank[1][:, :], bank[2][:, :]
                if g:
                    dve.wait_ge(y_part.sem, y_part.at(s, g))
                step(V.tensor_tensor(p_cr, br, cg, ALU.mult))
                step(V.tensor_tensor(p_si, bi, sg, ALU.mult))
                step(V.tensor_tensor(p_ci, bi, cg, ALU.mult))
                V.tensor_tensor(p_sr, br, sg, ALU.mult).then_inc(bu_free.sem, 1)
                dve.wait_ge(bu_free.sem, bu_free.at(s, g + 1))
                step(V.tensor_tensor(v_re, p_cr, p_si, ALU.add))
                link(V.tensor_tensor(v_im, p_ci, p_sr, ALU.subtract))
                for j in range(SQ):
                    t = SQ * g + j
                    decay = rad[:, t:t + 1].broadcast_to([P, P])
                    for part, (v, z) in enumerate(((v_re, z_re), (v_im, z_im))):
                        step(V.tensor_tensor_scan(z[:, P * j:P * (j + 1)], decay, v[:, P * j:P * (j + 1)],
                                                  start[:, ST * part + t:ST * part + t + 1], ALU.mult, ALU.add))
                settle()
                step(V.tensor_tensor(p_cr, cg, z_re, ALU.mult))
                step(V.tensor_tensor(p_si, sg, z_im, ALU.mult))
                step(V.tensor_tensor(p_sr, sg, z_re, ALU.mult))
                V.tensor_tensor(p_ci, cg, z_im, ALU.mult).then_inc(prod_ready.sem, 1)
                dve.wait_ge(prod_ready.sem, prod_ready.at(s, g + 1))
                last = lambda a: a.rearrange("p (j t) -> p j t", j=SQ)[:, :, P - 1]
                step(V.tensor_tensor(keep_at[:, SQ * g:SQ * (g + 1)], last(p_cr), last(p_si), ALU.subtract))
                step(V.tensor_tensor(keep_at[:, ST + SQ * g:ST + SQ * (g + 1)], last(p_sr), last(p_ci), ALU.add))
                settle()

            def masked(m, place, mask, scale):
                o, half = place
                V.tensor_tensor_reduce(out=scored(m), in0=o[:, half:half + 256], in1=mask, scale=-scale,
                                       scalar=3.0e38, op0=ALU.add, op1=ALU.min,
                                       accum_out=nmax[:, m:m + 1]).then_inc(masked_ready.sem, 1)

            dve.wait_ge(ssq_done.sem, ssq_done.at(s, 1))
            norm_scale(1, ssq, 1.0 / D)
            V.tensor_copy(rstd[:, 1:2], rstd[:, 0:1]).then_inc(rstd_ready.sem, 1)
            dve.wait_ge(rows_in, 16 * s + 16)
            yield 1
            turned_gain(bank[0:2], hn_turned, row("g1"), hT_ready)
            step(V.tensor_tensor(lprod, row("lam_q1"), row("lam_k1"), ALU.mult))
            settle()
            link(V.tensor_reduce(lsum[:, 0:1], lprod, AX_X, ALU.add))
            link(V.tensor_tensor(lprod, row("lam_q2"), row("lam_k2"), ALU.mult))
            link(V.tensor_reduce(lsum[:, 1:2], lprod, AX_X, ALU.add))
            dve.wait_ge(par_exp.sem, par_exp.at(s, 1))
            step(V.tensor_tensor(theta, row("lam_im"), step_t, ALU.mult))
            V.tensor_tensor(ta, row("lam_re"), step_t, ALU.mult).then_inc(par_vec.sem, 1)
            yield 2
            settle()
            link(V.tensor_scalar(turn_n, theta, 1.0 / (2 * PI), ROUND, ALU.mult, ALU.add))
            link(V.tensor_scalar(turn_n, turn_n, ROUND, None, ALU.subtract))
            for part in (6.28125, 0.001934051513671875, 1.2556659146e-06):
                link(V.scalar_tensor_tensor(theta, turn_n, -part, theta, ALU.mult, ALU.add))
            link(V.tensor_scalar(theta, theta, 3.1415925, -3.1415925, ALU.min, ALU.max))
            link(V.scalar_tensor_tensor(tb, theta, -1.0, theta, ALU.mult, ALU.max))
            V.tensor_scalar(tb, tb, -1.0, PI / 2, ALU.mult, ALU.add).then_inc(par_vec.sem, 1)
            yield 3
            dve.wait_ge(proj_kept.sem, proj_kept.at(s, 1))
            spread(0)
            dve.wait_ge(par_exp.sem, par_exp.at(s, 3))
            step(V.tensor_tensor(f_re, cos1, cos1, ALU.mult))
            link(V.tensor_tensor(f_im, sin1, sin1, ALU.mult))
            link(V.tensor_tensor(f_re, f_re, f_im, ALU.add))
            link(V.tensor_scalar(f_re, f_re, -0.5, 1.5, ALU.mult, ALU.add))
            step(V.tensor_tensor(cos1, cos1, f_re, ALU.mult))
            link(V.tensor_tensor(sin1, sin1, f_re, ALU.mult))
            step(V.tensor_tensor(f_re, rad, cos1, ALU.mult))
            link(V.tensor_tensor(f_im, rad, sin1, ALU.mult))
            link(V.tensor_scalar(f_re, f_re, 1.0, None, ALU.subtract))
            step(V.tensor_tensor(ta, row("lam_re"), row("lam_re"), ALU.mult))
            link(V.tensor_tensor(tb, row("lam_im"), row("lam_im"), ALU.mult))
            link(V.tensor_tensor(ta, ta, tb, ALU.add))
            link(V.reciprocal(turn_n, ta))
            step(V.tensor_tensor(ta, f_re, row("lam_re"), ALU.mult))
            step(V.tensor_tensor(tb, f_im, row("lam_im"), ALU.mult))
            step(V.tensor_tensor(theta, f_im, row("lam_re"), ALU.mult))
            link(V.tensor_tensor(step_t, f_re, row("lam_im"), ALU.mult))
            step(V.tensor_tensor(ta, ta, tb, ALU.add))
            link(V.tensor_tensor(theta, theta, step_t, ALU.subtract))
            step(V.tensor_tensor(f_re, ta, turn_n, ALU.mult))
            link(V.tensor_tensor(f_im, theta, turn_n, ALU.mult))
            yield 4
            spread(1)
            step(V.tensor_copy(cos3[:, :, 0:1], cos1.unsqueeze(2)))
            link(V.tensor_copy(sin3[:, :, 0:1], sin1.unsqueeze(2)))
            double(1, 64)
            yield 5
            double(64, P)
            spread(2)
            yield 6
            scan(0)
            yield 7
            cr = crot[:, :].rearrange("p (c j n) -> p c j n", c=3, j=ST)
            c_re = row("c_re").rearrange("p (j n) -> p j n", j=ST)
            c_im = row("c_im").rearrange("p (j n) -> p j n", j=ST)
            fr = f_re.unsqueeze(2).broadcast_to([P, ST, 32])
            fi = f_im.unsqueeze(2).broadcast_to([P, ST, 32])
            t1, t2 = (d[:, 0:ST * 32].rearrange("p (j t) -> p j t", j=ST) for d in (v_re, v_im))
            step(V.tensor_tensor(t1, c_re, fr, ALU.mult))
            link(V.tensor_tensor(t2, c_im, fi, ALU.mult))
            step(V.tensor_tensor(cr[:, 0], t1, t2, ALU.subtract))
            link(V.tensor_tensor(cr[:, 1], t2, t1, ALU.subtract))
            step(V.tensor_tensor(t1, c_re, fi, ALU.mult))
            link(V.tensor_tensor(t2, c_im, fr, ALU.mult))
            link(V.tensor_tensor(t1, t1, t2, ALU.add))
            step(V.tensor_scalar(cr[:, 2], t1, -1.0, None, ALU.mult))
            for i in range(SSM_T):
                ins = V.tensor_scalar(ddiag[:, P * i:P * (i + 1)], ident[:, :], row("d_skip")[:, i:i + 1], None, ALU.mult)
                if i < SSM_T - 1:
                    step(ins)
            ins.then_inc(tables_ready.sem, 1)
            apart(dve, scores_done.sem, scores_done.at(s, 3))
            for m in range(5):
                masked(m, dil_scores(m), row("mask_dil"), DIL_SCALE)
            yield 8
            scan(1)
            yield 9
            apart(dve, scores_done.sem, scores_done.at(s, 4))
            masked(5, dil_scores(5), row("mask_dil"), DIL_SCALE)
            yield 10
            scan(2)
            yield 12
            y_ps = bank[0][:, 0:SSM_W]
            dve.wait_ge(y_sq_ready.sem, y_sq_ready.at(s))
            link(V.tensor_scalar(y_in, y_sq, GELU_B, GELU_A, ALU.mult, ALU.add))
            V.tensor_tensor(y_in, y_in, y_ps, ALU.mult).then_inc(y_in_ready.sem, 1)
            dve.wait_ge(exp_ready.sem, exp_ready.at(s, 6))
            link(V.reciprocal(rden[:, 0:6], den[:, 0:6]))
            dve.wait_ge(o_done.sem, o_done.at(s, 1))
            y_dil = hy[:, SSM_W:SSM_W + DIL_W]
            V.tensor_tensor(y_dil.rearrange("p (h d) -> p h d", h=DIL_HEADS),
                            bank[3][:, 0:DIL_W].rearrange("p (h d) -> p h d", h=DIL_HEADS),
                            rden[:, 0:6].unsqueeze(2).broadcast_to([P, DIL_HEADS, HD]), ALU.mult).then_inc(dil_out.sem, 1)
            yield 13
            dve.wait_ge(y_th_ready.sem, y_th_ready.at(s))
            V.scalar_tensor_tensor(g_x2, y_th, 1.0, y_ps, ALU.add, ALU.mult).then_inc(g_ready.sem, 1)
            apart(dve, scores_done.sem, scores_done.at(s, 8))
            for m in range(8):
                masked(6 + m, diff_scores(m // 2, m % 2), row("mask_diff"), DIFF_SCALE)
            dve.wait_ge(ssq_done.sem, ssq_done.at(s, 2))
            norm_scale(1, ssq, 1.0 / DIL_W)
            link(V.tensor_scalar(y_dil, y_dil, rstd[:, 0:1], None, ALU.mult))
            link(V.tensor_tensor(lam, lexp[:, 0:1], lexp[:, 1:2], ALU.subtract))
            link(V.tensor_tensor(lam, lam, row("lambda_init"), ALU.add))
            yield 14
            for h in range(DIFF_HEADS):
                a = 6 + 2 * h
                dve.wait_ge(exp_ready.sem, exp_ready.at(s, a + 2))
                link(V.reciprocal(rden[:, a:a + 2], den[:, a:a + 2]))
                link(V.tensor_tensor(rden[:, a + 1:a + 2], rden[:, a + 1:a + 2], lam, ALU.mult))
                m1, m2 = probs[:, 512 * h:512 * h + 256], probs[:, 512 * h + 256:512 * (h + 1)]
                link(V.tensor_scalar(m2, m2, rden[:, a + 1:a + 2], None, ALU.mult))
                V.scalar_tensor_tensor(m1, m1, rden[:, a:a + 1], m2, ALU.mult, ALU.subtract).then_inc(attn_ready.sem, 1)
            yield 15
            dve.wait_ge(glu_th_ready.sem, glu_th_ready.at(s))
            V.scalar_tensor_tensor(y_glu, glu_th, 1.0, g_x2, ALU.add, ALU.mult).then_inc(gated_ready.sem, 1)
            yield 16
            dve.wait_ge(ssq_done.sem, ssq_done.at(s, 3))
            norm_scale(1, ssq, 1.0 / (16 * SSM_W))
            link(V.tensor_scalar(hy[:, 0:SSM_W], y_glu, rstd[:, 0:1], 0.25, ALU.mult, ALU.mult))
            dve.wait_ge(o_done.sem, o_done.at(s, 2))
            y_diff = hy[:, SSM_W + DIL_W:D]
            yd3 = y_diff.rearrange("p (h d) -> p h d", h=DIFF_HEADS)
            link(V.tensor_copy(y_diff, bank[4][:, 0:DIFF_W]))
            link(V.tensor_tensor(o_sq, y_diff, y_diff, ALU.mult))
            link(V.tensor_reduce(ssq4, o_sq.rearrange("p (h d) -> p h d", h=DIFF_HEADS), AX_X, ALU.add))
            norm_scale(4, ssq4, 1.0 / HD)
            link(V.tensor_scalar(rstd, rstd, row("one_less_init"), None, ALU.mult))
            V.tensor_tensor(yd3, yd3, rstd.unsqueeze(2).broadcast_to([P, DIFF_HEADS, HD]), ALU.mult).then_inc(y_ready.sem, 1)
            yield 17
            turned_gain((bank[0], bank[5]), y_turned, row("gy"), yT_ready)
            for n in range(2):
                yield 18 + n
                dve.wait_ge(mixed_done.sem, mixed_done.at(s, n + 1))
                ins = V.tensor_tensor(xs[:, 512 * n:512 * (n + 1)], xs[:, 512 * n:512 * (n + 1)], bank[1 + n][:, :], ALU.add)
                if n == 0:
                    step(ins)
            ins.then_inc(x_mid.sem, 1)
            dve.wait_ge(ssq_done.sem, ssq_done.at(s, 4))
            norm_scale(1, ssq, 1.0 / D)
            V.scalar_tensor_tensor(h2[:, :], xs, rstd[:, 0:1], row("g2"), ALU.mult, ALU.mult).then_inc(h2_ready.sem, 1)

            def top16(parts, width, vals, where):
                def part(a, i):
                    return a[:, width * i:width * (i + 1)]

                for i in parts:
                    step(V.max(vals[:, TOPK * i:TOPK * i + 8], part(wide_a, i)))
                apart(dve, vec.sem, vec.at(s, steps[0]))
                for i in parts:
                    step(V.match_replace(part(wide_b, i), vals[:, TOPK * i:TOPK * i + 8], part(wide_a, i), -3.0e38))
                    step(V.max_index(where[:, TOPK * i:TOPK * i + 8], vals[:, TOPK * i:TOPK * i + 8], part(wide_a, i)))
                apart(dve, vec.sem, vec.at(s, steps[0]))
                for i in parts:
                    step(V.max(vals[:, TOPK * i + 8:TOPK * i + 16], part(wide_b, i)))
                apart(dve, vec.sem, vec.at(s, steps[0]))
                for i in parts:
                    step(V.max_index(where[:, TOPK * i + 8:TOPK * i + 16], vals[:, TOPK * i + 8:TOPK * i + 16], part(wide_b, i)))
                settle()

            def key_top(g):
                apart(dve, key_scores_kept.sem, key_scores_kept.at(s, g + 1))
                top16(range(4 * g, 4 * g + 4), KEYS, top_s, top_i)

            ts4 = top_s[:, :].rearrange("p (h c k) -> p h c k", h=HEADS, c=2)
            tf4 = top_f[:, :].rearrange("p (h c k) -> p h c k", h=HEADS, c=2)

            def pair_top(g):
                hs = slice(2 * g, 2 * g + 2)
                link(V.tensor_tensor(wide_a[:, 512 * g:512 * (g + 1)].rearrange("p (h i j) -> p h i j", h=2, i=TOPK),
                                     ts4[:, hs, 0, :].unsqueeze(3).broadcast_to([P, 2, TOPK, TOPK]),
                                     ts4[:, hs, 1, :].unsqueeze(2).broadcast_to([P, 2, TOPK, TOPK]), ALU.add))
                step(V.tensor_copy(top_f[:, 64 * g:64 * (g + 1)], top_i[:, 64 * g:64 * (g + 1)]))
                apart(dve, vec.sem, vec.at(s, steps[0]))
                top16(range(2 * g, 2 * g + 2), TOPK * TOPK, best_s, best_j)

            def pick(half):
                H, n = HEADS // 2, SLOTS // 2
                hs, at = slice(H * half, H * (half + 1)), slice(n * half, n * (half + 1))
                hits = wide_b[:, 1024 * half:1024 * (half + 1)]
                for c, e in ((0, e_row), (1, e_col)):
                    if c == 0:
                        link(V.tensor_scalar(jpart[:, at], best_j[:, at], 4, None, ALU.logical_shift_right))
                    else:
                        link(V.tensor_scalar(jpart[:, at], best_j[:, at], TOPK - 1, None, ALU.bitwise_and))
                    link(V.tensor_copy(jf[:, at], jpart[:, at]))
                    hit = hits.rearrange("p (n i) -> p n i", i=TOPK)
                    link(V.tensor_tensor(hit, iota16.unsqueeze(1).broadcast_to([P, n, TOPK]),
                                         jf[:, at].unsqueeze(2).broadcast_to([P, n, TOPK]), ALU.is_equal))
                    hit4 = hits.rearrange("p (h k i) -> p h k i", h=H, k=TOPK)
                    link(V.tensor_tensor(hit4, hit4, tf4[:, hs, c, :].unsqueeze(2).broadcast_to([P, H, TOPK, TOPK]), ALU.mult))
                    link(V.tensor_reduce(e[:, at], hit, AX_X, ALU.add))
                link(V.scalar_tensor_tensor(e_row[:, at], e_row[:, at], float(KEYS), e_col[:, at], ALU.mult, ALU.add))
                V.tensor_scalar(idx[:, bass.ds((s & 1) * SLOTS + n * half, n)], e_row[:, at], row("first_expert"), None,
                                ALU.add).then_inc(picked.sem, 1)

            yield 24
            key_top(0)
            yield 25
            key_top(1)
            yield 26
            pair_top(0)
            pair_top(1)
            yield 27
            pick(0)
            yield 28
            key_top(2)
            key_top(3)
            yield 29
            pair_top(2)
            pair_top(3)
            b3 = best_s[:, :].rearrange("p (h k) -> p h k", h=HEADS)
            g3 = gate[:, chunk_cols(s, SLOTS)].rearrange("p (h k) -> p h k", h=HEADS)
            V.tensor_tensor(g3, b3, b3[:, :, 0:1].broadcast_to([P, HEADS, TOPK]), ALU.subtract).then_inc(gate_in.sem, 1)
            yield 30
            pick(1)
            apart(dve, gate_exp.sem, gate_exp.at(s))
            link(V.tensor_reduce(gsum, g3, AX_X, ALU.add))
            link(V.reciprocal(grec, gsum))
            link(V.tensor_scalar(grec, grec, 0.5, None, ALU.mult))
            V.tensor_tensor(g3, g3, grec.unsqueeze(2).broadcast_to([P, HEADS, TOPK]), ALU.mult).then_inc(mixer_done.sem, 1)
            assert steps[0] == VEC_STEPS, steps[0]

        def experts_dve_start(dve, p):
            dve.wait_ge(mixer_done.sem, mixer_done.at(p))
            nc.vector.tensor_copy(h2_cur[:, :], h2[:, :]).then_inc(handed.sem, 1)
            apart(dve, handed.sem, handed.at(p))

        def experts_dve(dve, p, i, q):
            V = nc.vector
            dots, inner, th = peer[:, 0:RING], peer[:, RING:RING + HALF], peer[:, RING + HALF:2 * RING]
            weight = peer[:, 2 * RING:3 * RING]
            act_x = peer[:, 3 * RING:3 * RING + HALF]
            for r in range(HALF * q, HALF * (q + 1)):
                g = gathered[r]
                dve.wait_ge(g.sem, (p * ITERS + i + 1) * 16)
                V.tensor_tensor_reduce(out=u_of[r], in0=u_of[r], in1=h2_cur[:, :], scale=1.0, scalar=0.0,
                                       op0=ALU.mult, op1=ALU.add, accum_out=dots[:, r:r + 1]).then_inc(dots_done.sem, 1)
            d = dots[:, HALF * q:HALF * (q + 1)]
            m = i * 6 + 3 * q
            dve.wait_ge(dots_done.sem, dots_done.at(p, 0) + (i * RING + HALF * (q + 1)))
            V.tensor_tensor(inner, d, d, ALU.mult).then_inc(gelu_step.sem, 1)
            dve.wait_ge(gelu_step.sem, gelu_step.at(p, 0) + (m + 1))
            V.tensor_scalar(inner, inner, GELU_B, GELU_A, ALU.mult, ALU.add).then_inc(gelu_step.sem, 1)
            dve.wait_ge(gelu_step.sem, gelu_step.at(p, 0) + (m + 2))
            V.tensor_tensor(inner, inner, d, ALU.mult).then_inc(inner_ready.sem, 1)
            dve.wait_ge(tanh_ready.sem, tanh_ready.at(p, 0) + (i * 2 + (q + 1)))
            V.scalar_tensor_tensor(act_x, th, 1.0, d, ALU.add, ALU.mult).then_inc(gelu_step.sem, 1)
            dve.wait_ge(gelu_step.sem, gelu_step.at(p, 0) + (m + 3))
            V.tensor_tensor(weight[:, HALF * q:HALF * (q + 1)], act_x, gate[:, slot_cols(p, i, q)],
                            ALU.mult).then_inc(weight_ready.sem, 1)

        def experts_dve_end(dve, p):
            dve.wait_ge(slot_free.sem, slot_free.at(p, SLOTS))
            xs = x[:, chunk_cols(p, D)]
            nc.vector.tensor_copy(xs[:, 0:512], acc[:, 0, :]).then_inc(copied.sem, 1)
            nc.vector.tensor_copy(xs[:, 512:D], acc[:, 1, :]).then_inc(x_ready.sem, 1)

        def experts_pool(pool, p, i):
            for q in range(2):
                apart(pool, slot_free.sem, p * SLOTS + i * RING + (HALF * q + 1))
                nc.gpsimd.tensor_copy(idx_stage[:, HALF * q:HALF * (q + 1)],
                                      idx[:, slot_cols(p, i, q)]).then_inc(staged.sem, 1)
                apart(pool, staged.sem, staged.at(p, 0) + (i * 2 + (q + 1)))
                for r in range(HALF * q, HALF * (q + 1)):
                    if r % HALF:
                        apart(pool, slot_free.sem, p * SLOTS + i * RING + (r + 1))
                    nc.gpsimd.indirect_dma_start(ring[:, 2 * D * r:2 * D * (r + 1)], None, uv,
                                                 bass.IndirectOffsetOnAxis(idx_stage[:, r:r + 1], 0)).then_inc(gathered[r].sem, 16)

        def run(mixer):
            for _ in mixer:
                pass

        def run_over_experts(mixer, experts, eng, s):
            done = 0
            for at in mixer:
                while done < at:
                    experts(eng, s - 1, done // 2, done % 2)
                    done += 1
            while done < 2 * ITERS:
                experts(eng, s - 1, done // 2, done % 2)
                done += 1

        def run_experts(experts, eng, p):
            with eng.Fori(0, ITERS) as i:
                for q in range(2):
                    experts(eng, p, i, q)

        @block.gpsimd
        def _(pool):
            nc.gpsimd.iota(iota16.bitcast(I32), pattern=[[1, TOPK]], base=0, channel_multiplier=0).then_inc(iota_ready, 1)
            with pool.Fori(0, STAGES) as p:
                for half in range(2):
                    apart(pool, picked.sem, picked.at(p, half + 1))
                    with pool.Fori(half * (ITERS // 2), (half + 1) * (ITERS // 2)) as i:
                        experts_pool(pool, p, i)

        @block.scalar
        def _(act):
            act.wait_ge(consts_in, 32)
            run(mixer_act(act, 0))
            with act.Fori(1, STAGES) as s:
                run_over_experts(mixer_act(act, s), experts_act, act, s)
            run_experts(experts_act, act, STAGES - 1)
            for c in range(CHUNKS):
                act.wait_ge(x_ready.sem, x_ready.at(STAGES - 2 + c, 1))
                if c:
                    act.wait_ge(fin_vec, 1)
                nc.scalar.activation(hy[:, :], x[:, D * c:D * (c + 1)], ACT.Square, accum_out=ssq).then_inc(fin_ssq, 1)

        @block.tensor
        def _(pe):
            pe.sem_inc(w_free.sem, W_SLOTS)
            pe.sem_inc(slot_free.sem, RING)
            pe.wait_ge(mem_ready, 2)
            run(mixer_pe(pe, 0))
            with pe.Fori(1, STAGES) as s:
                experts_pe_start(pe, s - 1)
                run_over_experts(mixer_pe(pe, s), experts_pe, pe, s)
            experts_pe_start(pe, STAGES - 1)
            run_experts(experts_pe, pe, STAGES - 1)

        @block.vector
        def _(dve):
            V = nc.vector
            dve.sem_inc(x_ready.sem, 2)
            for k, t in enumerate((kT, fkT, dv, fv, carry)):
                V.memset(t[:, :], 0.0).then_inc(copied.sem, 1)
            dve.wait_ge(copied.sem, 5)
            dve.sem_inc(mem_ready, 1)
            dve.wait_ge(consts_in, 32)
            dve.wait_ge(iota_ready, 1)
            V.tensor_copy(iota16, iota16.bitcast(I32)).then_inc(mem_ready, 1)
            run(mixer_dve(dve, 0))
            with dve.Fori(1, STAGES) as s:
                experts_dve_start(dve, s - 1)
                run_over_experts(mixer_dve(dve, s), experts_dve, dve, s)
                experts_dve_end(dve, s - 1)
            experts_dve_start(dve, STAGES - 1)
            run_experts(experts_dve, dve, STAGES - 1)
            experts_dve_end(dve, STAGES - 1)

            n_own = [0]

            def own(ins):
                n_own[0] += 1
                ins.then_inc(mem_ready, 1)
                dve.wait_ge(mem_ready, 2 + n_own[0])

            dve.wait_ge(fin_rows, 16)
            for c in range(CHUNKS):
                dve.wait_ge(fin_ssq, c + 1)
                y, m, t = rstd[:, 0:1], ms[:, 0:1], nt[:, 0:1]
                ti = ti_a[:, 0:1].bitcast(I32)
                own(V.tensor_scalar(m, ssq, 1.0 / D, EPS, ALU.mult, ALU.add))
                own(V.tensor_scalar(ti, m.bitcast(I32), 1, None, ALU.logical_shift_right))
                own(V.tensor_scalar(y.bitcast(I32), ti, -1.0, RSQRT_SEED, ALU.mult, ALU.add))
                for _ in range(3):
                    own(V.tensor_tensor(t, y, y, ALU.mult))
                    own(V.tensor_tensor(t, t, m, ALU.mult))
                    own(V.tensor_scalar(t, t, -0.5, 1.5, ALU.mult, ALU.add))
                    own(V.tensor_tensor(y, y, t, ALU.mult))
                V.scalar_tensor_tensor(work[:, D * c:D * (c + 1)], x[:, D * c:D * (c + 1)], y, rows[:, 0:D],
                                       ALU.mult, ALU.mult).then_inc(fin_vec, 1)


def kernel(**inputs):
    import numpy as np
    import concourse.bacc as bacc
    from concourse import mybir as _mybir
    from concourse.bass_utils import run_bass_kernel_spmd

    a = {k: np.asarray(v) for k, v in inputs.items()}
    f32 = np.float32

    def cols(w, width):
        n = w.shape[1] // width
        return w.reshape(KT, P, n, width).transpose(2, 1, 0, 3).reshape(n, P, KT * width)

    wts = np.zeros((L, BLOCKS, P, WB), f32)
    rows = np.zeros((STAGES, P, ROWS_W), f32)
    for l in range(L):
        wts[l, B_IN:B_IN + 9] = cols(a["w_in"][l], 256)
        glu = a["ssm_w_glu"][l].reshape(SSM_T, P, SSM_W).transpose(1, 0, 2).reshape(P, -1)
        wts[l, B_SSM, :, 0:1152] = glu
        for n, name in ((1152, "ssm_b_re"), (1536, "ssm_b_im")):
            b = a[name][l]
            for g in range(GROUPS):
                t, ch = g // 2, (g % 8) * GROUP_CH
                at = n + P * (g // 8) + STATE * (g % 2)
                wts[l, B_SSM, ch:ch + GROUP_CH, at:at + STATE] = b[g].T
        wts[l, B_OUT:B_OUT + 4] = cols(a["w_out"][l], 256)
        wts[l, B_QUERY:B_QUERY + 8] = cols(a["peer_w_query"][l], 256)
        wts[l, B_KEYS] = a["peer_sub_keys"][l].reshape(HC, KEYS, P).transpose(2, 0, 1).reshape(P, -1)

    q = np.arange(P)[:, None]
    k = np.arange(2 * P)[None, :]
    for s in range(STAGES):
        l, c = s // 2, s % 2
        r = rows[s]

        def put(name, value):
            at, n = ROW_AT[name]
            r[:, at:at + n] = value

        put("g2", a["norm2_g"][l])
        back = P * c + q - k
        held = sum(((back >= 0) & (back <= w) & (back % d == 0)).astype(f32) for w, d in ((128, 1), (512, 4), (2048, 16)))
        put("mask_dil", np.where(held > 0, np.log(np.maximum(held, 1)) / DIL_SCALE, -1e30))
        put("mask_diff", np.where(back >= 0, 0.0, -1e30))
        for name, field in (("ssm_c_re", "c_re"), ("ssm_c_im", "c_im")):
            at, _ = ROW_AT[field]
            cm = a[name][l]
            for g in range(GROUPS):
                p0, o = STATE * (g % 2), at + 32 * (g // 2) + GROUP_CH * (g % 2)
                r[p0:p0 + STATE, o:o + GROUP_CH] = cm[g].T
        put("quarter", (np.arange(P)[:, None] // 32 == np.arange(SQ)[None, :]).astype(f32))
        put("d_skip", a["ssm_d"][l].reshape(SSM_T, P).T)
        put("g1", a["norm1_g"][l].reshape(KT, P).T)
        gy = np.concatenate([a["ssm_norm_g"][l], a["dil_norm_g"][l]] + [a["diff_subln_g"][l]] * DIFF_HEADS)
        put("gy", gy.reshape(KT, P).T)
        put("lam_re", a["ssm_lam_re"][l].reshape(ST, P).T)
        put("lam_im", a["ssm_lam_im"][l].reshape(ST, P).T)
        put("log_step", np.repeat(a["ssm_log_step"][l], STATE).reshape(ST, P).T)
        for name in ("lam_q1", "lam_k1", "lam_q2", "lam_k2"):
            put(name, a[f"diff_{name}"][l])
        init = 0.8 - 0.6 * np.exp(-0.3 * l)
        put("lambda_init", init)
        put("one_less_init", 1.0 - init)
        put("first_expert", float(EXPERTS * l))
    uv = np.concatenate([a["peer_u"], a["peer_v"]], axis=2).reshape(L * EXPERTS, 2 * D)
    arrays = {
        "x_dram": np.ascontiguousarray(a["x"]), "wts_dram": wts.reshape(L * BLOCKS, P, WB), "rows_dram": rows,
        "uv_dram": uv, "ident_dram": np.eye(P, dtype=f32),
        "final_g_dram": np.ascontiguousarray(np.broadcast_to(a["final_norm_g"], (P, D))),
    }
    nc = bacc.Bacc("TRN2", target_bir_lowering=False, num_devices=1)
    args = [nc.dram_tensor(n, t.shape, _mybir.dt.float32, kind="ExternalInput").ap() for n, t in arrays.items()]
    out = nc.dram_tensor("out_dram", a["x"].shape, _mybir.dt.float32, kind="ExternalOutput").ap()
    trunk(nc, *args, out)
    r = run_bass_kernel_spmd(nc, [arrays], core_ids=[0])
    return r.results[0]["out_dram"]
```

```python
from contextlib import ExitStack

import concourse.bass as bass
from concourse import mybir

ALU = mybir.AluOpType
ACT = mybir.ActivationFunctionType
AX_X = mybir.AxisListType.X
F32 = mybir.dt.float32
I32 = mybir.dt.int32
U32 = mybir.dt.uint32

P = 128
D = 1024
KT = D // P
L = 2
CHUNKS = 2
STAGES = L * CHUNKS
EPS = 1e-6
PI = 3.14159265358979

SSM_W, DIL_W, DIFF_W = 384, 384, 256
SSM_T = SSM_W // P
GROUPS, GROUP_CH, STATE = 24, 16, 64
ST = GROUPS * STATE // P
SQ = 4
DIL_HEADS, DIFF_HEADS, HD, DQK = 6, 4, 64, 32
HEADS, TOPK, KEYS = 8, 16, 128
HC = 2 * HEADS
SLOTS = HEADS * TOPK
EXPERTS = KEYS * KEYS

RING = 8
HALF = RING // 2
ITERS = SLOTS // RING

WB = 2048
W_SLOTS = 4
IN_BLOCK = (0, 1, 2, 3, 4, 5, 7, 8, 9)
B_SSM, B_GLU, B_OUT = 6, 10, 11
QUERY_BLOCK = (15, 16, 18, 19, 20, 22, 23, 25)
KEY_BLOCK = (17, 21, 24, 26)
BLOCKS = 27
B_WIDTH = {B_SSM: 2 * SSM_W, B_GLU: SSM_T * SSM_W, **{b: 4 * P for b in KEY_BLOCK}}
W_PER_SLOT = [len(range(j, BLOCKS, W_SLOTS)) for j in range(W_SLOTS)]

ROW_FIELDS = [("g2", D), ("mask_dil", 2 * P), ("mask_diff", 2 * P), ("c_re", ST * 32), ("c_im", ST * 32),
              ("d_skip", SSM_T), ("quarter", SQ), ("g1", KT), ("gy", KT), ("g2_col", KT),
              ("lam_re", ST), ("lam_im", ST), ("log_step", ST),
              ("lam_q1", DQK), ("lam_k1", DQK), ("lam_q2", DQK), ("lam_k2", DQK),
              ("lambda_init", 1), ("one_less_init", 1), ("first_expert", 1)]
ROW_AT, _at = {}, 0
for _name, _n in ROW_FIELDS:
    ROW_AT[_name] = (_at, _n)
    _at += _n
ROWS_W = _at

GELU_A = 0.7978845608028654
GELU_B = GELU_A * 0.044715
DIL_SCALE = HD ** -0.5
DIFF_SCALE = DQK ** -0.5
ROUND = 1.5 * 2.0 ** 23
RSQRT_SEED = float(0x5F3759DF)

VEC_STEPS, PICK_STEPS = 280, 89

MIXER_LATE = 3


def trunk(nc, x_in, wts, rows_in_dram, uv, ident_in, final_g, out):
    with ExitStack() as ctx:
        def sb(name, width, dt=F32):
            return ctx.enter_context(nc.sbuf_tensor(name, [P, width], dt))

        def sem(name):
            return ctx.enter_context(nc.semaphore(name))

        ring = sb("ring", RING * 2 * D)
        wring = sb("wring", W_SLOTS * WB)
        x = sb("x", CHUNKS * D)
        hy = sb("hy", D)
        h2 = sb("h2", D)
        h2_cur = sb("h2_cur", D)
        hT = sb("hT", KT * P)
        uqT = sb("uqT", 6 * P)
        fqT = sb("fqT", 2 * P)
        kT = sb("kT", 3 * 2 * P)
        fkT = sb("fkT", 2 * 2 * P)
        dv = sb("dv", 2 * DIL_W)
        fv = sb("fv", 2 * DIFF_W)
        rows = sb("rows", ROWS_W)
        cos = sb("cos", ST * P)
        sin = sb("sin", ST * P)
        crot = sb("crot", 3 * ST * 32)
        ddiag = sb("ddiag", SSM_W)
        work = sb("work", 7680)
        ident = sb("ident", P)
        diag = sb("diag", RING * P)
        carry = sb("carry", (STAGES + 1) * 2 * ST)
        small = sb("small", 640)
        gate = sb("gate", 2 * SLOTS)
        idx = sb("idx", 2 * SLOTS, I32)
        idx_stage = sb("idx_stage", RING, I32)
        peer = sb("peer", 4 * RING)

        def row(name):
            a, n = ROW_AT[name]
            return rows[:, a:a + n]

        taken = [0]

        def tiny(n, dt=F32):
            a = small[:, taken[0]:taken[0] + n]
            taken[0] += n
            assert taken[0] <= 640
            return a

        v_re, v_im, z_re, z_im = (work[:, 512 * i:512 * i + 512] for i in range(4))
        p_cr, p_si, p_sr, p_ci = (work[:, 2048 + 512 * i:2560 + 512 * i] for i in range(4))
        dbl = [work[:, 6144 + 768 * i:6144 + 768 * i + 768] for i in range(2)]
        y_sq, y_in, y_th, gT_x2, glu_th, y_glu = (work[:, SSM_W * i:SSM_W * (i + 1)] for i in (0, 1, 2, 3, 5, 6))
        u_spread = work[:, 4096:5632]
        probs = work[:, 4096:6144]
        pT = work[:, 6144:7680]
        wide_a, wide_b, wide_c = (work[:, 2048 * i:2048 * i + 2048] for i in range(3))
        squares, squares_d = work[:, 2688:3072], work[:, 2048:3072]
        o_sq = work[:, 7424:7680]

        wslot = [wring[:, WB * j:WB * (j + 1)] for j in range(W_SLOTS)]
        u_of = [ring[:, 2 * D * r:2 * D * r + D] for r in range(RING)]
        v_of = [ring[:, 2 * D * r + D:2 * D * (r + 1)] for r in range(RING)]
        w_as = lambda b, k, n: wslot[b % W_SLOTS].rearrange("p (k n) -> p k n", k=k)[:, :, 0:n]
        w_glu = wslot[B_GLU % W_SLOTS][:, 0:SSM_T * SSM_W].rearrange("p (k n) -> p k n", k=SSM_T)
        b_re, b_im = (wslot[B_SSM % W_SLOTS][:, SSM_W * i:SSM_W * (i + 1)].rearrange("p (k n) -> p k n", k=3)
                      for i in range(2))

        ssq, sums, ms, rstd, nt = tiny(1), tiny(6), tiny(6), tiny(6), tiny(6)
        ti_a = tiny(6)
        step_t, theta, rad, turn_n = (tiny(ST) for _ in range(4))
        cos1, sin1, f_re, f_im, ta, tb = (tiny(ST) for _ in range(6))
        lam = tiny(1)
        lsum = tiny(2)
        lexp = tiny(2)
        nmax = tiny(14)
        den = tiny(14)
        rden = tiny(14)
        lprod = tiny(DQK)
        gsum, grec = tiny(HEADS // 2), tiny(HEADS // 2)
        base = tiny(1)
        iota16 = tiny(TOPK)

        top_s = sb("top_s", HC * TOPK)
        top_i = sb("top_i", HC * TOPK, U32)
        top_f = sb("top_f", HC * TOPK)
        best_s = sb("best_s", SLOTS)
        best_j = sb("best_j", SLOTS, U32)
        jpart = sb("jpart", 2 * TOPK, U32)
        jlow = sb("jlow", 2 * TOPK, U32)
        jf = sb("jf", 2 * TOPK)
        e_row = sb("e_row", 2 * TOPK)
        e_col = sb("e_col", 2 * TOPK)

        acc = ctx.enter_context(nc.psum_tensor("acc", [P, 2, 512], F32))
        bank = [ctx.enter_context(nc.psum_tensor(f"bank{i}", [P, 512], F32)) for i in range(6)]

        class Signal:

            def __init__(self, name, per_stage=1, before=0):
                self.sem, self.n, self.before = sem(name), per_stage, before

            def at(self, s, k=1):
                return s * self.n + (self.before + k)

        consts_in = sem("consts_in")
        x1_in = sem("x1_in")
        rows_in = sem("rows_in")
        w_in = [sem(f"w_in{j}") for j in range(W_SLOTS)]
        w_free = [Signal(f"w_free{j}", W_PER_SLOT[j], 1) for j in range(W_SLOTS)]
        x_ready = Signal("x_ready", 1, 2)
        mixer_done = Signal("mixer_done")
        picked = Signal("picked", 4)
        all_picked = Signal("all_picked")
        mem_ready = sem("mem_ready")
        iota_ready = sem("iota_ready")
        sep = sem("sep")

        ssq_done = Signal("ssq_done", 3)
        rstd_ready = Signal("rstd_ready")
        hn_ready = Signal("hn_ready")
        hn_turned = Signal("hn_turned", 2)
        hT_ready = Signal("hT_ready", 2)
        proj_done = Signal("proj_done", 5)
        proj_kept = Signal("proj_kept", 8)
        par_exp = Signal("par_exp", 3)
        par_vec = Signal("par_vec", 2)
        spread_ready = Signal("spread_ready", 3)
        tables_ready = Signal("tables_ready")
        ddiag_ready = Signal("ddiag_ready")
        bu_done = Signal("bu_done", 3)
        bu_free = Signal("bu_free", 3)
        prod_ready = Signal("prod_ready", 3)
        y_part = Signal("y_part", 3)
        y_sq_ready = Signal("y_sq_ready")
        y_in_ready = Signal("y_in_ready")
        y_th_ready = Signal("y_th_ready")
        g_ready = Signal("g_ready")
        g_turned = Signal("g_turned")
        glu_done = Signal("glu_done")
        glu_th_ready = Signal("glu_th_ready")
        gated_ready = Signal("gated_ready")
        dil_out = Signal("dil_out")
        scores_done = Signal("scores_done", 8)
        masked_ready = Signal("masked_ready", 14)
        exp_ready = Signal("exp_ready", 14)
        attn_ready = Signal("attn_ready", 4)
        p_turned = Signal("p_turned", 5)
        pT_ready = Signal("pT_ready", 5)
        o_done = Signal("o_done", 2)
        y_ready = Signal("y_ready")
        y_turned = Signal("y_turned", 2)
        yT_ready = Signal("yT_ready", 2)
        mixed_done = Signal("mixed_done", 2)
        x_mid = Signal("x_mid")
        x_kept = Signal("x_kept")
        h2_ready = Signal("h2_ready")
        x_turned = Signal("x_turned", 2)
        xT_ready = Signal("xT_ready", 2)
        q_done = Signal("q_done", 4)
        q_kept = Signal("q_kept", 4)
        key_scores_done = Signal("key_scores_done", 4)
        key_scores_kept = Signal("key_scores_kept", 4)
        gate_in = Signal("gate_in", 2)
        gate_exp = Signal("gate_exp", 2)
        vec = Signal("vec_step", VEC_STEPS)
        pick_vec = Signal("pick_step", PICK_STEPS)

        handed = Signal("handed")
        staged = Signal("staged", 2 * ITERS)
        gathered = [Signal(f"gathered{r}", ITERS) for r in range(RING)]
        dots_done = Signal("dots_done", SLOTS)
        gelu_step = Signal("gelu_step", 3 * 2 * ITERS)
        inner_ready = Signal("inner_ready", 2 * ITERS)
        tanh_ready = Signal("tanh_ready", 2 * ITERS)
        weight_ready = Signal("weight_ready", 2 * ITERS)
        diag_ready = Signal("diag_ready", SLOTS)
        slot_free = Signal("slot_free", SLOTS, RING)
        copied = Signal("copied", 1)
        fin_ssq, fin_vec, fin_rows = sem("fin_ssq"), sem("fin_vec"), sem("fin_rows")
        fin_step = [sem(f"fin_step{c}") for c in range(CHUNKS)]
        stored = sem("stored")

        def chunk_cols(s, width):
            return bass.ds((s & 1) * width, width)

        def half_slots(t, s, half):
            return t[:, bass.ds((s & 1) * SLOTS + (SLOTS // 2) * half, SLOTS // 2)]

        def slot_cols(p, i, q):
            return bass.ds((p & 1) * SLOTS + i * RING + HALF * q, HALF)

        def apart(eng, sem_, value):
            eng.wait_ge(sem_, value)
            eng.sem_inc(sep, 1)

        block = ctx.enter_context(nc.Block())

        def load_stage(sp, s):
            first = type(s) is int and s == 0

            def load_rows():
                if not first:
                    sp.wait_ge(mixer_done.sem, mixer_done.at(s, 0))
                sp.dma_start(rows[:, :], rows_in_dram[bass.ds(s, 1)].rearrange("a p n -> (a p) n")).then_inc(rows_in, 16)

            if first:
                load_rows()
                sp.dma_start(x[:, D:2 * D], x_in[0, P:2 * P, :]).then_inc(x1_in, 16)
            for b in range(BLOCKS):
                if b == W_SLOTS and not first:
                    load_rows()
                j = b % W_SLOTS
                sp.wait_ge(w_free[j].sem, w_free[j].at(s, b // W_SLOTS))
                width = B_WIDTH.get(b, WB)
                src = wts[bass.ds((s // 2) * BLOCKS + b, 1)].rearrange("a p n -> (a p) n")[:, 0:width]
                sp.dma_start(wslot[j][:, 0:width], src).then_inc(w_in[j], 16)

        @block.sync
        def _(sp):
            sp.dma_start(x[:, 0:D], x_in[0, 0:P, :]).then_inc(consts_in, 16)
            sp.dma_start(ident[:, :], ident_in).then_inc(consts_in, 16)
            load_stage(sp, 0)
            with sp.Fori(1, STAGES) as s:
                load_stage(sp, s)
            sp.wait_ge(mixer_done.sem, STAGES)
            sp.dma_start(rows[:, 0:D], final_g).then_inc(fin_rows, 16)
            for c in range(CHUNKS):
                sp.wait_ge(fin_vec, c + 1)
                sp.dma_start(out[0, P * c:P * (c + 1), :], work[:, D * c:D * (c + 1)]).then_inc(stored, 16)
            sp.wait_ge(stored, 16 * CHUNKS)

        def block_here(eng, s, b):
            j = b % W_SLOTS
            eng.wait_ge(w_in[j], s * (16 * W_PER_SLOT[j]) + 16 * (b // W_SLOTS + 1))

        def block_used(b):
            return w_free[b % W_SLOTS].sem

        def block_used_at(s, b):
            return w_free[b % W_SLOTS].at(s, b // W_SLOTS + 1)

        def dil_scores(h):
            return (bank[3], bank[4], bank[3], bank[4], bank[5], bank[5])[h], 256 * (h in (2, 3, 5))

        def diff_scores(h, m):
            return (bank[1], bank[2], bank[4], bank[5])[2 * (h % 2) + m], 256 * (h // 2)

        def scored(m):
            if m < 4:
                return h2[:, 256 * m:256 * (m + 1)]
            if m < 6:
                return work[:, 5632 + 256 * (m - 4):5888 + 256 * (m - 4)]
            return probs[:, 256 * (m - 6):256 * (m - 5)]

        def dil_probs(h, kc):
            return scored(h)[:, P * kc:P * (kc + 1)]

        dil_turn = (bank[3], bank[4], bank[5])
        diff_turn = (bank[1], bank[2])
        key_bank = (bank[4], bank[5], bank[0], bank[1])

        def mixer_pe(pe, s):
            yield 0
            mm = nc.tensor.matmul

            def turn(src, banks, done):
                for j in range(2):
                    for k in range(4):
                        t = 4 * j + k
                        last = nc.tensor.transpose(banks[j][:, P * k:P * (k + 1)], src[:, P * t:P * (t + 1)], ident[:, :])
                    last.then_inc(done.sem, 1)

            def project(n, tiles):
                for i in tiles:
                    b = IN_BLOCK[i // 2]
                    if i % 2 == 0:
                        block_here(pe, s, b)
                    w = w_as(b, KT, 256)[:, :, P * (i % 2):P * (i % 2 + 1)]
                    for k in range(KT):
                        h = hT[:, P * k:P * (k + 1)]
                        lhsT, rhs = (h, w[:, k, :]) if i in (9, 10, 11, 16, 17) else (w[:, k, :], h)
                        last = mm(bank[n][:, P * (i % 4):P * (i % 4 + 1)], lhsT, rhs, start=(k == 0), stop=(k == KT - 1))
                    if i % 2:
                        last.then_inc(block_used(b), 1)
                pe.wait_ge(block_used(b), block_used_at(s, b))
                pe.sem_inc(proj_done.sem, 1)

            def state_inputs(g):
                pe.wait_ge(spread_ready.sem, spread_ready.at(s, g + 1))
                for b_w, o in ((b_re, bank[1]), (b_im, bank[2])):
                    last = mm(o[:, :], b_w[:, g, :], u_spread[:, 512 * g:512 * (g + 1)], start=True, stop=True)
                last.then_inc(bu_done.sem, 1)

            y_ps = bank[0]
            cr = crot[:, :].rearrange("p (c j n) -> p c j n", c=3, j=ST)

            def state_outputs(g):
                pe.wait_ge(prod_ready.sem, prod_ready.at(s, g + 1))
                for j in range(SQ):
                    t = SQ * g + j
                    for prod, which in ((p_cr, 0), (p_si, 1), (p_sr, 2), (p_ci, 2)):
                        last = mm(y_ps[32 * j:32 * (j + 1), P * g:P * (g + 1)], cr[:, which, t, :], prod[:, P * j:P * (j + 1)],
                                  start=False, stop=False, skip_group_check=True)
                last.then_inc(y_part.sem, 1)

            def dil_score(h):
                a, i = HD * (h % 2), h // 2
                o, half = dil_scores(h)
                return mm(o[:, half:half + 256], uqT[a:a + HD, P * (3 + i):P * (4 + i)],
                          kT[a:a + HD, 256 * i:256 * (i + 1)], start=True, stop=True)

            def dil_turned(i):
                for b in range(4):
                    last = nc.tensor.transpose(dil_turn[i][:, P * b:P * (b + 1)], dil_probs(2 * i + b // 2, b % 2),
                                               ident[:, :])
                last.then_inc(p_turned.sem, 1)

            def dil_values(i):
                pe.wait_ge(pT_ready.sem, pT_ready.at(s, i + 1))
                for b in range(2):
                    h = 2 * i + b
                    for kc in range(2):
                        last = mm(bank[3][:, HD * h:HD * (h + 1)], pT[:, 512 * i + P * (2 * b + kc):512 * i + P * (2 * b + kc + 1)],
                                  dv[:, DIL_W * kc + HD * h:DIL_W * kc + HD * (h + 1)],
                                  start=(h == 0 and kc == 0), stop=False, skip_group_check=True)
                return last

            pe.wait_ge(hn_ready.sem, hn_ready.at(s))
            turn(hy, bank[0:2], hn_turned)
            yield 1
            pe.wait_ge(hT_ready.sem, hT_ready.at(s, 2))
            project(0, range(0, 4))
            yield 2
            project(1, range(4, 8))
            yield 3
            project(2, range(8, 12))
            yield 4
            block_here(pe, s, B_SSM)
            pe.wait_ge(proj_kept.sem, proj_kept.at(s, 5))
            state_inputs(0)
            project(3, range(12, 16))
            yield 6
            pe.wait_ge(bu_free.sem, bu_free.at(s, 1))
            state_inputs(1)
            project(4, range(16, 18))
            yield 7
            pe.wait_ge(ddiag_ready.sem, ddiag_ready.at(s))
            for i in range(SSM_T):
                mm(y_ps[:, P * i:P * (i + 1)], ddiag[:, P * i:P * (i + 1)], uqT[:, P * i:P * (i + 1)],
                   start=(i == 0), stop=False, skip_group_check=True)
            pe.wait_ge(tables_ready.sem, tables_ready.at(s))
            state_outputs(0)
            pe.wait_ge(proj_kept.sem, proj_kept.at(s, 8))
            for h in range(DIL_HEADS):
                if h == 5:
                    pe.wait_ge(scores_done.sem, scores_done.at(s, 3))
                last = dil_score(h)
                if h in (1, 3, 4, 5):
                    last.then_inc(scores_done.sem, 1)
            yield 9
            pe.wait_ge(bu_free.sem, bu_free.at(s, 2))
            state_inputs(2)
            pe.wait_ge(bu_done.sem, bu_done.at(s, 3))
            pe.sem_inc(block_used(B_SSM), 1)
            state_outputs(1)
            yield 10
            for i, last_map in enumerate((3, 4, 6)):
                pe.wait_ge(exp_ready.sem, exp_ready.at(s, last_map))
                dil_turned(i)
            yield 11
            dil_values(0)
            dil_values(1)
            dil_values(2).then_inc(o_done.sem, 1)
            pe.wait_ge(bu_free.sem, bu_free.at(s, 3))
            for h in range(DIFF_HEADS):
                for m in range(2):
                    a = HD * (h % 2) + DQK * m
                    o, half = diff_scores(h, m)
                    last = mm(o[:, half:half + 256], fqT[a:a + DQK, P * (h // 2):P * (h // 2 + 1)],
                              fkT[a:a + DQK, 256 * (h // 2):256 * (h // 2 + 1)], start=True, stop=True)
                last.then_inc(scores_done.sem, 1)
            state_outputs(2)
            yield 13
            pe.wait_ge(g_ready.sem, g_ready.at(s))
            for i in range(SSM_T):
                last = nc.tensor.transpose(bank[0][:, P * i:P * (i + 1)], gT_x2[:, P * i:P * (i + 1)], ident[:, :])
            last.then_inc(g_turned.sem, 1)
            block_here(pe, s, B_GLU)
            pe.wait_ge(dil_out.sem, dil_out.at(s))
            for i in range(SSM_T):
                last = mm(bank[3][:, 0:SSM_W], gT_x2[:, P * i:P * (i + 1)], w_glu[:, i, :],
                          start=(i == 0), stop=(i == SSM_T - 1))
            last.then_inc(glu_done.sem, 1)
            pe.wait_ge(glu_done.sem, glu_done.at(s))
            pe.sem_inc(block_used(B_GLU), 1)
            for i, o in enumerate(diff_turn):
                pe.wait_ge(attn_ready.sem, attn_ready.at(s, 2 * i + 2))
                for b in range(2):
                    for kc in range(2):
                        a = 512 * (2 * i + b) + P * kc
                        last = nc.tensor.transpose(o[:, P * (2 * b + kc):P * (2 * b + kc + 1)], probs[:, a:a + P], ident[:, :])
                last.then_inc(p_turned.sem, 1)
            yield 14
            for i in range(2):
                pe.wait_ge(pT_ready.sem, pT_ready.at(s, 4 + i))
                for b in range(2):
                    h = 2 * i + b
                    for kc in range(2):
                        a = 512 * i + P * (2 * b + kc)
                        last = mm(bank[4][:, HD * h:HD * (h + 1)], pT[:, a:a + P],
                                  fv[:, DIFF_W * kc + HD * h:DIFF_W * kc + HD * (h + 1)],
                                  start=(h == 0 and kc == 0), stop=False, skip_group_check=True)
            last.then_inc(o_done.sem, 1)
            yield 15
            pe.wait_ge(y_ready.sem, y_ready.at(s))
            turn(hy, (bank[0], bank[5]), y_turned)
            for half in range(2):
                yield 16 + half
                if half == 0:
                    pe.wait_ge(yT_ready.sem, yT_ready.at(s, 2))
                for n in (2 * half, 2 * half + 1):
                    b = B_OUT + n
                    block_here(pe, s, b)
                    w = w_as(b, KT, 256)
                    for k in range(KT):
                        last = mm(bank[1 + half][:, 256 * (n % 2):256 * (n % 2) + 256], hT[:, P * k:P * (k + 1)], w[:, k, :],
                                  start=(k == 0), stop=(k == KT - 1))
                    last.then_inc(block_used(b), 1)
                pe.wait_ge(block_used(b), block_used_at(s, b))
                pe.sem_inc(mixed_done.sem, 1)
            yield 18
            pe.wait_ge(x_mid.sem, x_mid.at(s))
            turn(hy, bank[4:6], x_turned)

            def queries(half):
                b = QUERY_BLOCK[half]
                block_here(pe, s, b)
                n = half // 2
                for i in (2 * half, 2 * half + 1):
                    w = w_as(b, KT, 256)[:, :, P * (i % 2):P * (i % 2 + 1)]
                    for k in range(KT):
                        last = mm(bank[n][:, P * (i % 4):P * (i % 4 + 1)], w[:, k, :], hT[:, P * k:P * (k + 1)],
                                  start=(k == 0), stop=(k == KT - 1))
                last.then_inc(block_used(b), 1)
                if half % 2:
                    pe.wait_ge(block_used(b), block_used_at(s, b))
                    pe.sem_inc(q_done.sem, 1)

            def key_scores(g):
                b = KEY_BLOCK[g]
                block_here(pe, s, b)
                pe.wait_ge(q_kept.sem, q_kept.at(s, g + 1))
                for i in range(4):
                    last = mm(key_bank[g][:, P * i:P * (i + 1)], wide_c[:, P * (4 * g + i):P * (4 * g + i + 1)],
                              wslot[b % W_SLOTS][:, P * i:P * (i + 1)], start=True, stop=True)
                last.then_inc(key_scores_done.sem, 1)

            def keys_used(g):
                pe.wait_ge(key_scores_done.sem, key_scores_done.at(s, g + 1))
                pe.sem_inc(block_used(KEY_BLOCK[g]), 1)

            yield 19
            pe.wait_ge(xT_ready.sem, xT_ready.at(s, 2))
            queries(0)
            queries(1)
            yield 20
            key_scores(0)
            queries(2)
            keys_used(0)
            queries(3)
            for g in range(1, 4):
                yield 20 + g
                if g < 3:
                    queries(2 * g + 2)
                key_scores(g)
                if g < 3:
                    queries(2 * g + 3)
                keys_used(g)

        def experts_pe_start(pe, p):
            pe.wait_ge(x_kept.sem, x_kept.at(p))
            apart(pe, x_ready.sem, x_ready.at(p, 0))
            xs = x[:, chunk_cols(p, D)]
            for n in range(2):
                nc.tensor.matmul(acc[:, n, :], ident[:, :], xs[:, 512 * n:512 * (n + 1)],
                                 start=True, stop=False, skip_group_check=True)

        def experts_pe(pe, p, i, q):
            for r in range(HALF * q, HALF * (q + 1)):
                pe.wait_ge(diag_ready.sem, diag_ready.at(p, i * RING + (r + 1)))
                for n in range(2):
                    last = nc.tensor.matmul(acc[:, n, :], diag[:, P * r:P * (r + 1)], v_of[r][:, 512 * n:512 * (n + 1)],
                                            start=False, stop=False, skip_group_check=True)
                last.then_inc(slot_free.sem, 1)

        def mixer_act(act, s):
            yield 0
            A = nc.scalar.activation
            xs = x[:, chunk_cols(s, D)]

            def keep(out_ap, in_ap, sig):
                A(out_ap, in_ap, ACT.Copy).then_inc(sig.sem, 1)

            kT3 = kT[:, :].rearrange("p (t c n) -> p t c n", t=3, c=2)
            fkT3 = fkT[:, :].rearrange("p (t c n) -> p t c n", t=2, c=2)
            one = bass.ds(s & 1, 1)

            def bk(i, a, b):
                return bank[i][:, P * a:P * b]

            def spread(g):
                for j in range(SQ):
                    at = 512 * g + P * j
                    ins = A(u_spread[:, at:at + P], uqT[:, P * g:P * (g + 1)], ACT.Copy, scale=row("quarter")[:, j:j + 1])
                ins.then_inc(spread_ready.sem, 1)

            def soften(m):
                act.wait_ge(masked_ready.sem, masked_ready.at(s, m + 1))
                pm = scored(m)
                A(pm, pm, ACT.Exp, scale=-1.0, bias=nmax[:, m:m + 1], accum_out=den[:, m:m + 1]).then_inc(exp_ready.sem, 1)

            apart(act, x_ready.sem, x_ready.at(s, -1))
            A(hy[:, :], xs, ACT.Square, accum_out=ssq).then_inc(ssq_done.sem, 1)
            act.wait_ge(rows_in, 16 * s + 16)
            A(step_t, row("log_step"), ACT.Exp).then_inc(par_exp.sem, 1)
            apart(act, rstd_ready.sem, rstd_ready.at(s))
            A(hy[:, :], xs, ACT.Copy, scale=rstd[:, 0:1]).then_inc(hn_ready.sem, 1)
            yield 2
            act.wait_ge(par_vec.sem, par_vec.at(s, 1))
            A(rad, ta, ACT.Exp).then_inc(par_exp.sem, 1)
            A(lexp, lsum, ACT.Exp)
            act.wait_ge(par_vec.sem, par_vec.at(s, 2))
            A(sin1, theta, ACT.Sin)
            A(cos1, tb, ACT.Sin).then_inc(par_exp.sem, 1)
            act.wait_ge(proj_done.sem, proj_done.at(s, 1))
            keep(uqT[:, 0:4 * P], bk(0, 0, 4), proj_kept)
            act.wait_ge(proj_kept.sem, proj_kept.at(s, 1))
            spread(0)
            yield 3
            spread(1)
            act.wait_ge(proj_done.sem, proj_done.at(s, 2))
            keep(uqT[:, 4 * P:6 * P], bk(1, 0, 2), proj_kept)
            keep(kT3[:, 0:2, one, :], bk(1, 2, 4).rearrange("p (t c n) -> p t c n", t=2, c=1), proj_kept)
            yield 4
            spread(2)
            apart(act, proj_done.sem, proj_done.at(s, 3))
            keep(kT3[:, 2:3, one, :], bk(2, 0, 1).rearrange("p (t c n) -> p t c n", t=1, c=1), proj_kept)
            keep(dv[:, chunk_cols(s, DIL_W)], bk(2, 1, 4), proj_kept)
            yield 5
            act.wait_ge(proj_done.sem, proj_done.at(s, 4))
            keep(fqT[:, :], bk(3, 0, 2), proj_kept)
            keep(fkT3[:, :, one, :], bk(3, 2, 4).rearrange("p (t c n) -> p t c n", t=2, c=1), proj_kept)
            for i in range(SSM_T):
                ins = A(ddiag[:, P * i:P * (i + 1)], ident[:, :], ACT.Copy, scale=row("d_skip")[:, i:i + 1])
            ins.then_inc(ddiag_ready.sem, 1)
            yield 7
            apart(act, proj_done.sem, proj_done.at(s, 5))
            keep(fv[:, chunk_cols(s, DIFF_W)], bk(4, 0, 2), proj_kept)
            yield 9
            for m in range(6):
                soften(m)
            yield 11
            for i in range(3):
                act.wait_ge(p_turned.sem, p_turned.at(s, i + 1))
                A(pT[:, 512 * i:512 * (i + 1)], dil_turn[i][:, :], ACT.Copy).then_inc(pT_ready.sem, 1)
            yield 12
            act.wait_ge(y_part.sem, y_part.at(s, 3))
            A(y_sq, bank[0][:, 0:SSM_W], ACT.Square).then_inc(y_sq_ready.sem, 1)
            for m in range(6, 9):
                soften(m)
            act.wait_ge(y_in_ready.sem, y_in_ready.at(s))
            A(y_th, y_in, ACT.Tanh).then_inc(y_th_ready.sem, 1)
            for m in range(9, 14):
                soften(m)
            act.wait_ge(dil_out.sem, dil_out.at(s))
            A(squares, hy[:, SSM_W:SSM_W + DIL_W], ACT.Square, accum_out=sums[:, 0:1])
            yield 14
            act.wait_ge(glu_done.sem, glu_done.at(s))
            A(glu_th, bank[3][:, 0:SSM_W], ACT.Tanh, scale=0.25).then_inc(glu_th_ready.sem, 1)
            for i in range(2):
                act.wait_ge(p_turned.sem, p_turned.at(s, 4 + i))
                A(pT[:, 512 * i:512 * (i + 1)], diff_turn[i][:, :], ACT.Copy).then_inc(pT_ready.sem, 1)
            act.wait_ge(gated_ready.sem, gated_ready.at(s))
            A(y_sq, y_glu, ACT.Square, accum_out=sums[:, 1:2]).then_inc(ssq_done.sem, 1)
            yield 18
            act.wait_ge(x_mid.sem, x_mid.at(s))
            A(squares_d, hy[:, :], ACT.Square, accum_out=ssq).then_inc(ssq_done.sem, 1)
            A(xs, hy[:, :], ACT.Copy).then_inc(x_kept.sem, 1)
            for n in range(5):
                yield 20 + n
                if n < 4:
                    act.wait_ge(q_done.sem, q_done.at(s, n + 1))
                    A(wide_c[:, 512 * n:512 * (n + 1)], bank[n][:, :], ACT.Copy).then_inc(q_kept.sem, 1)
                if n >= 1:
                    g = n - 1
                    if g == 0:
                        act.wait_ge(h2_ready.sem, h2_ready.at(s))
                    act.wait_ge(key_scores_done.sem, key_scores_done.at(s, g + 1))
                    A(wide_a[:, 512 * g:512 * (g + 1)], key_bank[g][:, :], ACT.Copy,
                      scale=rstd[:, 0:1]).then_inc(key_scores_kept.sem, 1)
            gate_exps(act, s, 0)

        def gate_exps(act, s, half):
            apart(act, gate_in.sem, gate_in.at(s, half + 1))
            own_gate = half_slots(gate, s, half)
            nc.scalar.activation(own_gate, own_gate, ACT.Exp).then_inc(gate_exp.sem, 1)

        def retrieval_act(act, s):
            yield 6
            gate_exps(act, s, 1)

        def experts_act(act, p, i, q):
            m = i * 2 + (q + 1)
            act.wait_ge(inner_ready.sem, inner_ready.at(p, 0) + m)
            inner = peer[:, RING:RING + HALF]
            nc.scalar.activation(peer[:, RING + HALF:2 * RING], inner, ACT.Tanh).then_inc(tanh_ready.sem, 1)
            act.wait_ge(weight_ready.sem, weight_ready.at(p, 0) + m)
            for r in range(HALF * q, HALF * (q + 1)):
                nc.scalar.activation(diag[:, P * r:P * (r + 1)], ident[:, :], ACT.Copy,
                                     scale=peer[:, 2 * RING + r:2 * RING + r + 1]).then_inc(diag_ready.sem, 1)

        def rsqrt(V, link, n):
            y, m, t = rstd[:, 0:n], ms[:, 0:n], nt[:, 0:n]
            ti = ti_a[:, 0:n].bitcast(I32)
            link(V.tensor_scalar(ti, m.bitcast(I32), 1, None, ALU.logical_shift_right))
            link(V.tensor_scalar(y.bitcast(I32), ti, -1.0, RSQRT_SEED, ALU.mult, ALU.add))
            link(V.tensor_scalar(m, m, -0.5, None, ALU.mult))
            for _ in range(3):
                if n == 1:
                    link(V.scalar_tensor_tensor(t, y, y, m, ALU.mult, ALU.mult))
                else:
                    link(V.tensor_tensor(t, y, y, ALU.mult))
                    link(V.tensor_tensor(t, t, m, ALU.mult))
                link(V.scalar_tensor_tensor(y, t, 1.5, y, ALU.add, ALU.mult))

        class Chain:

            def __init__(self, dve, counter, s):
                self.dve, self.counter, self.s, self.n = dve, counter, s, 0

            def step(self, ins):
                self.n += 1
                ins.then_inc(self.counter.sem, 1)

            def settle(self):
                self.dve.wait_ge(self.counter.sem, self.counter.at(self.s, self.n))

            def settle_apart(self):
                apart(self.dve, self.counter.sem, self.counter.at(self.s, self.n))

            def link(self, ins):
                self.step(ins)
                self.settle()

        def retrieval(dve, s, chain):
            V = nc.vector
            step, settle, link = chain.step, chain.settle, chain.link

            def top16(parts, width, vals, where):
                def part(a, i):
                    return a[:, width * i:width * (i + 1)]

                for i in parts:
                    step(V.max(vals[:, TOPK * i:TOPK * i + 8], part(wide_a, i)))
                chain.settle_apart()
                for i in parts:
                    step(V.match_replace(part(wide_b, i), vals[:, TOPK * i:TOPK * i + 8], part(wide_a, i), -3.0e38))
                    step(V.max_index(where[:, TOPK * i:TOPK * i + 8], vals[:, TOPK * i:TOPK * i + 8], part(wide_a, i)))
                chain.settle_apart()
                for i in parts:
                    step(V.max(vals[:, TOPK * i + 8:TOPK * i + 16], part(wide_b, i)))
                chain.settle_apart()
                for i in parts:
                    step(V.max_index(where[:, TOPK * i + 8:TOPK * i + 16], vals[:, TOPK * i + 8:TOPK * i + 16], part(wide_b, i)))
                settle()

            def keys(g):
                apart(dve, key_scores_kept.sem, key_scores_kept.at(s, g + 1))
                top16(range(4 * g, 4 * g + 4), KEYS, top_s, top_i)

            ts4 = top_s[:, :].rearrange("p (h c k) -> p h c k", h=HEADS, c=2)
            tf4 = top_f[:, :].rearrange("p (h c k) -> p h c k", h=HEADS, c=2)

            def pairs(g):
                hs = slice(2 * g, 2 * g + 2)
                link(V.tensor_tensor(wide_a[:, 512 * g:512 * (g + 1)].rearrange("p (h i j) -> p h i j", h=2, i=TOPK),
                                     ts4[:, hs, 0, :].unsqueeze(3).broadcast_to([P, 2, TOPK, TOPK]),
                                     ts4[:, hs, 1, :].unsqueeze(2).broadcast_to([P, 2, TOPK, TOPK]), ALU.add))
                step(V.tensor_copy(top_f[:, 64 * g:64 * (g + 1)], top_i[:, 64 * g:64 * (g + 1)]))
                chain.settle_apart()
                top16(range(2 * g, 2 * g + 2), TOPK * TOPK, best_s, best_j)

            def experts(g):
                H, n = 2, 2 * TOPK
                hs, at = slice(H * g, H * (g + 1)), slice(n * g, n * (g + 1))
                hits = wide_b[:, 512 * g:512 * (g + 1)]
                link(V.tensor_scalar(jpart[:, :], best_j[:, at], 4, None, ALU.logical_shift_right))
                step(V.tensor_copy(jf[:, :], jpart[:, :]))
                link(V.tensor_scalar(jlow[:, :], best_j[:, at], TOPK - 1, None, ALU.bitwise_and))
                for c, e in ((0, e_row), (1, e_col)):
                    if c:
                        link(V.tensor_copy(jf[:, :], jlow[:, :]))
                    hit = hits.rearrange("p (n i) -> p n i", i=TOPK)
                    link(V.tensor_tensor(hit, iota16.unsqueeze(1).broadcast_to([P, n, TOPK]),
                                         jf[:, :].unsqueeze(2).broadcast_to([P, n, TOPK]), ALU.is_equal))
                    hit4 = hits.rearrange("p (h k i) -> p h k i", h=H, k=TOPK)
                    link(V.tensor_tensor(hit4, hit4, tf4[:, hs, c, :].unsqueeze(2).broadcast_to([P, H, TOPK, TOPK]), ALU.mult))
                    link(V.tensor_reduce(e[:, :], hit, AX_X, ALU.add))
                link(V.scalar_tensor_tensor(e_row[:, :], e_row[:, :], float(KEYS), e_col[:, :], ALU.mult, ALU.add))
                V.tensor_scalar(idx[:, bass.ds((s & 1) * SLOTS + n * g, n)], e_row[:, :], base, None,
                                ALU.add).then_inc(picked.sem, 1)

            def gates(half, done):
                H, at = HEADS // 2, slice(SLOTS // 2 * half, SLOTS // 2 * (half + 1))
                b3 = best_s[:, at].rearrange("p (h k) -> p h k", h=H)
                g3 = half_slots(gate, s, half).rearrange("p (h k) -> p h k", h=H)
                V.tensor_tensor(g3, b3, b3[:, :, 0:1].broadcast_to([P, H, TOPK]), ALU.subtract).then_inc(gate_in.sem, 1)
                apart(dve, gate_exp.sem, gate_exp.at(s, half + 1))
                link(V.tensor_reduce(gsum, g3, AX_X, ALU.add))
                link(V.reciprocal(grec, gsum))
                link(V.tensor_scalar(grec, grec, 0.5, None, ALU.mult))
                V.tensor_tensor(g3, g3, grec.unsqueeze(2).broadcast_to([P, H, TOPK]), ALU.mult).then_inc(done.sem, 1)

            return keys, pairs, experts, gates

        def mixer_dve(dve, s):
            yield 0
            V = nc.vector
            chain = Chain(dve, vec, s)
            step, settle, link = chain.step, chain.settle, chain.link

            def norm_scale(n, src, scale):
                link(V.tensor_scalar(ms[:, 0:n], src, scale, EPS, ALU.mult, ALU.add))
                rsqrt(V, link, n)

            def turned_gain(banks, done, gain, ready):
                for j in range(2):
                    dve.wait_ge(done.sem, done.at(s, j + 1))
                    V.tensor_tensor(hT3[:, 4 * j:4 * j + 4, :], banks[j][:, :].rearrange("p (k n) -> p k n", k=4),
                                    gain[:, 4 * j:4 * j + 4].unsqueeze(2).broadcast_to([P, 4, P]),
                                    ALU.mult).then_inc(ready.sem, 1)

            hT3 = hT[:, :].rearrange("p (k n) -> p k n", k=KT)
            xs = x[:, chunk_cols(s, D)]
            cos3 = cos[:, :].rearrange("p (j t) -> p j t", j=ST)
            sin3 = sin[:, :].rearrange("p (j t) -> p j t", j=ST)
            start = carry[:, bass.ds(s * (2 * ST), 2 * ST)]
            keep_at = carry[:, bass.ds((s // 2) * (4 * ST) + 2 * ST, 2 * ST)]

            def double(n, top):
                while n < top:
                    t1, t2 = (d[:, 0:ST * n].rearrange("p (j t) -> p j t", j=ST) for d in dbl)
                    cn = cos3[:, :, n - 1:n].broadcast_to([P, ST, n])
                    sn = sin3[:, :, n - 1:n].broadcast_to([P, ST, n])
                    step(V.tensor_tensor(t1, cos3[:, :, 0:n], cn, ALU.mult))
                    link(V.tensor_tensor(t2, sin3[:, :, 0:n], sn, ALU.mult))
                    link(V.tensor_tensor(cos3[:, :, n:2 * n], t1, t2, ALU.subtract))
                    step(V.tensor_tensor(t1, cos3[:, :, 0:n], sn, ALU.mult))
                    link(V.tensor_tensor(t2, sin3[:, :, 0:n], cn, ALU.mult))
                    link(V.tensor_tensor(sin3[:, :, n:2 * n], t1, t2, ALU.add))
                    n *= 2

            def scan(g):
                dve.wait_ge(bu_done.sem, bu_done.at(s, g + 1))
                cg, sg = cos[:, 512 * g:512 * (g + 1)], sin[:, 512 * g:512 * (g + 1)]
                br, bi = bank[1][:, :], bank[2][:, :]
                step(V.tensor_tensor(v_im, bi, cg, ALU.mult))
                step(V.tensor_tensor(v_re, br, sg, ALU.mult))
                step(V.tensor_tensor(z_re, br, cg, ALU.mult))
                V.tensor_tensor(z_im, bi, sg, ALU.mult).then_inc(bu_free.sem, 1)
                dve.wait_ge(bu_free.sem, bu_free.at(s, g + 1))
                link(V.tensor_tensor(v_im, v_im, v_re, ALU.subtract))
                link(V.tensor_tensor(v_re, z_re, z_im, ALU.add))
                for j in range(SQ):
                    t = SQ * g + j
                    decay = rad[:, t:t + 1].broadcast_to([P, P])
                    for part, (v, z) in enumerate(((v_re, z_re), (v_im, z_im))):
                        step(V.tensor_tensor_scan(z[:, P * j:P * (j + 1)], decay, v[:, P * j:P * (j + 1)],
                                                  start[:, ST * part + t:ST * part + t + 1], ALU.mult, ALU.add))
                settle()
                if g:
                    dve.wait_ge(y_part.sem, y_part.at(s, g))
                step(V.tensor_tensor(p_cr, cg, z_re, ALU.mult))
                step(V.tensor_tensor(p_si, sg, z_im, ALU.mult))
                step(V.tensor_tensor(p_sr, sg, z_re, ALU.mult))
                V.tensor_tensor(p_ci, cg, z_im, ALU.mult).then_inc(prod_ready.sem, 1)
                dve.wait_ge(prod_ready.sem, prod_ready.at(s, g + 1))
                last = lambda a: a.rearrange("p (j t) -> p j t", j=SQ)[:, :, P - 1]
                step(V.tensor_tensor(keep_at[:, SQ * g:SQ * (g + 1)], last(p_cr), last(p_si), ALU.subtract))
                step(V.tensor_tensor(keep_at[:, ST + SQ * g:ST + SQ * (g + 1)], last(p_sr), last(p_ci), ALU.add))
                settle()

            def masked(m, place, mask, scale):
                o, half = place
                V.tensor_tensor_reduce(out=scored(m), in0=o[:, half:half + 256], in1=mask, scale=-scale,
                                       scalar=3.0e38, op0=ALU.add, op1=ALU.min,
                                       accum_out=nmax[:, m:m + 1]).then_inc(masked_ready.sem, 1)

            dve.wait_ge(ssq_done.sem, ssq_done.at(s, 1))
            norm_scale(1, ssq, 1.0 / D)
            V.tensor_copy(rstd[:, 1:2], rstd[:, 0:1]).then_inc(rstd_ready.sem, 1)
            dve.wait_ge(rows_in, 16 * s + 16)
            step(V.tensor_tensor(lprod, row("lam_q1"), row("lam_k1"), ALU.mult))
            settle()
            link(V.tensor_reduce(lsum[:, 0:1], lprod, AX_X, ALU.add))
            link(V.tensor_tensor(lprod, row("lam_q2"), row("lam_k2"), ALU.mult))
            link(V.tensor_reduce(lsum[:, 1:2], lprod, AX_X, ALU.add))
            dve.wait_ge(par_exp.sem, par_exp.at(s, 1))
            step(V.tensor_tensor(theta, row("lam_im"), step_t, ALU.mult))
            V.tensor_tensor(ta, row("lam_re"), step_t, ALU.mult).then_inc(par_vec.sem, 1)
            yield 1
            turned_gain(bank[0:2], hn_turned, row("g1"), hT_ready)
            settle()
            link(V.tensor_scalar(turn_n, theta, 1.0 / (2 * PI), ROUND, ALU.mult, ALU.add))
            link(V.tensor_scalar(turn_n, turn_n, ROUND, None, ALU.subtract))
            for part in (6.28125, 0.001934051513671875, 1.2556659146e-06):
                link(V.scalar_tensor_tensor(theta, turn_n, -part, theta, ALU.mult, ALU.add))
            link(V.tensor_scalar(theta, theta, 3.1415925, -3.1415925, ALU.min, ALU.max))
            link(V.scalar_tensor_tensor(tb, theta, -1.0, theta, ALU.mult, ALU.max))
            V.tensor_scalar(tb, tb, -1.0, PI / 2, ALU.mult, ALU.add).then_inc(par_vec.sem, 1)
            yield 3
            dve.wait_ge(par_exp.sem, par_exp.at(s, 3))
            step(V.tensor_tensor(f_re, cos1, cos1, ALU.mult))
            link(V.tensor_tensor(f_im, sin1, sin1, ALU.mult))
            link(V.tensor_tensor(f_re, f_re, f_im, ALU.add))
            link(V.tensor_scalar(f_re, f_re, -0.5, 1.5, ALU.mult, ALU.add))
            step(V.tensor_tensor(cos1, cos1, f_re, ALU.mult))
            link(V.tensor_tensor(sin1, sin1, f_re, ALU.mult))
            step(V.tensor_tensor(f_re, rad, cos1, ALU.mult))
            link(V.tensor_tensor(f_im, rad, sin1, ALU.mult))
            link(V.tensor_scalar(f_re, f_re, 1.0, None, ALU.subtract))
            step(V.tensor_tensor(ta, row("lam_re"), row("lam_re"), ALU.mult))
            link(V.tensor_tensor(tb, row("lam_im"), row("lam_im"), ALU.mult))
            link(V.tensor_tensor(ta, ta, tb, ALU.add))
            link(V.reciprocal(turn_n, ta))
            step(V.tensor_tensor(ta, f_re, row("lam_re"), ALU.mult))
            step(V.tensor_tensor(tb, f_im, row("lam_im"), ALU.mult))
            step(V.tensor_tensor(theta, f_im, row("lam_re"), ALU.mult))
            link(V.tensor_tensor(step_t, f_re, row("lam_im"), ALU.mult))
            step(V.tensor_tensor(ta, ta, tb, ALU.add))
            link(V.tensor_tensor(theta, theta, step_t, ALU.subtract))
            step(V.tensor_tensor(f_re, ta, turn_n, ALU.mult))
            link(V.tensor_tensor(f_im, theta, turn_n, ALU.mult))
            yield 4
            step(V.tensor_copy(cos3[:, :, 0:1], cos1.unsqueeze(2)))
            link(V.tensor_copy(sin3[:, :, 0:1], sin1.unsqueeze(2)))
            double(1, 32)
            yield 5
            double(32, P)
            cr = crot[:, :].rearrange("p (c j n) -> p c j n", c=3, j=ST)
            c_re = row("c_re").rearrange("p (j n) -> p j n", j=ST)
            c_im = row("c_im").rearrange("p (j n) -> p j n", j=ST)
            fr = f_re.unsqueeze(2).broadcast_to([P, ST, 32])
            fi = f_im.unsqueeze(2).broadcast_to([P, ST, 32])
            t1, t2 = (d[:, 0:ST * 32].rearrange("p (j t) -> p j t", j=ST) for d in dbl)
            step(V.tensor_tensor(t1, c_re, fr, ALU.mult))
            link(V.tensor_tensor(t2, c_im, fi, ALU.mult))
            step(V.tensor_tensor(cr[:, 0], t1, t2, ALU.subtract))
            link(V.tensor_tensor(cr[:, 1], t2, t1, ALU.subtract))
            step(V.tensor_tensor(t1, c_re, fi, ALU.mult))
            link(V.tensor_tensor(t2, c_im, fr, ALU.mult))
            link(V.tensor_tensor(t1, t1, t2, ALU.add))
            V.tensor_scalar(cr[:, 2], t1, -1.0, None, ALU.mult).then_inc(tables_ready.sem, 1)
            yield 6
            scan(0)
            yield 8
            scan(1)
            yield 9
            apart(dve, scores_done.sem, scores_done.at(s, 4))
            for m in range(6):
                masked(m, dil_scores(m), row("mask_dil"), DIL_SCALE)
            yield 10
            scan(2)
            yield 12
            apart(dve, scores_done.sem, scores_done.at(s, 8))
            for m in range(8):
                masked(6 + m, diff_scores(m // 2, m % 2), row("mask_diff"), DIFF_SCALE)
            y_ps = bank[0][:, 0:SSM_W]
            dve.wait_ge(y_sq_ready.sem, y_sq_ready.at(s))
            link(V.tensor_scalar(y_in, y_sq, GELU_B, GELU_A, ALU.mult, ALU.add))
            V.tensor_tensor(y_in, y_in, y_ps, ALU.mult).then_inc(y_in_ready.sem, 1)
            dve.wait_ge(exp_ready.sem, exp_ready.at(s, 6))
            link(V.reciprocal(rden[:, 0:6], den[:, 0:6]))
            dve.wait_ge(o_done.sem, o_done.at(s, 1))
            y_dil = hy[:, SSM_W:SSM_W + DIL_W]
            V.tensor_tensor(y_dil.rearrange("p (h d) -> p h d", h=DIL_HEADS),
                            bank[3][:, 0:DIL_W].rearrange("p (h d) -> p h d", h=DIL_HEADS),
                            rden[:, 0:6].unsqueeze(2).broadcast_to([P, DIL_HEADS, HD]), ALU.mult).then_inc(dil_out.sem, 1)
            dve.wait_ge(y_th_ready.sem, y_th_ready.at(s))
            V.scalar_tensor_tensor(gT_x2, y_th, 1.0, y_ps, ALU.add, ALU.mult).then_inc(g_ready.sem, 1)
            link(V.tensor_tensor(lam, lexp[:, 0:1], lexp[:, 1:2], ALU.subtract))
            link(V.tensor_tensor(lam, lam, row("lambda_init"), ALU.add))
            yield 13
            dve.wait_ge(exp_ready.sem, exp_ready.at(s, 14))
            link(V.reciprocal(rden[:, 6:14], den[:, 6:14]))
            second = rden[:, 6:14].rearrange("p (h m) -> p h m", m=2)[:, :, 1]
            link(V.tensor_scalar(second, second, lam, None, ALU.mult))
            maps = [(probs[:, 512 * h:512 * h + 256], probs[:, 512 * h + 256:512 * (h + 1)]) for h in range(DIFF_HEADS)]
            for h, (m1, m2) in enumerate(maps):
                step(V.tensor_scalar(m2, m2, rden[:, 2 * h + 7:2 * h + 8], None, ALU.mult))
            settle()
            for h, (m1, m2) in enumerate(maps):
                V.scalar_tensor_tensor(m1, m1, rden[:, 2 * h + 6:2 * h + 7], m2, ALU.mult, ALU.subtract).then_inc(attn_ready.sem, 1)
            yield 14
            dve.wait_ge(g_turned.sem, g_turned.at(s))
            dve.wait_ge(glu_th_ready.sem, glu_th_ready.at(s))
            V.scalar_tensor_tensor(y_glu, glu_th, 1.0, bank[0][:, 0:SSM_W], ALU.add, ALU.mult).then_inc(gated_ready.sem, 1)
            yield 15
            dve.wait_ge(o_done.sem, o_done.at(s, 2))
            y_diff = hy[:, SSM_W + DIL_W:D]
            yd3 = y_diff.rearrange("p (h d) -> p h d", h=DIFF_HEADS)
            link(V.tensor_copy(y_diff, bank[4][:, 0:DIFF_W]))
            link(V.tensor_tensor(o_sq, y_diff, y_diff, ALU.mult))
            step(V.tensor_reduce(sums[:, 2:6], o_sq.rearrange("p (h d) -> p h d", h=DIFF_HEADS), AX_X, ALU.add))
            dve.wait_ge(ssq_done.sem, ssq_done.at(s, 2))
            step(V.tensor_scalar(ms[:, 0:1], sums[:, 0:1], 1.0 / DIL_W, EPS, ALU.mult, ALU.add))
            step(V.tensor_scalar(ms[:, 1:2], sums[:, 1:2], 1.0 / (16 * SSM_W), EPS, ALU.mult, ALU.add))
            settle()
            link(V.tensor_scalar(ms[:, 2:6], sums[:, 2:6], 1.0 / HD, EPS, ALU.mult, ALU.add))
            rsqrt(V, link, 6)
            step(V.tensor_scalar(y_dil, y_dil, rstd[:, 0:1], None, ALU.mult))
            step(V.tensor_scalar(hy[:, 0:SSM_W], y_glu, rstd[:, 1:2], 0.25, ALU.mult, ALU.mult))
            step(V.tensor_tensor(yd3, yd3, rstd[:, 2:6].unsqueeze(2).broadcast_to([P, DIFF_HEADS, HD]), ALU.mult))
            settle()
            V.tensor_scalar(y_diff, y_diff, row("one_less_init"), None, ALU.mult).then_inc(y_ready.sem, 1)
            yield 16
            turned_gain((bank[0], bank[5]), y_turned, row("gy"), yT_ready)
            for n in range(2):
                yield 17 + n
                dve.wait_ge(mixed_done.sem, mixed_done.at(s, n + 1))
                ins = V.tensor_tensor(hy[:, 512 * n:512 * (n + 1)], xs[:, 512 * n:512 * (n + 1)], bank[1 + n][:, :], ALU.add)
                if n == 0:
                    step(ins)
            ins.then_inc(x_mid.sem, 1)
            yield 19
            turned_gain(bank[4:6], x_turned, row("g2_col"), xT_ready)
            dve.wait_ge(ssq_done.sem, ssq_done.at(s, 3))
            norm_scale(1, ssq, 1.0 / D)
            V.scalar_tensor_tensor(h2[:, :], hy[:, :], rstd[:, 0:1], row("g2"), ALU.mult, ALU.mult).then_inc(h2_ready.sem, 1)

            keys, pairs, experts, gates = retrieval(dve, s, chain)
            link(V.tensor_copy(base, row("first_expert")))
            for g in range(2):
                yield 21 + 2 * g
                keys(g)
                pairs(g)
                yield 22 + 2 * g
                experts(g)
            gates(0, mixer_done)
            assert chain.n == VEC_STEPS, chain.n

        def retrieval_dve(dve, s):
            chain = Chain(dve, pick_vec, s)
            keys, pairs, experts, gates = retrieval(dve, s, chain)
            for g in (2, 3):
                yield 3 * g - 5
                keys(g)
                yield 3 * g - 4
                pairs(g)
                yield 3 * g - 3
                experts(g)
            gates(1, all_picked)
            dve.wait_ge(all_picked.sem, all_picked.at(s))
            assert chain.n == PICK_STEPS, chain.n

        def experts_dve_start(dve, p):
            dve.wait_ge(mixer_done.sem, mixer_done.at(p))
            nc.vector.tensor_copy(h2_cur[:, :], h2[:, :]).then_inc(handed.sem, 1)
            apart(dve, handed.sem, handed.at(p))

        def experts_dve(dve, p, i, q):
            V = nc.vector
            dots, inner, th = peer[:, 0:RING], peer[:, RING:RING + HALF], peer[:, RING + HALF:2 * RING]
            weight = peer[:, 2 * RING:3 * RING]
            act_x = peer[:, 3 * RING:3 * RING + HALF]
            for r in range(HALF * q, HALF * (q + 1)):
                g = gathered[r]
                dve.wait_ge(g.sem, (p * ITERS + i + 1) * 16)
                V.tensor_tensor_reduce(out=u_of[r], in0=u_of[r], in1=h2_cur[:, :], scale=1.0, scalar=0.0,
                                       op0=ALU.mult, op1=ALU.add, accum_out=dots[:, r:r + 1]).then_inc(dots_done.sem, 1)
            d = dots[:, HALF * q:HALF * (q + 1)]
            m = i * 6 + 3 * q
            dve.wait_ge(dots_done.sem, dots_done.at(p, 0) + (i * RING + HALF * (q + 1)))
            V.tensor_tensor(inner, d, d, ALU.mult).then_inc(gelu_step.sem, 1)
            dve.wait_ge(gelu_step.sem, gelu_step.at(p, 0) + (m + 1))
            V.tensor_scalar(inner, inner, GELU_B, GELU_A, ALU.mult, ALU.add).then_inc(gelu_step.sem, 1)
            dve.wait_ge(gelu_step.sem, gelu_step.at(p, 0) + (m + 2))
            V.tensor_tensor(inner, inner, d, ALU.mult).then_inc(inner_ready.sem, 1)
            dve.wait_ge(tanh_ready.sem, tanh_ready.at(p, 0) + (i * 2 + (q + 1)))
            V.scalar_tensor_tensor(act_x, th, 1.0, d, ALU.add, ALU.mult).then_inc(gelu_step.sem, 1)
            dve.wait_ge(gelu_step.sem, gelu_step.at(p, 0) + (m + 3))
            V.tensor_tensor(weight[:, HALF * q:HALF * (q + 1)], act_x, gate[:, slot_cols(p, i, q)],
                            ALU.mult).then_inc(weight_ready.sem, 1)

        def experts_dve_end(dve, p):
            dve.wait_ge(slot_free.sem, slot_free.at(p, SLOTS))
            xs = x[:, chunk_cols(p, D)]
            nc.vector.tensor_copy(xs[:, 0:512], acc[:, 0, :]).then_inc(copied.sem, 1)
            nc.vector.tensor_copy(xs[:, 512:D], acc[:, 1, :]).then_inc(x_ready.sem, 1)

        def experts_pool(pool, p, i):
            for q in range(2):
                apart(pool, slot_free.sem, p * SLOTS + i * RING + (HALF * q + 1))
                nc.gpsimd.tensor_copy(idx_stage[:, HALF * q:HALF * (q + 1)],
                                      idx[:, slot_cols(p, i, q)]).then_inc(staged.sem, 1)
                apart(pool, staged.sem, staged.at(p, 0) + (i * 2 + (q + 1)))
                for r in range(HALF * q, HALF * (q + 1)):
                    if r % HALF:
                        apart(pool, slot_free.sem, p * SLOTS + i * RING + (r + 1))
                    nc.gpsimd.indirect_dma_start(ring[:, 2 * D * r:2 * D * (r + 1)], None, uv,
                                                 bass.IndirectOffsetOnAxis(idx_stage[:, r:r + 1], 0)).then_inc(gathered[r].sem, 16)

        def run(mixer):
            for _ in mixer:
                pass

        def run_over_experts(eng, p, experts, *others, stop=2 * ITERS):
            done = 0
            pending = [[next(o) + late, late, o] for o, late in others]
            while pending:
                pending.sort(key=lambda n: n[0])
                at, late, other = pending[0]
                while done < at:
                    experts(eng, p, done // 2, done % 2)
                    done += 1
                following = next(other, None)
                if following is None:
                    pending.pop(0)
                else:
                    pending[0][0] = following + late
            while done < stop:
                experts(eng, p, done // 2, done % 2)
                done += 1

        def run_experts(eng, p, experts, *others):
            run_over_experts(eng, p, experts, *others, stop=6)
            with eng.Fori(3, ITERS) as i:
                for q in range(2):
                    experts(eng, p, i, q)

        def last_x(c):
            return x[:, 0:D] if c == 0 else acc[:, :, :].rearrange("p a n -> p (a n)")

        def final_square(act, c):
            if c == 0:
                act.wait_ge(x_ready.sem, x_ready.at(STAGES - 2))
            else:
                act.wait_ge(slot_free.sem, slot_free.at(STAGES - 1, SLOTS))
                act.wait_ge(fin_vec, 1)
            nc.scalar.activation(hy[:, :], last_x(c), ACT.Square, accum_out=ssq).then_inc(fin_ssq, 1)

        def final_norm(dve, c):
            V = nc.vector
            n_own = [0]

            def own(ins):
                n_own[0] += 1
                ins.then_inc(fin_step[c], 1)
                dve.wait_ge(fin_step[c], n_own[0])

            dve.wait_ge(fin_ssq, c + 1)
            own(V.tensor_scalar(ms[:, 0:1], ssq, 1.0 / D, EPS, ALU.mult, ALU.add))
            rsqrt(V, own, 1)
            V.scalar_tensor_tensor(work[:, D * c:D * (c + 1)], last_x(c), rstd[:, 0:1], rows[:, 0:D],
                                   ALU.mult, ALU.mult).then_inc(fin_vec, 1)

        @block.gpsimd
        def _(pool):
            nc.gpsimd.iota(iota16.bitcast(I32), pattern=[[1, TOPK]], base=0, channel_multiplier=0).then_inc(iota_ready, 1)
            with pool.Fori(0, STAGES) as p:
                for g in range(4):
                    apart(pool, picked.sem, picked.at(p, g + 1))
                    with pool.Fori(g * (ITERS // 4), (g + 1) * (ITERS // 4)) as i:
                        experts_pool(pool, p, i)

        @block.scalar
        def _(act):
            act.wait_ge(consts_in, 32)
            run(mixer_act(act, 0))
            with act.Fori(1, STAGES) as s:
                run_over_experts(act, s - 1, experts_act, (retrieval_act(act, s - 1), 0), (mixer_act(act, s), MIXER_LATE))
            final_square(act, 0)
            run_experts(act, STAGES - 1, experts_act, (retrieval_act(act, STAGES - 1), 0))
            final_square(act, 1)

        @block.tensor
        def _(pe):
            for free in w_free:
                pe.sem_inc(free.sem, 1)
            pe.sem_inc(slot_free.sem, RING)
            pe.wait_ge(mem_ready, 2)
            run(mixer_pe(pe, 0))
            with pe.Fori(1, STAGES) as s:
                experts_pe_start(pe, s - 1)
                run_over_experts(pe, s - 1, experts_pe, (mixer_pe(pe, s), MIXER_LATE))
            experts_pe_start(pe, STAGES - 1)
            run_experts(pe, STAGES - 1, experts_pe)

        @block.vector
        def _(dve):
            V = nc.vector
            dve.sem_inc(x_ready.sem, 1)
            for k, t in enumerate((kT, fkT, dv, fv, carry)):
                V.memset(t[:, :], 0.0).then_inc(copied.sem, 1)
            dve.wait_ge(copied.sem, 5)
            dve.sem_inc(mem_ready, 1)
            dve.wait_ge(consts_in, 32)
            dve.wait_ge(iota_ready, 1)
            V.tensor_copy(iota16, iota16.bitcast(I32)).then_inc(mem_ready, 1)
            run(mixer_dve(dve, 0))
            dve.wait_ge(x1_in, 16)
            dve.sem_inc(x_ready.sem, 1)
            with dve.Fori(1, STAGES) as s:
                experts_dve_start(dve, s - 1)
                run_over_experts(dve, s - 1, experts_dve, (retrieval_dve(dve, s - 1), 0), (mixer_dve(dve, s), MIXER_LATE))
                experts_dve_end(dve, s - 1)
            experts_dve_start(dve, STAGES - 1)
            dve.wait_ge(fin_rows, 16)
            final_norm(dve, 0)
            run_experts(dve, STAGES - 1, experts_dve, (retrieval_dve(dve, STAGES - 1), 0))
            final_norm(dve, 1)


def kernel(**inputs):
    import numpy as np
    import concourse.bacc as bacc
    from concourse import mybir as _mybir
    from concourse.bass_utils import run_bass_kernel_spmd

    a = {k: np.asarray(v) for k, v in inputs.items()}
    f32 = np.float32

    def cols(w, width):
        n = w.shape[1] // width
        return w.reshape(KT, P, n, width).transpose(2, 1, 0, 3).reshape(n, P, KT * width)

    wts = np.zeros((L, BLOCKS, P, WB), f32)
    rows = np.zeros((STAGES, P, ROWS_W), f32)
    for l in range(L):
        wts[l, list(IN_BLOCK)] = cols(a["w_in"][l], 256)
        glu = a["ssm_w_glu"][l].reshape(SSM_T, P, SSM_W).transpose(1, 0, 2).reshape(P, -1)
        wts[l, B_GLU, :, 0:SSM_T * SSM_W] = glu
        for n, name in ((0, "ssm_b_re"), (SSM_W, "ssm_b_im")):
            b = a[name][l]
            for g in range(GROUPS):
                t, ch = g // 2, (g % 8) * GROUP_CH
                at = n + P * (g // 8) + STATE * (g % 2)
                wts[l, B_SSM, ch:ch + GROUP_CH, at:at + STATE] = b[g].T
        wts[l, B_OUT:B_OUT + 4] = cols(a["w_out"][l], 256)
        wts[l, list(QUERY_BLOCK)] = cols(a["peer_w_query"][l], 256)
        keys_t = a["peer_sub_keys"][l].reshape(HC, KEYS, P).transpose(2, 0, 1).reshape(P, 4, 4 * P)
        for g in range(4):
            wts[l, KEY_BLOCK[g], :, 0:4 * P] = keys_t[:, g]

    q = np.arange(P)[:, None]
    k = np.arange(2 * P)[None, :]
    for s in range(STAGES):
        l, c = s // 2, s % 2
        r = rows[s]

        def put(name, value):
            at, n = ROW_AT[name]
            r[:, at:at + n] = value

        put("g2", a["norm2_g"][l])
        back = P * c + q - k
        held = sum(((back >= 0) & (back <= w) & (back % d == 0)).astype(f32) for w, d in ((128, 1), (512, 4), (2048, 16)))
        put("mask_dil", np.where(held > 0, np.log(np.maximum(held, 1)) / DIL_SCALE, -1e30))
        put("mask_diff", np.where(back >= 0, 0.0, -1e30))
        for name, field in (("ssm_c_re", "c_re"), ("ssm_c_im", "c_im")):
            at, _ = ROW_AT[field]
            cm = a[name][l]
            for g in range(GROUPS):
                p0, o = STATE * (g % 2), at + 32 * (g // 2) + GROUP_CH * (g % 2)
                r[p0:p0 + STATE, o:o + GROUP_CH] = cm[g].T
        put("quarter", (np.arange(P)[:, None] // 32 == np.arange(SQ)[None, :]).astype(f32))
        put("d_skip", a["ssm_d"][l].reshape(SSM_T, P).T)
        put("g1", a["norm1_g"][l].reshape(KT, P).T)
        gy = np.concatenate([a["ssm_norm_g"][l], a["dil_norm_g"][l]] + [a["diff_subln_g"][l]] * DIFF_HEADS)
        put("gy", gy.reshape(KT, P).T)
        put("g2_col", a["norm2_g"][l].reshape(KT, P).T)
        put("lam_re", a["ssm_lam_re"][l].reshape(ST, P).T)
        put("lam_im", a["ssm_lam_im"][l].reshape(ST, P).T)
        put("log_step", np.repeat(a["ssm_log_step"][l], STATE).reshape(ST, P).T)
        for name in ("lam_q1", "lam_k1", "lam_q2", "lam_k2"):
            put(name, a[f"diff_{name}"][l])
        init = 0.8 - 0.6 * np.exp(-0.3 * l)
        put("lambda_init", init)
        put("one_less_init", 1.0 - init)
        put("first_expert", float(EXPERTS * l))
    uv = np.concatenate([a["peer_u"], a["peer_v"]], axis=2).reshape(L * EXPERTS, 2 * D)
    arrays = {
        "x_dram": np.ascontiguousarray(a["x"]), "wts_dram": wts.reshape(L * BLOCKS, P, WB), "rows_dram": rows,
        "uv_dram": uv, "ident_dram": np.eye(P, dtype=f32),
        "final_g_dram": np.ascontiguousarray(np.broadcast_to(a["final_norm_g"], (P, D))),
    }
    nc = bacc.Bacc("TRN2", target_bir_lowering=False, num_devices=1)
    args = [nc.dram_tensor(n, t.shape, _mybir.dt.float32, kind="ExternalInput").ap() for n, t in arrays.items()]
    out = nc.dram_tensor("out_dram", a["x"].shape, _mybir.dt.float32, kind="ExternalOutput").ap()
    trunk(nc, *args, out)
    r = run_bass_kernel_spmd(nc, [arrays], core_ids=[0])
    return r.results[0]["out_dram"]
```
